# Optimizing a Trainium2 kernel written in Bass

```python
import jax
import jax.numpy as jnp
from jax import lax
import numpy as np

D_MODEL = 2048
BATCH = 1
SEQ = 256
DEPTH = 1

N_ATTN_HEADS = 8
ATTN_HEAD_DIM = 128
ATTN_WIDTH = N_ATTN_HEADS * ATTN_HEAD_DIM
MOBA_BLOCK = 256
MOBA_TOPK = 3
MOBA_Q_CHUNK = 16
RET_HEADS = 4
RET_HEAD_DIM = 256
RET_WIDTH = RET_HEADS * RET_HEAD_DIM
RET_CHUNK = 128
MIX_WIDTH = ATTN_WIDTH + RET_WIDTH
IN_WIDTH = 3 * ATTN_WIDTH + 4 * RET_WIDTH
N_GROUPS = 4
EXPERTS_PER_GROUP = 8
N_EXPERTS = N_GROUPS * EXPERTS_PER_GROUP
INNER_TOP_K = 2
D_EXPERT = 512
MOE_ROW_BLOCK = 128
N_MOD = 6
NORM_EPS = 1e-6
F32 = jnp.float32

kernel_name = 'hymba_moba_retnet_hmoe_block'

def rmsnorm(x, w):
    xf = x.astype(F32)
    y = xf * lax.rsqrt(jnp.mean(xf * xf, axis=-1, keepdims=True) + NORM_EPS)
    return (y * w.astype(F32)).astype(x.dtype)

def modulate(h, shift, scale):
    return h * (1 + scale[:, None, :]) + shift[:, None, :]

def split_heads(z, n_heads, head_dim):
    b, t, _ = z.shape
    return z.reshape(b, t, n_heads, head_dim).transpose(0, 2, 1, 3)

def merge_heads(z):
    b, h, t, dh = z.shape
    return z.transpose(0, 2, 1, 3).reshape(b, t, h * dh)

def moba_attention(q, k, v):
    b, h, t, dh = q.shape
    nb = -(-t // MOBA_BLOCK)
    tp = nb * MOBA_BLOCK
    pad = ((0, 0), (0, 0), (0, tp - t), (0, 0))
    k_p = jnp.pad(k, pad)
    v_p = jnp.pad(v, pad)
    kb = k_p.reshape(b, h, nb, MOBA_BLOCK, dh)
    vb = v_p.reshape(b, h, nb, MOBA_BLOCK, dh)
    k_mean = jnp.mean(kb.astype(F32), axis=3)
    q_block = jnp.arange(t) // MOBA_BLOCK
    past = jnp.arange(nb)[None, :] < q_block[:, None]
    gate = jnp.einsum('bhtd,bhnd->bhtn', q.astype(F32), k_mean)
    gate = jnp.where(past[None, None], gate, -jnp.inf)
    n_sel = min(MOBA_TOPK, nb)
    gate_top, sel = lax.top_k(gate, n_sel)
    valid = jnp.isfinite(gate_top)
    slopes = jnp.exp2(-8.0 * jnp.arange(1, h + 1, dtype=F32) / h)
    scale = dh ** -0.5
    b_idx = jnp.arange(b)[:, None, None, None]
    h_idx = jnp.arange(h)[None, :, None, None]
    offs = jnp.arange(MOBA_BLOCK)
    n_keys_sel = n_sel * MOBA_BLOCK

    def chunk(ci):
        t0 = ci * MOBA_Q_CHUNK
        qc = lax.dynamic_slice_in_dim(q, t0, MOBA_Q_CHUNK, axis=2)
        sel_c = lax.dynamic_slice_in_dim(sel, t0, MOBA_Q_CHUNK, axis=2)
        valid_c = lax.dynamic_slice_in_dim(valid, t0, MOBA_Q_CHUNK, axis=2)
        tq_i = t0 + jnp.arange(MOBA_Q_CHUNK)
        tq = tq_i.astype(F32)
        k_sel = kb[b_idx, h_idx, sel_c]
        v_sel = vb[b_idx, h_idx, sel_c]
        s_sel = jnp.einsum('bhqd,bhqjsd->bhqjs', qc, k_sel).astype(F32) * scale
        pos_sel = (sel_c[..., None] * MOBA_BLOCK + offs).astype(F32)
        s_sel = s_sel - slopes[None, :, None, None, None] * (tq[None, None, :, None, None] - pos_sel)
        s_sel = jnp.where(valid_c[..., None], s_sel, -jnp.inf).reshape(b, h, MOBA_Q_CHUNK, n_keys_sel)
        b0 = (t0 // MOBA_BLOCK) * MOBA_BLOCK
        k_own = lax.dynamic_slice_in_dim(k_p, b0, MOBA_BLOCK, axis=2)
        v_own = lax.dynamic_slice_in_dim(v_p, b0, MOBA_BLOCK, axis=2)
        pos_own = b0 + offs
        s_own = jnp.einsum('bhqd,bhsd->bhqs', qc, k_own).astype(F32) * scale
        s_own = s_own - slopes[None, :, None, None] * (tq[:, None] - pos_own.astype(F32)[None, :])[None, None]
        causal = pos_own[None, :] <= tq_i[:, None]
        s_own = jnp.where(causal[None, None], s_own, -jnp.inf)
        logits = jnp.concatenate([s_sel, s_own], axis=-1)
        p = jax.nn.softmax(logits, axis=-1).astype(v.dtype)
        out = jnp.einsum('bhqs,bhqsd->bhqd', p[..., :n_keys_sel],
                         v_sel.reshape(b, h, MOBA_Q_CHUNK, n_keys_sel, dh))
        out = out + jnp.einsum('bhqs,bhsd->bhqd', p[..., n_keys_sel:], v_own)
        return out

    out = lax.map(chunk, jnp.arange(t // MOBA_Q_CHUNK))
    return out.transpose(1, 2, 0, 3, 4).reshape(b, h, t, dh)

def multiscale_retention(q, k, v):
    b, h, t, dk = q.shape
    dv = v.shape[-1]
    n = t // RET_CHUNK
    dt = q.dtype
    log_gamma = jnp.log1p(-jnp.exp2(-5.0 - jnp.arange(h, dtype=F32)))
    pos = jnp.arange(RET_CHUNK, dtype=F32)
    diff = pos[:, None] - pos[None, :]
    decay_mask = jnp.where(diff >= 0, jnp.exp(jnp.maximum(diff, 0.0) * log_gamma[:, None, None]), 0.0).astype(dt)
    k_decay = jnp.exp((RET_CHUNK - 1 - pos) * log_gamma[:, None]).astype(dt)
    q_decay = jnp.exp((pos + 1) * log_gamma[:, None]).astype(dt)
    chunk_decay = jnp.exp(RET_CHUNK * log_gamma)
    qc = q.reshape(b, h, n, RET_CHUNK, dk)
    kc = (k * (dk ** -0.5)).reshape(b, h, n, RET_CHUNK, dk)
    vc = v.reshape(b, h, n, RET_CHUNK, dv)
    scores = jnp.einsum('bhnid,bhnjd->bhnij', qc, kc) * decay_mask[None, :, None]
    inner = jnp.einsum('bhnij,bhnje->bhnie', scores, vc)
    chunk_kv = jnp.einsum('bhnjd,bhnje->nbhde', kc * k_decay[None, :, None, :, None], vc).astype(F32)

    def step(state, kv_n):
        return state * chunk_decay[None, :, None, None] + kv_n, state

    _, state_prev = lax.scan(step, jnp.zeros((b, h, dk, dv), F32), chunk_kv)
    cross = jnp.einsum('bhnid,nbhde->bhnie', qc, state_prev.astype(dt)) * q_decay[None, :, None, :, None]
    return (inner + cross).reshape(b, h, t, dv)

def grouped_expert_ffn(hf, expert_id, weights, w1, w3, w2):
    n, d = hf.shape
    eid = expert_id.reshape(-1)
    tok = jnp.repeat(jnp.arange(n, dtype=jnp.int32), expert_id.shape[1])
    wts = weights.reshape(-1)
    a = eid.shape[0]
    p_rows = a + N_EXPERTS * MOE_ROW_BLOCK
    n_blk = p_rows // MOE_ROW_BLOCK
    order = jnp.argsort(eid)
    eid_s = eid[order]
    counts = jnp.bincount(eid, length=N_EXPERTS)
    starts = jnp.cumsum(counts) - counts
    padded = (counts + MOE_ROW_BLOCK - 1) // MOE_ROW_BLOCK * MOE_ROW_BLOCK
    pad_end = jnp.cumsum(padded)
    pad_start = pad_end - padded
    dest = pad_start[eid_s] + jnp.arange(a) - starts[eid_s]
    row_tok = jnp.zeros((p_rows,), jnp.int32).at[dest].set(tok[order])
    row_w = jnp.zeros((p_rows,), wts.dtype).at[dest].set(wts[order])
    blk_expert = jnp.minimum(jnp.searchsorted(pad_end, jnp.arange(n_blk) * MOE_ROW_BLOCK, side='right'), N_EXPERTS - 1)

    def block_ffn(args):
        rows, e = args
        xb = hf[rows]
        return (jax.nn.silu(xb @ w1[e]) * (xb @ w3[e])) @ w2[e]

    y_rows = lax.map(block_ffn, (row_tok.reshape(n_blk, MOE_ROW_BLOCK), blk_expert))
    y_rows = y_rows.reshape(p_rows, d) * row_w[:, None]
    return jax.ops.segment_sum(y_rows, row_tok, num_segments=n)

def hier_moe(h, w_group, b_group, w_router, b_router, w1, w3, w2):
    b, t, d = h.shape
    n = b * t
    hf = h.reshape(n, d)
    g_prob = jax.nn.softmax((hf @ w_group + b_group).astype(F32), axis=-1)
    g_sel = jnp.argmax(g_prob, axis=-1)
    g_w = jnp.take_along_axis(g_prob, g_sel[:, None], axis=1)
    e_logits = jnp.einsum('nd,gde->nge', hf, w_router) + b_router
    e_logits = jnp.take_along_axis(e_logits, g_sel[:, None, None], axis=1)[:, 0]
    e_prob = jax.nn.softmax(e_logits.astype(F32), axis=-1)
    top_p, top_e = lax.top_k(e_prob, INNER_TOP_K)
    weights = g_w * top_p / jnp.sum(top_p, axis=-1, keepdims=True)
    expert_id = g_sel[:, None] * EXPERTS_PER_GROUP + top_e
    y = grouped_expert_ffn(hf, expert_id, weights.astype(h.dtype), w1, w3, w2)
    return y.reshape(b, t, d)

def setup_inputs(seed: int = 0) -> dict:
    key = jax.random.key(seed)
    ks = jax.random.split(key, 17)
    nrm = jax.random.normal
    return {
        'x': nrm(ks[0], (BATCH, SEQ, D_MODEL), F32),
        'c': nrm(ks[1], (BATCH, D_MODEL), F32),
        'w_ada': nrm(ks[2], (DEPTH, D_MODEL, N_MOD * D_MODEL), F32) * D_MODEL ** -0.5,
        'b_ada': nrm(ks[3], (DEPTH, N_MOD * D_MODEL), F32) * 0.01,
        'norm_mix_w': 1.0 + 0.02 * nrm(ks[4], (DEPTH, D_MODEL), F32),
        'w_in': nrm(ks[5], (DEPTH, D_MODEL, IN_WIDTH), F32) * D_MODEL ** -0.5,
        'ret_norm_w': 1.0 + 0.02 * nrm(ks[6], (DEPTH, RET_WIDTH), F32),
        'w_out': nrm(ks[7], (DEPTH, MIX_WIDTH, D_MODEL), F32) * MIX_WIDTH ** -0.5,
        'norm_ffn_w': 1.0 + 0.02 * nrm(ks[8], (DEPTH, D_MODEL), F32),
        'w_group': nrm(ks[9], (DEPTH, D_MODEL, N_GROUPS), F32) * D_MODEL ** -0.5,
        'b_group': nrm(ks[10], (DEPTH, N_GROUPS), F32) * 0.01,
        'w_router': nrm(ks[11], (DEPTH, N_GROUPS, D_MODEL, EXPERTS_PER_GROUP), F32) * D_MODEL ** -0.5,
        'b_router': nrm(ks[12], (DEPTH, N_GROUPS, EXPERTS_PER_GROUP), F32) * 0.01,
        'w1': nrm(ks[13], (DEPTH, N_EXPERTS, D_MODEL, D_EXPERT), F32) * D_MODEL ** -0.5,
        'w3': nrm(ks[14], (DEPTH, N_EXPERTS, D_MODEL, D_EXPERT), F32) * D_MODEL ** -0.5,
        'w2': nrm(ks[15], (DEPTH, N_EXPERTS, D_EXPERT, D_MODEL), F32) * D_EXPERT ** -0.5,
        'norm_final_w': 1.0 + 0.02 * nrm(ks[16], (D_MODEL,), F32),
    }

def reference(x, c, w_ada, b_ada, norm_mix_w, w_in, ret_norm_w, w_out, norm_ffn_w,
              w_group, b_group, w_router, b_router, w1, w3, w2, norm_final_w):
    b, t, d = x.shape
    c_act = jax.nn.silu(c)
    splits = [ATTN_WIDTH, 2 * ATTN_WIDTH, 3 * ATTN_WIDTH,
              3 * ATTN_WIDTH + RET_WIDTH, 3 * ATTN_WIDTH + 2 * RET_WIDTH, 3 * ATTN_WIDTH + 3 * RET_WIDTH]
    for l in range(DEPTH):
        mod = c_act @ w_ada[l] + b_ada[l]
        shift_m, scale_m, gate_m, shift_f, scale_f, gate_f = jnp.split(mod, N_MOD, axis=-1)
        h = modulate(rmsnorm(x, norm_mix_w[l]), shift_m, scale_m)
        proj = h @ w_in[l]
        qa, ka, va, qr, kr, vr, gr = jnp.split(proj, splits, axis=-1)
        attn = moba_attention(split_heads(qa, N_ATTN_HEADS, ATTN_HEAD_DIM),
                              split_heads(ka, N_ATTN_HEADS, ATTN_HEAD_DIM),
                              split_heads(va, N_ATTN_HEADS, ATTN_HEAD_DIM))
        ret = multiscale_retention(split_heads(qr, RET_HEADS, RET_HEAD_DIM),
                                   split_heads(kr, RET_HEADS, RET_HEAD_DIM),
                                   split_heads(vr, RET_HEADS, RET_HEAD_DIM))
        rf = ret.astype(F32)
        rf = rf * lax.rsqrt(jnp.mean(rf * rf, axis=-1, keepdims=True) + NORM_EPS)
        ret_out = merge_heads(rf.astype(x.dtype)) * ret_norm_w[l] * jax.nn.silu(gr)
        mix = jnp.concatenate([merge_heads(attn), ret_out.astype(x.dtype)], axis=-1) @ w_out[l]
        x = x + gate_m[:, None, :] * mix
        h2 = modulate(rmsnorm(x, norm_ffn_w[l]), shift_f, scale_f)
        x = x + gate_f[:, None, :] * hier_moe(h2, w_group[l], b_group[l], w_router[l], b_router[l],
                                             w1[l], w3[l], w2[l])
    return rmsnorm(x, norm_final_w)


_drawn_inputs = setup_inputs


def setup_inputs(seed=0):
    import zlib

    import numpy as np

    out = dict(_drawn_inputs(seed))
    spreads = {}
    factors = {'norm_mix_w': 3.229,
     'ret_norm_w': 7.707,
     'b_group': 27.312,
     'b_router': 22.576,
     'norm_final_w': 8.281,
     'norm_ffn_w': 7.911}
    for name, (base, spread) in spreads.items():
        noise = np.random.default_rng([zlib.crc32(name.encode()), seed]).standard_normal(out[name].shape)
        drawn = base * np.exp(spread * noise) if base else spread * noise
        out[name] = jnp.asarray(drawn.astype(out[name].dtype))
    for name, factor in factors.items():
        out[name] = (out[name] * factor).astype(out[name].dtype)
    return out
```

```python
from contextlib import ExitStack

import concourse.bass as bass
from concourse import mybir

F32 = mybir.dt.float32
I32 = mybir.dt.int32
ALU = mybir.AluOpType
ACT = mybir.ActivationFunctionType
AX = mybir.AxisListType.X

P = 128
D = 2048
T = 256
NB = T // P
K16 = D // P
HEADS, DH = 8, 128
PAIRS = HEADS // 2
RHEADS, DR = 4, 256
CW = 256
SECT = D // CW
E, DE = 32, 512
GROUPS, EPG = 4, 8
K4 = DE // P
CAP = 64
OVER = (2 * T - 1) // CAP
SLOTS = 2 * T + CAP
RING = 6
LATE = 10
CH = 4096
EPS = 1e-6
ROUTE_AT, ROUTE = 2816, 1280
TRI = 384
N_A, N_B1, N_B2, N_C = 2 * SECT, 6 * PAIRS, 9 * RHEADS, 8
B1_0, B2_0 = N_A, N_A + N_B1
C_0 = B2_0 + N_B2
D_0 = C_0 + N_C


def build(nc, x, c, w_ada, b_ada, norm_mix_w, w_in, ret_norm_w, w_out, norm_ffn_w, w_group, b_group,
          w_router, b_router, w1, w3, w2, norm_final_w, decay, rows_dram, out):
    ctx = ExitStack()
    with ctx:
        def sb(name, shape, dt=F32):
            return ctx.enter_context(nc.sbuf_tensor(name, shape, dt))

        def sem(name):
            return ctx.enter_context(nc.semaphore(name))

        ring = sb("ring", [P, RING, CH])
        xs = sb("xs", [P, NB, D])
        buf_a = sb("buf_a", [P, CH])
        buf_b = sb("buf_b", [P, CH])
        buf_g = sb("buf_g", [P, K16 * SLOTS])
        buf_m = sb("buf_m", [P, D])
        buf_r = sb("buf_r", [P, D])
        ada_row = sb("ada_row", [P, 2, CW])
        c_pad = sb("c_pad", [P, K16, 32])
        ident = sb("ident", [P, P])
        ones = sb("ones", [P, P])
        before = sb("before", [P, P])
        w_route = sb("w_route", [P, K16, 4 + E])
        b_route = sb("b_route", [P, 4 + E])
        c_col = sb("c_col", [P, K16])
        b_col = sb("b_col", [P, 6, K16])
        mix_w = sb("mix_w", [P, K16])
        ffn_w = sb("ffn_w", [P, K16])
        ret_w = sb("ret_w", [P, 8])
        mod_raw = sb("mod_raw", [P, 4, 2, K16])
        shift = sb("shift", [P, K16])
        scale = sb("scale", [P, K16])
        sumsq = sb("sumsq", [P, NB, 4])
        ms = sb("ms", [P, NB])
        rt = sb("rt", [P, NB])
        rinv = sb("rinv", [P, NB])
        smax = sb("smax", [P, 2, 2])
        ssum = sb("ssum", [P, 2, 2])
        sinv = sb("sinv", [P, 2, 2])
        rev8 = sb("rev8", [P, 8])
        e256 = sb("e256", [P, 1, E])
        lane = sb("lane", [P, 1])
        key_tab = sb("key_tab", [P, E + OVER + 1])
        start_tab = sb("start_tab", [1, E + OVER + 1], I32)
        item_e = sb("item_e", [1, OVER + 1], I32)
        n_over = sb("n_over", [1, 1], I32)
        key_col = sb("key_col", [P, 1])
        over_cap = sb("over_cap", [P, OVER + 1])
        over_t = sb("over_t", [P, OVER + 1])
        sums2 = sb("sums2", [P, 2 * K16])

        used = [0]

        def small(n, rows=P):
            used[0] += n
            assert used[0] <= ROUTE
            return buf_a[0:rows, ROUTE_AT + used[0] - n:ROUTE_AT + used[0]]

        lg = small(NB * 36).rearrange("p (b n) -> p b n", b=NB)
        gmax, top1, m1, m2, gsum = (small(NB) for _ in range(5))
        eq4 = small(NB * 4).rearrange("p (b n) -> p b n", b=NB)
        og = small(NB * 4).rearrange("p (b n) -> p b n", b=NB)
        exp_in = [small(NB * 4), small(NB)]
        exp_out = [small(NB * 4), small(NB)]
        lsel = small(NB * E).rearrange("p (b g e) -> p b g e", b=NB, g=GROUPS)
        el, eq8, o1, o2 = (small(NB * EPG).rearrange("p (b e) -> p b e", b=NB) for _ in range(4))
        chosen = small(2 * NB * E).rearrange("p (q b e) -> p q b e", q=2, b=NB)
        both = small(NB * E).rearrange("p (b e) -> p b e", b=NB)
        w_tok = small(2 * NB).rearrange("p (q b) -> p q b", q=2)
        cnt = small(3 * E)
        cnt_col = small(2, E)
        cnt_rep = buf_a[0:E, 1280:1536].rearrange("p (q m) -> p q m", q=2)
        first = small(2 * E)
        where = small(2 * NB * E).rearrange("p (s b e) -> p s b e", s=2, b=NB)
        wtmp = small(NB * E).rearrange("p (b e) -> p b e", b=NB)
        slot_key = small(2 * 2 * NB).rearrange("p (s q b) -> p s q b", s=2, q=2)
        tab = small(2 * E)
        item_is, item_slot, item_key, item_pad = (small(OVER + 1) for _ in range(4))

        xnT = buf_a[:, :].rearrange("p (k t) -> p k t", k=K16)
        xn = buf_b[:, :].rearrange("p (b d) -> p b d", b=NB)
        xn_k = buf_b[:, :].rearrange("p (b q k) -> p b k q", b=NB, k=K16)
        mixT = buf_b[:, :].rearrange("p (k t) -> p k t", k=K16)
        at = [0]

        def part(n):
            at[0] += n
            return buf_g[:, at[0] - n:at[0]]

        bias_sb = part(HEADS * TRI).rearrange("p (h n) -> p h n", h=HEADS)
        decay_sb = part(RHEADS * TRI)
        qT = part(512).rearrange("p (h t) -> p h t", h=2)
        kT = part(512).rearrange("p (h t) -> p h t", h=2)
        vv = part(512).rearrange("p (b n) -> p b n", b=2)
        pp = part(2 * TRI).rearrange("p (h n) -> p h n", h=2)
        ppT = part(2 * TRI).rearrange("p (h n) -> p h n", h=2)
        yy = part(512).rearrange("p (b n) -> p b n", b=2)
        sg = part(512).rearrange("p (b n) -> p b n", b=2)
        junk = part(512)
        assert at[0] <= K16 * SLOTS
        scoreT = pp[:, 0, :]
        xgT = buf_g[:, :].rearrange("p (k s) -> p k s", k=K16)
        is_item = buf_m[:, 1024:1024 + (OVER + 1) * E].rearrange("p (t e) -> p t e", e=E)
        item_tmp = buf_m[:, 1280:1280 + (OVER + 1) * E].rearrange("p (t e) -> p t e", e=E)
        onehot = buf_r[:, 0:1024].rearrange("p (b s) -> p b s", b=NB)
        diag = buf_r[:, 1024:2048].rearrange("p (b q n) -> p b q n", b=NB, q=4)
        iota_s = buf_m[:, 1024:1536]
        gate_f = buf_m[:, 0:1024]
        keys = buf_a[:, 0:1024].rearrange("p (q t) -> p q t", q=4)
        comb = buf_a[:, 1024:1280]
        comb2 = buf_a[:, 1280:1536]
        sil = buf_a[:, 1536:2048]
        gg = buf_a[:, 2048:2560]
        ggT = buf_a[:, 2560:2560 + K4 * CAP].rearrange("p (k s) -> p k s", k=K4)
        xe = buf_b[:, 0:K16 * CAP].rearrange("p (k s) -> p k s", k=K16)
        yg = buf_b[:, 1024:2048]
        answer = buf_g[:, 0:NB * D].rearrange("p (b d) -> p b d", b=NB)
        square = buf_g[:, NB * D:NB * D + 8 * 512].rearrange("p (j n) -> p j n", n=512)

        banks = [ctx.enter_context(nc.psum_tensor(f"bank{i}", [P, 512], F32)) for i in range(8)]
        ada_ps = banks[0:2]
        proj_ps = banks[2:4]
        turn_ps = banks[4:8]
        sc_ps, sc2_ps, tr_ps, pv_ps = banks[4:8]
        out_ps = [banks[2:4], banks[0:2]]
        h_ps, gt_ps = banks[0], banks[1]
        y_ps = banks[2:4]
        add_ps = banks[4:8]

        small_in = sem("small_in")
        x_in = sem("x_in")
        const_in = sem("const_in")
        late_in = sem("late_in")
        arrived = [sem(f"arrived{i}") for i in range(RING)]
        chunk_used = sem("chunk_used")
        consts_made = sem("consts_made")
        bias_step = sem("bias_step")
        c_ready = sem("c_ready")
        sq_done = sem("sq_done")
        ms_done = sem("ms_done")
        rt_done = sem("rt_done")
        rinv_done = sem("rinv_done")
        xn_ready = sem("xn_ready")
        turned = sem("turned")
        evac_dve = sem("evac_dve")
        evac_act = sem("evac_act")
        ada_copied = sem("ada_copied")
        row_stored = [sem("row_stored0"), sem("row_stored1")]
        cols_made = sem("cols_made")
        dve_step = sem("dve_step")
        mod_dve = sem("mod_dve")
        mod_act = sem("mod_act")
        col_ready = sem("col_ready")
        p0_out = sem("p0_out")
        p1_out = sem("p1_out")
        scored = sem("scored")
        logits = sem("logits")
        max_ready = sem("max_ready")
        exp_done = sem("exp_done")
        probs_ready = sem("probs_ready")
        probs_turned = sem("probs_turned")
        pT0_ready = sem("pT0_ready")
        pT1_ready = sem("pT1_ready")
        pv_done = sem("pv_done")
        mix_dve = sem("mix_dve")
        mix_act = sem("mix_act")
        decayed = sem("decayed")
        ret_pv = sem("ret_pv")
        ret_sq = sem("ret_sq")
        ret_ms = sem("ret_ms")
        ret_rt = sem("ret_rt")
        ret_step = sem("ret_step")
        ret_y = sem("ret_y")
        ret_turned = sem("ret_turned")
        ret_mix = sem("ret_mix")
        gate_rows = sem("gate_rows")
        gatef_rows = sem("gatef_rows")
        mod2_in = sem("mod2_in")
        gm_ps = sem("gm_ps")
        gm_ready = sem("gm_ready")
        x1_piece = sem("x1_piece")
        gf_ps = sem("gf_ps")
        gf_ready = sem("gf_ready")
        logits_ps = sem("logits_ps")
        route_exp_in = sem("route_exp_in")
        route_exp = sem("route_exp")
        picks = sem("picks")
        counts_ps = sem("counts_ps")
        counts_sb = sem("counts_sb")
        starts_ps = sem("starts_ps")
        onehot_ready = sem("onehot_ready")
        diag_ready = sem("diag_ready")
        keys_ps = sem("keys_ps")
        keys_ready = sem("keys_ready")
        iota_ready = sem("iota_ready")
        gathered = sem("gathered")
        starts_ready = sem("starts_ready")
        tables_ready = sem("tables_ready")
        final_w_in = sem("final_w_in")
        xe_ready = sem("xe_ready")
        sil_ready = sem("sil_ready")
        g_ready = sem("g_ready")
        gT_ps = sem("gT_ps")
        gT_ready = sem("gT_ready")
        yg_ready = sem("yg_ready")
        comb_step = sem("comb_step")
        comb_ready = sem("comb_ready")
        add_done = sem("add_done")
        added = sem("added")
        out_dve = sem("out_dve")
        out_act = sem("out_act")
        weighted = sem("weighted")
        inverse_ready = sem("inverse_ready")
        stored = sem("stored")

        ada_v = w_ada[0].rearrange("(p k) n -> p k n", k=K16)
        win_v = w_in[0].rearrange("(p k) n -> p k n", k=K16)
        wout_v = w_out[0].rearrange("(k p) n -> p k n", p=P)
        w13_v = [w[0].rearrange("e (p k) n -> p e k n", k=K16) for w in (w1, w3)]
        w2_v = w2[0].rearrange("e (p k) n -> p e k n", k=K4)

        def slot_cols(n):
            return ring[:, n % RING, :].rearrange("p (k n) -> p k n", k=K16)

        def slot_512(n):
            return ring[:, n % RING, :].rearrange("p (k n) -> p k n", n=512)

        def slot_w2(n):
            return ring[:, n % RING, :].rearrange("p (k n) -> p k n", n=D)

        def wait(eng, s, value):
            if isinstance(value, int) and value <= 0:
                return
            eng.wait_ge(s, value)

        def await_chunk(eng, n, turns=0):
            eng.wait_ge(arrived[n % RING], (turns + n // RING + 1) * 16)

        block = ctx.enter_context(nc.Block())

        @block.sync
        def _(sp):
            def load(n, turns, dst, src):
                wait(sp, chunk_used, turns * RING + (n - RING + 1))
                sp.dma_start(dst, src).then_inc(arrived[n % RING], 16)

            def ada(n, turns, a):
                load(n, turns, slot_cols(n), ada_v[:, :, bass.ds(a * CW, CW)])

            def win(n, turns, col):
                load(n, turns, slot_cols(n), win_v[:, :, bass.ds(col, CW)])

            def expert(n0, turns, e):
                for hf in range(2):
                    for m in range(2):
                        n = n0 + 2 * hf + m
                        load(n, turns, slot_512(n), w13_v[m][:, e, 8 * hf:8 * hf + 8, :].rearrange("p o k n -> p (o k) n"))
                for hf in range(2):
                    n = n0 + 4 + hf
                    load(n, turns, slot_w2(n), w2_v[:, e, 2 * hf:2 * hf + 2, :].rearrange("p o k n -> p (o k) n"))

            sp.dma_start(c_col[:], c.rearrange("o (p k) -> p (o k)", k=K16)).then_inc(small_in, 16)
            sp.dma_start(xs[:], x.rearrange("o (b p) d -> p (o b) d", p=P)).then_inc(x_in, 16)
            for n in range(RING):
                ada(n, 0, n)
            sp.dma_start(b_col[:], b_ada.rearrange("o (s p k) -> p (o s) k", k=K16, p=P)).then_inc(const_in, 16)
            sp.dma_start(mix_w[:], norm_mix_w.rearrange("o (p k) -> p (o k)", k=K16)).then_inc(const_in, 16)
            for n in range(RING, N_A):
                ada(n, 0, n)
            with sp.Fori(0, PAIRS) as i:
                for m in range(3):
                    win(B1_0 + 2 * m, i, 1024 * m + i * CW)
                    ada(B1_0 + 2 * m + 1, i, 2 * SECT + m + i * 3)
            sp.dma_start(ffn_w[:], norm_ffn_w.rearrange("o (p k) -> p (o k)", k=K16)).then_inc(late_in, 16)
            with nc.allow_non_contiguous_dma(reason="1024 weights, once"):
                sp.dma_start(ret_w[:], ret_norm_w.rearrange("o (k p) -> p (o k)", p=P)).then_inc(late_in, 16)
                sp.dma_start(w_route[:, :, 0:4], w_group.rearrange("o (p k) g -> p (o k) g", k=K16)).then_inc(late_in, 16)
                for g in range(GROUPS):
                    sp.dma_start(w_route[:, :, 4 + EPG * g:4 + EPG * (g + 1)],
                                 w_router[0, g].rearrange("(p k) e -> p k e", k=K16)).then_inc(late_in, 16)
            sp.dma_start(b_route[:, 0:4], b_group[0].partition_broadcast(P)).then_inc(late_in, 16)
            sp.dma_start(b_route[:, 4:4 + E], b_router.rearrange("o g e -> (o g e)").partition_broadcast(P)).then_inc(late_in, 16)
            sp.dma_start(decay_sb, decay).then_inc(late_in, 16)
            with sp.Fori(0, RHEADS // 2) as i:
                for r in range(2):
                    n = B2_0 + 9 * r
                    for m in range(4):
                        win(n + 2 * m, i * 3, 3072 + 1024 * m + r * CW + i * (2 * CW))
                        ada(n + 2 * m + 1, i * 3, 2 * SECT + 3 * PAIRS + 5 * r + m + i * 10)
                    ada(n + 8, i * 3, 2 * SECT + 3 * PAIRS + 5 * r + 4 + i * 10)
            for cc in range(4):
                for hf in range(2):
                    n = C_0 + 2 * cc + hf
                    load(n, 0, slot_512(n), wout_v[:, 8 * hf:8 * hf + 8, cc * 512:(cc + 1) * 512])
            with sp.Fori(0, E - 1) as e:
                expert(D_0, e, bass.ds(e, 1))
            sp.wait_ge(tables_ready, 1)
            items = sp.value_load(n_over[0:1, 0:1], min_val=0, max_val=OVER)
            with sp.Fori(0, OVER) as t:
                with sp.If(t < items):
                    e = sp.value_load(item_e[0:1, bass.ds(t, 1)], min_val=0, max_val=E - 1)
                    expert(D_0, t + (E - 1), bass.ds(e, 1))
                sp.end_ifs()
            expert(D_0, items + (E - 1), slice(E - 1, E))
            for h in range(4):
                b, q = h // 2, h % 2
                sp.wait_ge((out_dve, out_act)[q], b + 1)
                sp.dma_start(out[0, b * P:(b + 1) * P, q * 1024:(q + 1) * 1024],
                             answer[:, b, q * 1024:(q + 1) * 1024]).then_inc(stored, 16)
            sp.wait_ge(stored, 64)

        @block.gpsimd
        def _(pool):
            nc.gpsimd.memset(c_pad[:], 0.0).then_inc(consts_made, 1)
            nc.gpsimd.memset(ones[:], 1.0).then_inc(consts_made, 1)
            pool.wait_ge(consts_made, 2)
            nc.gpsimd.affine_select(out=ident[:], in_=ones[:], compare_op=ALU.is_equal, fill=0.0, base=0,
                                    pattern=[[-1, P]], channel_multiplier=1).then_inc(consts_made, 1)
            nc.gpsimd.affine_select(out=before[:], in_=ones[:], compare_op=ALU.is_gt, fill=0.0, base=0,
                                    pattern=[[1, P]], channel_multiplier=-1).then_inc(consts_made, 1)
            nc.gpsimd.iota(rev8[:], pattern=[[-1, 8]], base=8, channel_multiplier=0,
                           allow_small_or_imprecise_dtypes=True).then_inc(consts_made, 1)
            nc.gpsimd.iota(e256[:, 0, :], pattern=[[256, E]], base=0, channel_multiplier=0,
                           allow_small_or_imprecise_dtypes=True).then_inc(consts_made, 1)
            nc.gpsimd.iota(key_tab[:, 0:E], pattern=[[256, E]], base=0, channel_multiplier=0,
                           allow_small_or_imprecise_dtypes=True).then_inc(consts_made, 1)
            for hf in range(2):
                pool.wait_ge(consts_made, 7 + hf)
                nc.gpsimd.iota(lane[CAP * hf:CAP * (hf + 1), :], pattern=[[0, 1]], base=0, channel_multiplier=1,
                               allow_small_or_imprecise_dtypes=True).then_inc(consts_made, 1)
            pool.wait_ge(consts_made, 9)
            for j, base in enumerate((0, -P, 0)):
                nc.gpsimd.iota(junk[:, j * P:(j + 1) * P], pattern=[[1, P]], base=base, channel_multiplier=-1,
                               allow_small_or_imprecise_dtypes=True).then_inc(bias_step, 1)
            for j in (0, 2):
                pool.wait_ge(bias_step, 3)
                tile = junk[:, j * P:(j + 1) * P]
                nc.gpsimd.affine_select(out=tile, in_=tile, compare_op=ALU.is_ge, fill=-1e34, base=0,
                                        pattern=[[-1, P]], channel_multiplier=1).then_inc(bias_step, 1)
            pool.wait_ge(bias_step, 5)
            for h in range(HEADS):
                nc.gpsimd.tensor_scalar(bias_sb[:, h, :], junk[:, 0:TRI], 2.0 ** (-8.0 * (h + 1) / HEADS), None,
                                        ALU.mult).then_inc(bias_step, 1)
            nc.gpsimd.iota(over_cap[:], pattern=[[CAP, OVER + 1]], base=CAP, channel_multiplier=0,
                           allow_small_or_imprecise_dtypes=True).then_inc(bias_step, 1)
            nc.gpsimd.iota(over_t[:], pattern=[[1, OVER + 1]], base=0, channel_multiplier=0,
                           allow_small_or_imprecise_dtypes=True).then_inc(bias_step, 1)
            pool.wait_ge(x1_piece, 4 * NB)
            nc.gpsimd.iota(iota_s, pattern=[[1, 512]], base=0, channel_multiplier=0,
                           allow_small_or_imprecise_dtypes=True).then_inc(iota_ready, 1)
            pool.wait_ge(sq_done, NB + 4 * NB)
            nc.gpsimd.memset(xgT[:, :, 2 * T:SLOTS], 0.0).then_inc(iota_ready, 1)

        @block.tensor
        def _(pe):
            mm = nc.tensor.matmul

            def turn_group(g):
                bank = turn_ps[g % 4]
                for j in range(4):
                    last = nc.tensor.transpose(bank[:, j * P:(j + 1) * P], xn_k[:, j % 2, 2 * g + j // 2, :],
                                               ident[:])
                last.then_inc(turned, 1)

            def ada(n, turns, par, copied):
                await_chunk(pe, n, turns)
                wait(pe, ada_copied, copied)
                w = slot_cols(n)
                for k in range(K16):
                    g = 32 * (k % 4)
                    last = mm(ada_ps[par][g:g + 32, 0:CW], c_pad[:, k, :], w[:, k, :],
                              start=k < 4, stop=k >= K16 - 4)
                last.then_inc(chunk_used, 1)

            def proj_T(n, turns, bank):
                await_chunk(pe, n, turns)
                w = slot_cols(n)
                for h in range(2):
                    for k in range(K16):
                        last = mm(bank[:, h * T:(h + 1) * T], w[:, k, h * P:(h + 1) * P], xnT[:, k, :],
                                  start=k == 0, stop=k == K16 - 1)
                last.then_inc(chunk_used, 1)

            def proj(n, turns, bank):
                await_chunk(pe, n, turns)
                w = slot_cols(n)
                for b in range(NB):
                    for k in range(K16):
                        last = mm(bank[:, b * CW:(b + 1) * CW], xnT[:, k, b * P:(b + 1) * P], w[:, k, :],
                                  start=k == 0, stop=k == K16 - 1)
                last.then_inc(chunk_used, 1)

            pe.wait_ge(consts_made, 4)
            pe.wait_ge(xn_ready, 1)
            for g in range(8):
                if g >= 4:
                    pe.wait_ge(evac_dve if g % 2 == 0 else evac_act, (g - 4) // 2 + 1)
                turn_group(g)
            pe.wait_ge(c_ready, 1)
            for n in range(N_A):
                ada(n, 0, n % 2, n - 1)
            pe.wait_ge(ada_copied, N_A)
            pe.wait_ge(evac_dve, 4)
            pe.wait_ge(evac_act, 4)
            for s, rows in enumerate((buf_m, buf_r)):
                rows_k = rows[:, :].rearrange("p (q k) -> p k q", k=K16)
                for k in range(K16):
                    last = mm(sc_ps[:, s * K16 + k:s * K16 + k + 1], rows_k[:, k, :], ones[:, 0:1],
                              start=True, stop=True)
            last.then_inc(cols_made, 1)
            pe.wait_ge(mod_dve, 1)
            pe.wait_ge(mod_act, 1)

            with pe.Fori(0, PAIRS) as i:
                a0 = 2 * SECT
                proj_T(B1_0, i, proj_ps[0])
                ada(B1_0 + 1, i, 0, i * 3 + a0)
                proj_T(B1_0 + 2, i, proj_ps[1])
                ada(B1_0 + 3, i, 1, i * 3 + a0)
                pe.wait_ge(p0_out, i * 2 + 1)
                pe.wait_ge(p1_out, i + 1)
                for h, bank in enumerate((sc_ps, sc2_ps)):
                    mm(bank[:, 0:P], qT[:, h, 0:P], kT[:, h, 0:P], start=True, stop=True)
                    mm(bank[:, P:TRI], qT[:, h, P:T], kT[:, h, :], start=True, stop=True).then_inc(scored, 1)
                proj(B1_0 + 4, i, proj_ps[0])
                ada(B1_0 + 5, i, 0, i * 3 + a0 + 1)
                pe.wait_ge(probs_ready, i + 1)
                for h, bank in enumerate((tr_ps, sc2_ps)):
                    for j in range(3):
                        last = nc.tensor.transpose(bank[:, j * P:(j + 1) * P], pp[:, h, j * P:(j + 1) * P], ident[:])
                    last.then_inc(probs_turned, 1)
                pe.wait_ge(p0_out, i * 2 + 2)
                for h, bank in enumerate((pv_ps, tr_ps)):
                    pe.wait_ge((pT0_ready, pT1_ready)[h], i + 1)
                    v = vv[:, :, h * DH:(h + 1) * DH]
                    mm(bank[:, 0:P], v[:, 0, :], ppT[:, h, 0:P], start=True, stop=True)
                    mm(bank[:, P:T], v[:, 0, :], ppT[:, h, P:T], start=True, stop=False)
                    mm(bank[:, P:T], v[:, 1, :], ppT[:, h, T:TRI], start=False, stop=True).then_inc(pv_done, 1)
                pe.wait_ge(mix_dve, i + 1)
                pe.wait_ge(mix_act, i + 1)

            with pe.Fori(0, RHEADS // 2) as i:
                for r in range(2):
                    n, t3, head = B2_0 + 9 * r, i * 3, i * 2 + r
                    a0 = 2 * SECT + 3 * PAIRS + 5 * r
                    proj_T(n, t3, proj_ps[0])
                    ada(n + 1, t3, 0, i * 10 + a0)
                    proj_T(n + 2, t3, proj_ps[1])
                    ada(n + 3, t3, 1, i * 10 + a0)
                    pe.wait_ge(p0_out, head * 2 + (2 * PAIRS + 1))
                    pe.wait_ge(p1_out, head * 2 + (PAIRS + 1))
                    for j in range(2):
                        mm(sc_ps[:, 0:T], kT[:, j, 0:P], qT[:, j, :], start=j == 0, stop=j == 1)
                    for j in range(2):
                        last = mm(sc_ps[:, T:TRI], kT[:, j, P:T], qT[:, j, P:T], start=j == 0, stop=j == 1)
                    last.then_inc(scored, 1)
                    proj(n + 4, t3, proj_ps[0])
                    ada(n + 5, t3, 0, i * 10 + (a0 + 1))
                    pe.wait_ge(decayed, head + 1)
                    pe.wait_ge(p0_out, head * 2 + (2 * PAIRS + 2))
                    mm(pv_ps[:, 0:T], scoreT[:, 0:P], vv[:, 0, :], start=True, stop=True)
                    mm(pv_ps[:, T:512], scoreT[:, P:T], vv[:, 0, :], start=True, stop=False)
                    mm(pv_ps[:, T:512], scoreT[:, T:TRI], vv[:, 1, :], start=False, stop=True).then_inc(ret_pv, 1)
                    proj(n + 6, t3, proj_ps[1])
                    ada(n + 7, t3, 1, i * 10 + (a0 + 2))
                    ada(n + 8, t3, 0, i * 10 + (a0 + 3))
                    pe.wait_ge(ret_y, head + 1)
                    for j in range(4):
                        last = nc.tensor.transpose(tr_ps[:, j * P:(j + 1) * P], yy[:, j % 2, (j // 2) * P:(j // 2 + 1) * P],
                                                   ident[:])
                    last.then_inc(ret_turned, 1)

            pe.wait_ge(ret_mix, RHEADS)
            pe.wait_ge(ada_copied, 6 * SECT)
            for cc in range(4):
                wait(pe, x1_piece, NB * (cc - 1))
                for hf in range(2):
                    n = C_0 + 2 * cc + hf
                    await_chunk(pe, n)
                    w = slot_512(n)
                    for b in range(NB):
                        for k in range(8):
                            last = mm(out_ps[cc % 2][b][:, :], mixT[:, 8 * hf + k, b * P:(b + 1) * P], w[:, k, :],
                                      start=hf == 0 and k == 0, stop=hf == 1 and k == 7)
                    last.then_inc(chunk_used, 1)
                if cc == 0:
                    pe.wait_ge(gate_rows, 32)
                    for q in range(4):
                        mm(turn_ps[q][:, :], ones[0:5, :], buf_r[0:5, q * 512:(q + 1) * 512],
                           start=True, stop=True).then_inc(gm_ps, 1)

            pe.wait_ge(xn_ready, 2)
            pe.wait_ge(gm_ready, 4)
            for g in range(8):
                wait(pe, evac_dve if g % 2 == 0 else evac_act, 4 + (g - 4) // 2 + 1 if g >= 4 else 0)
                turn_group(g)
            pe.wait_ge(gatef_rows, 32)
            for q in range(2):
                for half in range(2):
                    last = mm(ada_ps[q][CAP * half:CAP * (half + 1), :], ones[0:5, 0:CAP],
                              buf_r[0:5, half * 1024 + q * 512:half * 1024 + (q + 1) * 512], start=True, stop=True)
                last.then_inc(gf_ps, 1)
            pe.wait_ge(evac_dve, 8)
            pe.wait_ge(evac_act, 8)
            pe.wait_ge(late_in, LATE * 16)
            for b in range(NB):
                for k in range(K16):
                    last = mm(proj_ps[0][:, b * 36:(b + 1) * 36], xnT[:, k, b * P:(b + 1) * P], w_route[:, k, :],
                              start=k == 0, stop=k == K16 - 1)
            last.then_inc(logits_ps, 1)
            pe.wait_ge(picks, 1)
            pe.wait_ge(gf_ready, 2)
            cps = proj_ps[1]
            mm(cps[:, 0:E], ones[:], both[:, 0, :], start=True, stop=False)
            mm(cps[:, 0:E], ones[:], both[:, 1, :], start=False, stop=True)
            mm(cps[:, E:2 * E], before[:], both[:, 0, :], start=True, stop=True)
            mm(cps[:, 2 * E:3 * E], ones[:], both[:, 0, :], start=True, stop=False)
            mm(cps[:, 2 * E:3 * E], before[:], both[:, 1, :], start=False, stop=True)
            mm(ada_ps[0][0:E, 0:1], both[:, 0, :], ones[:, 0:1], start=True, stop=False)
            mm(ada_ps[0][0:E, 0:1], both[:, 1, :], ones[:, 0:1], start=False, stop=True).then_inc(counts_ps, 1)
            pe.wait_ge(counts_sb, 1)
            mm(ada_ps[1][:, 0:E], cnt_rep[:, 0, :], before[0:E, 0:E], start=True, stop=True)
            mm(ada_ps[1][:, E:2 * E], cnt_rep[:, 1, :], before[0:E, 0:E], start=True, stop=True).then_inc(starts_ps, 1)
            pe.wait_ge(onehot_ready, 1)
            for k in range(K16):
                if k >= 4:
                    wait(pe, evac_dve if k % 2 == 0 else evac_act, 8 + (k - 4) // 2 + 1)
                for b in range(NB):
                    last = mm(turn_ps[k % 4][:, :], xn_k[:, b, k, :], onehot[:, b, :], start=b == 0, stop=b == 1)
                last.then_inc(gathered, 1)
            pe.wait_ge(diag_ready, 1)
            for b in range(NB):
                last = mm(proj_ps[b][:, :], ones[:], diag[:, b], start=True, stop=True)
            last.then_inc(keys_ps, 1)

            def hidden(n):
                pe.wait_ge(xe_ready, n + 1)
                for hf in range(2):
                    for m in range(2):
                        await_chunk(pe, D_0 + 2 * hf + m, n)
                    w = [slot_512(D_0 + 2 * hf + m) for m in range(2)]
                    for k in range(8):
                        for m in range(2):
                            last = mm(h_ps[CAP * m:CAP * (m + 1), :], xe[:, 8 * hf + k, :], w[m][:, k, :],
                                      start=hf == 0 and k == 0, stop=hf == 1 and k == 7)
                            if k == 7:
                                last.then_inc(chunk_used, 1)

            def turn_hidden(n):
                pe.wait_ge(g_ready, n + 1)
                g_k = gg[0:CAP, :].rearrange("p (q k) -> p k q", k=K4)
                for k in range(K4):
                    last = mm(gt_ps[:, k * CAP:(k + 1) * CAP], g_k[:, k, :], ident[0:CAP, 0:CAP],
                              start=True, stop=True)
                last.then_inc(gT_ps, 1)

            def outputs(n, yg_free):
                pe.wait_ge(gT_ready, n + 1)
                wait(pe, yg_ready, yg_free)
                for hf in range(2):
                    await_chunk(pe, D_0 + 4 + hf, n)
                    w = slot_w2(D_0 + 4 + hf)
                    for k in range(2):
                        for q in range(2):
                            for half in range(2):
                                col = half * 1024 + q * 512
                                last = mm(y_ps[q][CAP * half:CAP * (half + 1), :], ggT[:, 2 * hf + k, :],
                                          w[:, k, col:col + 512], start=hf == 0 and k == 0, stop=hf == 1 and k == 1)
                    last.then_inc(chunk_used, 1)

            def add_up(n):
                pe.wait_ge(comb_ready, n + 1)
                for j in range(4):
                    b, q = j // 2, j % 2
                    if j >= 2:
                        pe.wait_ge(added, n * 4 + (j - 1))
                    for half in range(2):
                        rows = slice(CAP * half, CAP * (half + 1))
                        last = mm(add_ps[2 * (j % 2) + half][:, :], comb[rows, b * P:(b + 1) * P],
                                  yg[rows, q * 512:(q + 1) * 512], start=True, stop=True)
                    last.then_inc(add_done, 1)

            pe.wait_ge(keys_ready, 1)
            pe.wait_ge(evac_dve, 16)
            pe.wait_ge(evac_act, 16)
            def item(n):
                hidden(n)
                add_up(n - 1)
                turn_hidden(n)
                outputs(n, n)

            hidden(0)
            turn_hidden(0)
            outputs(0, 0)
            with pe.Fori(1, E - 1) as n:
                item(n)
            pe.wait_ge(tables_ready, 1)
            items = pe.value_load(n_over[0:1, 0:1], min_val=0, max_val=OVER)
            with pe.Fori(0, OVER) as t:
                with pe.If(t < items):
                    item(t + (E - 1))
                pe.end_ifs()
            item(items + (E - 1))
            add_up(items + (E - 1))

        @block.scalar
        def _(act):
            act.wait_ge(small_in, 16)
            act.wait_ge(consts_made, 1)
            nc.scalar.activation(c_pad[:, :, 0], c_col[:], ACT.Silu).then_inc(c_ready, 1)
            act.wait_ge(x_in, 16)
            for b in range(NB):
                nc.scalar.activation(xn[:, b, :], xs[:, b, :], ACT.Square,
                                     accum_out=sumsq[:, b, 0:1]).then_inc(sq_done, 1)
            act.wait_ge(ms_done, 1)
            nc.scalar.activation(rt[:], ms[:], ACT.Sqrt).then_inc(rt_done, 1)
            for g in range(1, 8, 2):
                act.wait_ge(turned, g + 1)
                nc.scalar.copy(xnT[:, 2 * g:2 * g + 2, :].rearrange("p k t -> p (k t)"),
                               turn_ps[g % 4][:, :]).then_inc(evac_act, 1)
            for n in range(N_A):
                act.wait_ge(chunk_used, n + 1)
                rows = buf_m if n < SECT else buf_r
                nc.scalar.copy(rows[:, (n % SECT) * CW:(n % SECT + 1) * CW],
                               ada_ps[n % 2][:, 0:CW]).then_inc(ada_copied, 1)
            act.wait_ge(col_ready, 1)
            for k in range(1, K16, 2):
                last = nc.scalar.activation(xnT[:, k, :], xnT[:, k, :], ACT.Identity, bias=shift[:, k:k + 1],
                                            scale=scale[:, k:k + 1])
            last.then_inc(mod_act, 1)

            def ada_row_out(used, par, stored_before, copied, a):
                act.wait_ge(chunk_used, used)
                if stored_before is not None:
                    act.wait_ge(row_stored[par], stored_before)
                nc.scalar.copy(ada_row[:, par, :], ada_ps[par][:, 0:CW]).then_inc(ada_copied, 1)
                act.wait_ge(ada_copied, copied)
                act.dma_start(rows_dram[:, bass.ds(a * CW, CW)], ada_row[0:P:32, par, :]).then_inc(row_stored[par], 16)

            def attention_rows(i, m, par, before_):
                ada_row_out(i * 6 + (B1_0 + 2 * m + 2), par, before_, i * 3 + (2 * SECT + m + 1),
                            i * 3 + (2 * SECT + m))

            with act.Fori(0, PAIRS) as i:
                attention_rows(i, 0, 0, None)
                act.wait_ge(chunk_used, i * 6 + (B1_0 + 3))
                nc.scalar.copy(kT.rearrange("p h t -> p (h t)"), proj_ps[1][:, :]).then_inc(p1_out, 1)
                attention_rows(i, 1, 1, None)
                act.wait_ge(max_ready, i + 1)
                for h in range(2):
                    for b, (lo, hi) in enumerate(((0, P), (P, TRI))):
                        nc.scalar.activation(pp[:, h, lo:hi], pp[:, h, lo:hi], ACT.Exp, bias=smax[:, b, h:h + 1],
                                             accum_out=ssum[:, b, h:h + 1]).then_inc(exp_done, 1)
                attention_rows(i, 2, 0, i * 32 + 16)
                act.wait_ge(probs_turned, i * 2 + 2)
                nc.scalar.copy(ppT[:, 1, :], sc2_ps[:, 0:TRI]).then_inc(pT1_ready, 1)
                act.wait_ge(pv_done, i * 2 + 2)
                nc.scalar.copy(mixT[:, bass.ds(i * 2 + 1, 1), :], tr_ps[:, 0:T].rearrange("p (o t) -> p o t", o=1)
                               ).then_inc(mix_act, 1)
                act.wait_ge(row_stored[0], i * 32 + 32)
                act.wait_ge(row_stored[1], i * 16 + 16)

            def retention_rows(i, r, m, par, before_):
                a = 2 * SECT + 3 * PAIRS + 5 * r + m
                ada_row_out(i * 18 + (B2_0 + 9 * r + (2 * m + 2 if m < 4 else 9)), par, before_, i * 10 + (a + 1), i * 10 + a)

            with act.Fori(0, RHEADS // 2) as i:
                for r in range(2):
                    s0, s1 = 16 * (2 * PAIRS + 3 * r), 16 * (PAIRS + 2 * r)
                    head = i * 2 + r
                    retention_rows(i, r, 0, 0, None)
                    act.wait_ge(chunk_used, i * 18 + (B2_0 + 9 * r + 3))
                    nc.scalar.copy(kT.rearrange("p h t -> p (h t)"), proj_ps[1][:, :]).then_inc(p1_out, 1)
                    retention_rows(i, r, 1, 1, None)
                    retention_rows(i, r, 2, 0, i * 96 + (s0 + 16))
                    act.wait_ge(ret_pv, head + 1)
                    for b in range(NB):
                        nc.scalar.activation(junk[:, b * DR:(b + 1) * DR], pv_ps[:, b * DR:(b + 1) * DR], ACT.Square,
                                             accum_out=sumsq[:, b, 0:1]).then_inc(ret_sq, 1)
                    act.wait_ge(ret_ms, head + 1)
                    nc.scalar.activation(rt[:], ms[:], ACT.Sqrt).then_inc(ret_rt, 1)
                    act.wait_ge(chunk_used, i * 18 + (B2_0 + 9 * r + 7))
                    nc.scalar.activation(sg.rearrange("p b n -> p (b n)"), proj_ps[1][:, :], ACT.Silu).then_inc(p1_out, 1)
                    retention_rows(i, r, 3, 1, i * 64 + (s1 + 16))
                    retention_rows(i, r, 4, 0, i * 96 + (s0 + 32))
                    act.wait_ge(row_stored[0], i * 96 + (s0 + 48))
                    act.wait_ge(row_stored[1], i * 64 + (s1 + 32))

            act.wait_ge(row_stored[0], 16 * (2 * PAIRS + 3 * RHEADS))
            act.wait_ge(row_stored[1], 16 * (PAIRS + 2 * RHEADS))
            act.wait_ge(cols_made, 1)
            act.dma_start(buf_r[0:4, :], rows_dram[:, 2 * D:3 * D]).then_inc(gate_rows, 16)
            act.dma_start(buf_r[4:5, :], b_ada[:, 2 * D:3 * D]).then_inc(gate_rows, 16)
            for s in range(2):
                act.dma_start(mod_raw[:, :, s, :], rows_dram[:, (3 + s) * D:(4 + s) * D].rearrange(
                    "r (p k) -> p r k", k=K16)).then_inc(mod2_in, 16)
            for q in range(4):
                act.wait_ge(gm_ps, q + 1)
                nc.scalar.copy(buf_m[:, q * 512:(q + 1) * 512], turn_ps[q][:, :]).then_inc(gm_ready, 1)
            act.dma_start(buf_r[0:4, :], rows_dram[:, 5 * D:6 * D]).then_inc(gatef_rows, 16)
            act.dma_start(buf_r[4:5, :], b_ada[:, 5 * D:6 * D]).then_inc(gatef_rows, 16)
            for cc in range(4):
                for b in range(NB):
                    act.wait_ge(x1_piece, NB * cc + b + 1)
                    act.wait_ge(sq_done, NB + NB * cc + b)
                    nc.scalar.activation(junk, xs[:, b, cc * 512:(cc + 1) * 512], ACT.Square,
                                         accum_out=sumsq[:, b, cc:cc + 1]).then_inc(sq_done, 1)
            act.wait_ge(ms_done, 2)
            nc.scalar.activation(rt[:], ms[:], ACT.Sqrt).then_inc(rt_done, 1)
            act.wait_ge(col_ready, 2)
            for g in range(1, 8, 2):
                act.wait_ge(turned, 8 + g + 1)
                for j in range(2):
                    k = 2 * g + j
                    last = nc.scalar.activation(xnT[:, k, :], turn_ps[g % 4][:, j * T:(j + 1) * T], ACT.Identity,
                                                bias=shift[:, k:k + 1], scale=scale[:, k:k + 1])
                last.then_inc(evac_act, 1)
            for q in range(2):
                act.wait_ge(gf_ps, q + 1)
                nc.scalar.copy(gate_f[:, q * 512:(q + 1) * 512], ada_ps[q][:, :]).then_inc(gf_ready, 1)
            for j in range(2):
                act.wait_ge(route_exp_in, j + 1)
                nc.scalar.activation(exp_out[j], exp_in[j], ACT.Exp).then_inc(route_exp, 1)
            act.wait_ge(iota_ready, 2)
            for k in range(1, K16, 2):
                act.wait_ge(gathered, k + 1)
                nc.scalar.activation(xgT[:, k, 0:2 * T], turn_ps[k % 4][:, :], ACT.Identity, bias=shift[:, k:k + 1],
                                     scale=scale[:, k:k + 1]).then_inc(evac_act, 1)
            act.wait_ge(keys_ps, 1)
            act.dma_start(buf_r[:], norm_final_w.partition_broadcast(P)).then_inc(final_w_in, 16)

            def expert_act(n):
                act.wait_ge(chunk_used, n * 6 + (D_0 + 4))
                nc.scalar.activation(sil[0:CAP, :], h_ps[0:CAP, :], ACT.Silu).then_inc(sil_ready, 1)
                act.wait_ge(gT_ps, n + 1)
                nc.scalar.copy(ggT.rearrange("p k s -> p (k s)"), gt_ps[:, 0:K4 * CAP]).then_inc(gT_ready, 1)

            with act.Fori(0, E - 1) as n:
                expert_act(n)
            act.wait_ge(tables_ready, 1)
            items = act.value_load(n_over[0:1, 0:1], min_val=0, max_val=OVER)
            with act.Fori(0, OVER) as t:
                with act.If(t < items):
                    expert_act(t + (E - 1))
                act.end_ifs()
            expert_act(items + (E - 1))
            for j in range(4):
                act.wait_ge(added, items * 4 + (4 * (E - 1) + j + 1))
                b, q = j // 2, j % 2
                for half in range(2):
                    col = half * 1024 + q * 512
                    nc.scalar.activation(square[:, 2 * j + half, :], xs[:, b, col:col + 512], ACT.Square,
                                         accum_out=sumsq[:, b, 2 * q + half:2 * q + half + 1]).then_inc(sq_done, 1)
            act.wait_ge(ms_done, 3)
            nc.scalar.activation(rt[:], ms[:], ACT.Sqrt).then_inc(rt_done, 1)
            act.wait_ge(inverse_ready, 1)
            for b in range(NB):
                piece = answer[:, b, 1024:2048]
                nc.scalar.activation(piece, piece, ACT.Copy, scale=rinv[:, b:b + 1]).then_inc(out_act, 1)

        @block.vector
        def _(dve):
            v = nc.vector
            steps = [0]

            def step(ins):
                steps[0] += 1
                ins.then_inc(dve_step, 1)
                dve.wait_ge(dve_step, steps[0])

            def inverse_rms(nth, parts, ready=None):
                if parts > 1:
                    step(v.tensor_reduce(ms[:], sumsq[:, :, 0:parts], AX, ALU.add))
                    src = ms[:]
                else:
                    src = sumsq[:, :, 0]
                v.tensor_scalar(ms[:], src, 1.0 / D, EPS, ALU.mult, ALU.add).then_inc(ms_done, 1)
                dve.wait_ge(rt_done, nth)
                last = v.reciprocal(rinv[:], rt[:])
                if ready is None:
                    step(last)
                else:
                    last.then_inc(ready, 1)
                    dve.wait_ge(ready, 1)

            dve.wait_ge(sq_done, NB)
            inverse_rms(1, 1)
            for b in range(NB):
                last = v.tensor_scalar(xn[:, b, :], xs[:, b, :], rinv[:, b:b + 1], None, ALU.mult)
            last.then_inc(xn_ready, 1)
            for g in range(0, 8, 2):
                dve.wait_ge(turned, g + 1)
                v.tensor_copy(xnT[:, 2 * g:2 * g + 2, :].rearrange("p k t -> p (k t)"),
                              turn_ps[g % 4][:, :]).then_inc(evac_dve, 1)
            dve.wait_ge(const_in, 2 * 16)
            dve.wait_ge(cols_made, 1)
            v.tensor_tensor(shift[:], sc_ps[:, 0:K16], b_col[:, 0, :], ALU.add)
            step(v.tensor_tensor(scale[:], sc_ps[:, K16:2 * K16], b_col[:, 1, :], ALU.add))
            v.scalar_tensor_tensor(out=scale[:], in0=scale[:], scalar=1.0, in1=mix_w[:], op0=ALU.add,
                                   op1=ALU.mult).then_inc(col_ready, 1)
            dve.wait_ge(col_ready, 1)
            dve.wait_ge(evac_dve, 4)
            for k in range(0, K16, 2):
                last = v.tensor_scalar(xnT[:, k, :], xnT[:, k, :], scale[:, k:k + 1], shift[:, k:k + 1],
                                       ALU.mult, ALU.add)
            last.then_inc(mod_dve, 1)

            dve.wait_ge(bias_step, 5 + HEADS + 2)
            with dve.Fori(0, PAIRS) as i:
                dve.wait_ge(chunk_used, i * 6 + (B1_0 + 1))
                v.tensor_copy(qT.rearrange("p h t -> p (h t)"), proj_ps[0][:, :]).then_inc(p0_out, 1)
                for h, bank in enumerate((sc_ps, sc2_ps)):
                    dve.wait_ge(scored, i * 2 + (h + 1))
                    v.scalar_tensor_tensor(out=pp[:, h, :], in0=bank[:, 0:TRI], scalar=DH ** -0.5,
                                           in1=bias_sb[:, bass.ds(i * 2 + h, 1), :].rearrange("p o n -> p (o n)"),
                                           op0=ALU.mult, op1=ALU.add).then_inc(logits, 1)
                dve.wait_ge(logits, i * 4 + 2)
                v.tensor_reduce(smax[:, 0, :], pp[:, :, 0:P], AX, ALU.max).then_inc(logits, 1)
                v.tensor_reduce(smax[:, 1, :], pp[:, :, P:TRI], AX, ALU.max).then_inc(logits, 1)
                dve.wait_ge(logits, i * 4 + 4)
                v.tensor_scalar(smax[:], smax[:], -1.0, None, ALU.mult).then_inc(max_ready, 1)
                dve.wait_ge(exp_done, i * 4 + 4)
                v.reciprocal(sinv[:], ssum[:]).then_inc(ret_step, 1)
                dve.wait_ge(ret_step, i + 1)
                for h in range(2):
                    for b, (lo, hi) in enumerate(((0, P), (P, TRI))):
                        last = v.tensor_scalar(pp[:, h, lo:hi], pp[:, h, lo:hi], sinv[:, b, h:h + 1], None, ALU.mult)
                last.then_inc(probs_ready, 1)
                dve.wait_ge(chunk_used, i * 6 + (B1_0 + 5))
                v.tensor_copy(vv.rearrange("p b n -> p (b n)"), proj_ps[0][:, :]).then_inc(p0_out, 1)
                dve.wait_ge(probs_turned, i * 2 + 1)
                v.tensor_copy(ppT[:, 0, :], tr_ps[:, 0:TRI]).then_inc(pT0_ready, 1)
                dve.wait_ge(pv_done, i * 2 + 1)
                v.tensor_copy(mixT[:, bass.ds(i * 2, 1), :], pv_ps[:, 0:T].rearrange("p (o t) -> p o t", o=1)
                              ).then_inc(mix_dve, 1)

            dve.wait_ge(late_in, LATE * 16)
            with dve.Fori(0, RHEADS // 2) as i:
                for r in range(2):
                    head = i * 2 + r
                    used = B2_0 + 9 * r
                    dve.wait_ge(chunk_used, i * 18 + (used + 1))
                    v.tensor_copy(qT.rearrange("p h t -> p (h t)"), proj_ps[0][:, :]).then_inc(p0_out, 1)
                    dve.wait_ge(scored, head + (2 * PAIRS + 1))
                    v.tensor_tensor(scoreT, sc_ps[:, 0:TRI], decay_sb[:, bass.ds(head * TRI, TRI)],
                                    ALU.mult).then_inc(decayed, 1)
                    dve.wait_ge(chunk_used, i * 18 + (used + 5))
                    v.tensor_copy(vv.rearrange("p b n -> p (b n)"), proj_ps[0][:, :]).then_inc(p0_out, 1)
                    dve.wait_ge(ret_sq, head * 2 + 2)
                    v.tensor_scalar(ms[:], sumsq[:, :, 0], 1.0 / DR, EPS, ALU.mult, ALU.add).then_inc(ret_ms, 1)
                    dve.wait_ge(ret_rt, head + 1)
                    v.reciprocal(rinv[:], rt[:]).then_inc(ret_step, 1)
                    dve.wait_ge(ret_step, head * 3 + (PAIRS + 1))
                    for b in range(NB):
                        v.tensor_scalar(yy[:, b, :], pv_ps[:, b * DR:(b + 1) * DR], rinv[:, b:b + 1], None,
                                        ALU.mult).then_inc(ret_step, 1)
                    dve.wait_ge(ret_step, head * 3 + (PAIRS + 3))
                    dve.wait_ge(p1_out, head * 2 + (PAIRS + 2))
                    v.tensor_tensor(yy, yy, sg, ALU.mult).then_inc(ret_y, 1)
                    dve.wait_ge(ret_turned, head + 1)
                    for j in range(2):
                        last = v.tensor_scalar(mixT[:, bass.ds(head * 2 + (HEADS + j), 1), :],
                                               tr_ps[:, j * T:(j + 1) * T].rearrange("p (o t) -> p o t", o=1),
                                               ret_w[:, bass.ds(head * 2 + j, 1)], None, ALU.mult)
                    last.then_inc(ret_mix, 1)

            tmp = yy.rearrange("p b n -> p (b n)")
            tmps = [tmp, sg.rearrange("p b n -> p (b n)")]
            for cc in range(4):
                dve.wait_ge(chunk_used, C_0 + 2 * cc + 2)
                dve.wait_ge(gm_ready, cc + 1)
                for b in range(NB):
                    step(v.tensor_tensor(tmps[b], out_ps[cc % 2][b][:, :], buf_m[:, cc * 512:(cc + 1) * 512], ALU.mult))
                    piece = xs[:, b, cc * 512:(cc + 1) * 512]
                    v.tensor_tensor(piece, piece, tmps[b], ALU.add).then_inc(x1_piece, 1)
            dve.wait_ge(mod2_in, 32)
            step(v.tensor_reduce(sums2[:], mod_raw[:].rearrange("p r s k -> p (s k) r"), AX, ALU.add))
            v.tensor_tensor(shift[:], sums2[:, 0:K16], b_col[:, 3, :], ALU.add)
            step(v.tensor_tensor(scale[:], sums2[:, K16:2 * K16], b_col[:, 4, :], ALU.add))
            v.scalar_tensor_tensor(out=scale[:], in0=scale[:], scalar=1.0, in1=ffn_w[:], op0=ALU.add,
                                   op1=ALU.mult).then_inc(col_ready, 1)
            dve.wait_ge(col_ready, 2)
            dve.wait_ge(sq_done, NB + 4 * NB)
            inverse_rms(2, 4)
            for b in range(NB):
                last = v.tensor_scalar(xn[:, b, :], xs[:, b, :], rinv[:, b:b + 1], None, ALU.mult)
            last.then_inc(xn_ready, 1)
            for g in range(0, 8, 2):
                dve.wait_ge(turned, 8 + g + 1)
                for j in range(2):
                    k = 2 * g + j
                    last = v.tensor_scalar(xnT[:, k, :], turn_ps[g % 4][:, j * T:(j + 1) * T], scale[:, k:k + 1],
                                           shift[:, k:k + 1], ALU.mult, ALU.add)
                last.then_inc(evac_dve, 1)

            def wide(a, n):
                return a.rearrange("p (b o) -> p b o", o=1).to_broadcast([P, NB, n])

            def const(a, n):
                return a.rearrange("p (o n) -> p o n", o=1).to_broadcast([P, NB, n])

            def pick(values, rev, best, eq, top, onehot_):
                n = values.shape[2]
                step(v.tensor_reduce(best, values, AX, ALU.max))
                step(v.tensor_tensor(eq, values, wide(best, n), ALU.is_equal))
                step(v.tensor_tensor(eq, eq, const(rev, n), ALU.mult))
                step(v.tensor_reduce(top, eq, AX, ALU.max))
                step(v.tensor_tensor(onehot_, const(rev, n), wide(top, n), ALU.is_equal))

            dve.wait_ge(logits_ps, 1)
            dve.wait_ge(consts_made, 9)
            step(v.tensor_tensor(lg, proj_ps[0][:, 0:72].rearrange("p (b n) -> p b n", b=NB),
                                 const(b_route[:], 36), ALU.add))
            pick(lg[:, :, 0:4], rev8[:, 4:8], gmax, eq4, top1, og)
            v.tensor_tensor(exp_in[0].rearrange("p (b n) -> p b n", b=NB), lg[:, :, 0:4], wide(gmax, 4),
                            ALU.subtract).then_inc(route_exp_in, 1)
            lgr = lg[:, :, 4:36].rearrange("p b (g e) -> p b g e", g=GROUPS)
            for b in range(NB):
                last = v.tensor_tensor(lsel[:, b], lgr[:, b], og[:, b].rearrange("p (g o) -> p g o", o=1).to_broadcast(
                    [P, GROUPS, EPG]), ALU.mult)
            step(last)
            step(v.tensor_reduce(el, lsel.rearrange("p b g e -> p b e g"), AX, ALU.add))
            pick(el, rev8[:], m1, eq8, top1, o1)
            step(v.scalar_tensor_tensor(out=el, in0=o1, scalar=-1e30, in1=el, op0=ALU.mult, op1=ALU.add))
            pick(el, rev8[:], m2, eq8, top1, o2)
            v.tensor_tensor(exp_in[1], m2, m1, ALU.subtract).then_inc(route_exp_in, 1)
            dve.wait_ge(route_exp, 1)
            step(v.tensor_reduce(gsum, exp_out[0].rearrange("p (b n) -> p b n", b=NB), AX, ALU.add))
            for q, o in enumerate((o1, o2)):
                for b in range(NB):
                    last = v.tensor_tensor(chosen[:, q, b].rearrange("p (g e) -> p g e", g=GROUPS),
                                           og[:, b].rearrange("p (g o) -> p g o", o=1).to_broadcast([P, GROUPS, EPG]),
                                           o[:, b].rearrange("p (o e) -> p o e", o=1).to_broadcast([P, GROUPS, EPG]),
                                           ALU.mult)
            step(last)
            v.tensor_tensor(both, chosen[:, 0], chosen[:, 1], ALU.add).then_inc(picks, 1)
            dve.wait_ge(route_exp, 2)
            step(v.tensor_scalar(w_tok[:, 1, :], exp_out[1], 1.0, None, ALU.add))
            step(v.tensor_tensor(w_tok[:, 1, :], w_tok[:, 1, :], gsum, ALU.mult))
            step(v.reciprocal(w_tok[:, 0, :], w_tok[:, 1, :]))
            step(v.tensor_tensor(w_tok[:, 1, :], w_tok[:, 0, :], exp_out[1], ALU.mult))
            dve.wait_ge(counts_ps, 1)
            v.tensor_copy(cnt, proj_ps[1][:, 0:3 * E])
            step(v.tensor_copy(cnt_col[:, 0:1], ada_ps[0][0:E, 0:1]))
            step(v.tensor_scalar(cnt_col[:, 1:2], cnt_col[:, 0:1], float(CAP), None, ALU.is_gt))
            for j in range(2, 4):
                step(v.scalar_tensor_tensor(out=cnt_col[:, 1:2], in0=cnt_col[:, 0:1], scalar=float(CAP * j),
                                            in1=cnt_col[:, 1:2], op0=ALU.is_gt, op1=ALU.add))
            v.tensor_copy(cnt_rep, cnt_col.rearrange("p (q o) -> p q o", o=1).to_broadcast([E, 2, P])).then_inc(counts_sb, 1)
            dve.wait_ge(starts_ps, 1)
            step(v.tensor_copy(first, ada_ps[1][:, 0:2 * E]))
            ranks = cnt[:, E:3 * E].rearrange("p (b e) -> p b e", b=NB)
            v.tensor_tensor(where[:, 0], ranks, const(first[:, 0:E], E), ALU.add)
            step(v.tensor_tensor(where[:, 1], ranks, e256[:].to_broadcast([P, NB, E]), ALU.add))
            for s in range(2):
                for q in range(2):
                    step(v.tensor_tensor(wtmp, chosen[:, q], where[:, s], ALU.mult))
                    step(v.tensor_reduce(slot_key[:, s, q, :], wtmp, AX, ALU.add))
            dve.wait_ge(iota_ready, 1)
            dve.wait_ge(gf_ps, 2)
            for b in range(NB):
                step(v.tensor_scalar(onehot[:, b, :], iota_s, slot_key[:, 0, 0, b:b + 1], None, ALU.is_equal))
                last = v.scalar_tensor_tensor(out=onehot[:, b, :], in0=iota_s, scalar=slot_key[:, 0, 1, b:b + 1],
                                              in1=onehot[:, b, :], op0=ALU.is_equal, op1=ALU.add)
            last.then_inc(onehot_ready, 1)
            for b in range(NB):
                for q in range(4):
                    s = slot_key[:, 1, q, b:b + 1] if q < 2 else w_tok[:, q - 2, b:b + 1]
                    last = v.tensor_scalar(diag[:, b, q, :], ident[:], s, None, ALU.mult)
            last.then_inc(diag_ready, 1)
            dve.wait_ge(iota_ready, 2)
            for k in range(0, K16, 2):
                dve.wait_ge(gathered, k + 1)
                v.tensor_scalar(xgT[:, k, 0:2 * T], turn_ps[k % 4][:, :], scale[:, k:k + 1], shift[:, k:k + 1],
                                ALU.mult, ALU.add).then_inc(evac_dve, 1)
            v.tensor_copy(start_tab[:, 0:E], first[0:1, 0:E]).then_inc(starts_ready, 1)
            dve.wait_ge(keys_ps, 1)
            for b in range(NB):
                last = v.tensor_copy(keys[:, :, b * P:(b + 1) * P],
                                     proj_ps[b][:, :].rearrange("p (q n) -> p q n", q=4))
            last.then_inc(keys_ready, 1)

            def tables():
                over, upto, less = tab[:, 0:E], tab[:, E:2 * E], first[:, E:2 * E]
                step(v.tensor_scalar(over, cnt[:, 0:E], float(CAP), None, ALU.is_gt))
                for j in range(2, 4):
                    step(v.scalar_tensor_tensor(out=over, in0=cnt[:, 0:E], scalar=float(CAP * j), in1=over,
                                                op0=ALU.is_gt, op1=ALU.add))
                step(v.tensor_tensor(upto, over, less, ALU.add))
                step(v.tensor_copy(n_over[:], upto[0:1, E - 1:E]))

                def by_expert(a):
                    return a.rearrange("p (o e) -> p o e", o=1).to_broadcast([P, OVER + 1, E])

                def by_item(a):
                    return a.rearrange("p (t o) -> p t o", o=1).to_broadcast([P, OVER + 1, E])

                step(v.tensor_tensor(is_item, by_expert(less), by_item(over_t[:]), ALU.is_le))
                step(v.tensor_tensor(item_tmp, by_expert(upto), by_item(over_t[:]), ALU.is_gt))
                step(v.tensor_tensor(is_item, is_item, item_tmp, ALU.mult))
                step(v.tensor_reduce(item_is, is_item, AX, ALU.add))
                for src, dst, last_one in ((first[:, 0:E], item_slot, first[:, E - 1:E]),
                                           (e256[:, 0, :], item_key, e256[:, 0, E - 1:E])):
                    step(v.scalar_tensor_tensor(out=over, in0=less, scalar=-float(CAP), in1=src, op0=ALU.mult,
                                                op1=ALU.add))
                    step(v.tensor_tensor(item_tmp, is_item, by_expert(over), ALU.mult))
                    step(v.tensor_reduce(dst, item_tmp, AX, ALU.add))
                    step(v.tensor_scalar(item_pad, over_cap[:], last_one, None, ALU.subtract))
                    step(v.tensor_tensor(item_pad, item_pad, item_is, ALU.mult))
                    step(v.tensor_tensor(dst, dst, item_pad, ALU.add))
                    step(v.tensor_scalar(dst, dst, last_one, None, ALU.add))
                step(v.tensor_copy(start_tab[:, E - 1:E + OVER], item_slot[0:1, :]))
                step(v.tensor_copy(key_tab[:, E - 1:E + OVER], item_key))
                step(v.tensor_tensor(item_tmp, is_item, by_expert(e256[:, 0, :]), ALU.mult))
                step(v.tensor_reduce(item_pad, item_tmp, AX, ALU.add))
                v.tensor_scalar(item_e[:, 0:OVER + 1], item_pad[0:1, :], 1.0 / 256, None,
                                ALU.mult).then_inc(tables_ready, 1)

            def fetch(n):
                dve.wait_ge(chunk_used, n * 6 + (D_0 - 2))
                s = dve.value_load(start_tab[0:1, bass.ds(n, 1)], min_val=0, max_val=2 * T)
                v.tensor_copy(xe, xgT[:, :, bass.ds(s, CAP)]).then_inc(xe_ready, 1)

            def gate_answers(n):
                dve.wait_ge(chunk_used, n * 6 + (D_0 + 6))
                for q in range(2):
                    last = v.tensor_tensor(yg[:, q * 512:(q + 1) * 512], y_ps[q][:, :], gate_f[:, q * 512:(q + 1) * 512],
                                           ALU.mult)
                last.then_inc(yg_ready, 1)

            def weights_of(n):
                v.tensor_tensor(key_col[:], lane[:], key_tab[:, bass.ds(n, 1)], ALU.add).then_inc(comb_step, 1)
                dve.wait_ge(comb_step, n * 3 + 1)
                v.scalar_tensor_tensor(out=comb, in0=keys[:, 0, :], scalar=key_col[:, 0:1], in1=keys[:, 2, :],
                                       op0=ALU.is_equal, op1=ALU.mult).then_inc(comb_step, 1)
                v.scalar_tensor_tensor(out=comb2, in0=keys[:, 1, :], scalar=key_col[:, 0:1], in1=keys[:, 3, :],
                                       op0=ALU.is_equal, op1=ALU.mult).then_inc(comb_step, 1)
                dve.wait_ge(comb_step, n * 3 + 3)
                dve.wait_ge(yg_ready, n + 1)
                v.tensor_tensor(comb, comb, comb2, ALU.add).then_inc(comb_ready, 1)

            def gated(n):
                dve.wait_ge(sil_ready, n + 1)
                v.tensor_tensor(gg[0:CAP, :], sil[0:CAP, :], h_ps[CAP:2 * CAP, :], ALU.mult).then_inc(g_ready, 1)

            def add_pair(n, j):
                b, q = j // 2, j % 2
                dve.wait_ge(add_done, n * 4 + (j + 1))
                for half in range(2):
                    col = half * 1024 + q * 512
                    piece = xs[:, b, col:col + 512]
                    last = v.tensor_tensor(piece, piece, add_ps[2 * (j % 2) + half][:, :], ALU.add)
                last.then_inc(added, 1)

            def add_answers(n):
                for j in range(4):
                    add_pair(n, j)

            dve.wait_ge(starts_ready, 1)
            dve.wait_ge(evac_act, 16)
            dve.wait_ge(evac_dve, 16)
            dve.wait_ge(keys_ready, 1)
            fetch(0)
            tables()

            def item(n):
                fetch(n)
                gate_answers(n - 1)
                weights_of(n - 1)
                gated(n)
                add_answers(n - 1)

            gated(0)
            with dve.Fori(1, E - 1) as n:
                item(n)
            dve.wait_ge(tables_ready, 1)
            items = dve.value_load(n_over[0:1, 0:1], min_val=0, max_val=OVER)
            with dve.Fori(0, OVER) as t:
                with dve.If(t < items):
                    item(t + (E - 1))
                dve.end_ifs()
            item(items + (E - 1))
            gate_answers(items + (E - 1))
            weights_of(items + (E - 1))

            def weigh(b):
                return v.tensor_tensor(answer[:, b, :], xs[:, b, :], buf_r[:], ALU.mult)

            dve.wait_ge(final_w_in, 16)
            for j in range(4):
                add_pair(items + (E - 1), j)
                if j == 1:
                    dve.wait_ge(added, items * 4 + (4 * (E - 1) + 2))
                    weigh(0)
            dve.wait_ge(added, items * 4 + 4 * E)
            weigh(1).then_inc(weighted, 1)
            dve.wait_ge(weighted, 1)
            dve.wait_ge(sq_done, NB + 4 * NB + 8)
            inverse_rms(3, 4, inverse_ready)
            for b in range(NB):
                piece = answer[:, b, 0:1024]
                v.tensor_scalar(piece, piece, rinv[:, b:b + 1], None, ALU.mult).then_inc(out_dve, 1)


def decays():
    import numpy as np

    t = np.arange(P, dtype=np.float32)
    far = t[:, None] - t[None, :]
    causal = far >= 0
    decay = np.zeros((P, RHEADS, TRI), np.float32)
    for h in range(RHEADS):
        gamma = 1.0 - 2.0 ** (-5.0 - h)
        own = np.where(causal, gamma ** np.maximum(far, 0), 0.0).T
        decay[:, h] = np.concatenate([own, gamma ** (far + P).T, own], 1) * DR ** -0.5
    return decay.astype(np.float32).reshape(P, -1)


_INS = ["x", "c", "w_ada", "b_ada", "norm_mix_w", "w_in", "ret_norm_w", "w_out", "norm_ffn_w", "w_group",
        "b_group", "w_router", "b_router", "w1", "w3", "w2", "norm_final_w"]


def kernel(**inputs):
    import numpy as np
    import concourse.bacc as bacc
    from concourse.bass_utils import run_bass_kernel_spmd as run

    nc = bacc.Bacc("TRN2", target_bir_lowering=False, num_devices=1)
    arrays = {f"in_{n}": np.ascontiguousarray(inputs[n]) for n in _INS}
    arrays["decay"] = decays()
    args = [nc.dram_tensor(n, a.shape, mybir.dt.from_np(a.dtype), kind="ExternalInput").ap() for n, a in arrays.items()]
    rows_dram = nc.dram_tensor("ada_rows", [4, 6 * D], F32, kind="Internal").ap()
    out = nc.dram_tensor("out", [1, T, D], F32, kind="ExternalOutput").ap()
    build(nc, *args, rows_dram, out)
    return run(nc, [arrays], core_ids=[0]).results[0]["out"]
```

```python
from contextlib import ExitStack

import concourse.bass as bass
from concourse import mybir

F32 = mybir.dt.float32
F32R = mybir.dt.float32r
I32 = mybir.dt.int32
ALU = mybir.AluOpType
ACT = mybir.ActivationFunctionType
AX = mybir.AxisListType.X

P = 128
D = 2048
T = 256
NB = T // P
K16 = D // P
HEADS, DH = 8, 128
PAIRS = HEADS // 2
RHEADS, DR = 4, 256
CW = 256
SECT = D // CW
E, DE = 32, 512
GROUPS, EPG = 4, 8
K4 = DE // P
CAP = 64
OVER = (2 * T - 1) // CAP
SLOTS = 2 * T + CAP
RING = 6
LATE = 10
CH = 4096
EPS = 1e-6
ROUTE_AT, ROUTE = 2816, 1280
QUARTER = CH // 4
TRI = 384
N_A, N_B1, N_B2, N_C = 2 * SECT, 6 * PAIRS, 9 * RHEADS, 8
B1_0, B2_0 = N_A, N_A + N_B1
C_0 = B2_0 + N_B2
W_B2 = 4 * 3 * PAIRS
W_C = W_B2 + 4 * 4 * RHEADS
ROWS = 5
D_0 = C_0 + N_C


def build(nc, x, c, w_ada, b_ada, norm_mix_w, w_in, ret_norm_w, w_out, norm_ffn_w, w_group, b_group,
          w_router, b_router, w1, w3, w2, norm_final_w, decay, rows_dram, out):
    ctx = ExitStack()
    with ctx:
        def sb(name, shape, dt=F32):
            return ctx.enter_context(nc.sbuf_tensor(name, shape, dt))

        def sem(name):
            return ctx.enter_context(nc.semaphore(name))

        def place(name, shape):
            tile_ = sb(name, shape)
            return tile_, nc.sbuf_base - 4 * shape[1] * (shape + [1])[2]

        def in_place_of(name, shape, offset):
            return nc.alloc_sbuf_tensor_at(name, shape, F32R, offset=offset)

        ring = sb("ring", [P, RING, CH])
        buf_a, at_a = place("buf_a", [P, CH])
        xs, at_x = place("xs", [P, NB, D])
        buf_b, at_b = place("buf_b", [P, CH])
        buf_g, at_g = place("buf_g", [P, K16 * SLOTS])
        buf_mr, at_mr = place("buf_mr", [P, 2 * D])
        buf_m = buf_mr[:, 0:D]
        buf_r = buf_mr[:, D:2 * D]
        w_hi = in_place_of("w_hi", [P, 2, QUARTER], at_a)
        w_lo = in_place_of("w_lo", [P, 2, QUARTER], at_a + 4 * 2 * QUARTER)
        h_hi = in_place_of("h_hi", [P, K16, T], at_mr)
        h_lo = in_place_of("h_lo", [P, K16, T], at_x)
        mix_hi = in_place_of("mix_hi", [P, K16, T], at_g)
        mix_lo = in_place_of("mix_lo", [P, K16, T], at_b)
        c_pad = sb("c_pad", [P, K16, 32])
        ident = sb("ident", [P, P])
        ones = sb("ones", [P, P])
        before = sb("before", [P, P])
        w_route = sb("w_route", [P, K16, 4 + E])
        b_route = sb("b_route", [P, 4 + E])
        c_col = sb("c_col", [P, K16])
        b_col = sb("b_col", [P, 6, K16])
        mix_w = sb("mix_w", [P, K16])
        ffn_w = sb("ffn_w", [P, K16])
        ret_w = sb("ret_w", [P, 8])
        mod_raw = sb("mod_raw", [P, 4, 2, K16])
        shift = sb("shift", [P, K16])
        scale = sb("scale", [P, K16])
        sumsq = sb("sumsq", [P, NB, 4])
        ms = sb("ms", [P, NB])
        rt = sb("rt", [P, NB])
        rinv = sb("rinv", [P, NB])
        smax = sb("smax", [P, 2, 2])
        ssum = sb("ssum", [P, 2, 2])
        sinv = sb("sinv", [P, 2, 2])
        rev8 = sb("rev8", [P, 8])
        e256 = sb("e256", [P, 1, E])
        lane = sb("lane", [P, 1])
        key_tab = sb("key_tab", [P, E + OVER + 1])
        start_tab = sb("start_tab", [1, E + OVER + 1], I32)
        item_e = sb("item_e", [1, OVER + 1], I32)
        n_over = sb("n_over", [1, 1], I32)
        key_col = sb("key_col", [P, 1])
        over_cap = sb("over_cap", [P, OVER + 1])
        over_t = sb("over_t", [P, OVER + 1])
        sums2 = sb("sums2", [P, 2 * K16])

        used = [0]

        def small(n, rows=P):
            used[0] += n
            assert used[0] <= ROUTE
            return buf_a[0:rows, ROUTE_AT + used[0] - n:ROUTE_AT + used[0]]

        lg = small(NB * 36).rearrange("p (b n) -> p b n", b=NB)
        gmax, top1, m1, m2, gsum = (small(NB) for _ in range(5))
        eq4 = small(NB * 4).rearrange("p (b n) -> p b n", b=NB)
        og = small(NB * 4).rearrange("p (b n) -> p b n", b=NB)
        exp_in = [small(NB * 4), small(NB)]
        exp_out = [small(NB * 4), small(NB)]
        lsel = small(NB * E).rearrange("p (b g e) -> p b g e", b=NB, g=GROUPS)
        el, eq8, o1, o2 = (small(NB * EPG).rearrange("p (b e) -> p b e", b=NB) for _ in range(4))
        chosen = small(2 * NB * E).rearrange("p (q b e) -> p q b e", q=2, b=NB)
        both = small(NB * E).rearrange("p (b e) -> p b e", b=NB)
        w_tok = small(2 * NB).rearrange("p (q b) -> p q b", q=2)
        cnt = small(3 * E)
        cnt_col = small(2, E)
        cnt_rep = buf_a[0:E, 1280:1536].rearrange("p (q m) -> p q m", q=2)
        first = small(2 * E)
        where = small(2 * NB * E).rearrange("p (s b e) -> p s b e", s=2, b=NB)
        wtmp = small(NB * E).rearrange("p (b e) -> p b e", b=NB)
        slot_key = small(2 * 2 * NB).rearrange("p (s q b) -> p s q b", s=2, q=2)
        tab = small(2 * E)
        item_is, item_slot, item_key, item_pad = (small(OVER + 1) for _ in range(4))

        x_a = buf_a[:, :].rearrange("p (b d) -> p b d", b=NB)
        xnT = xs[:, :, :].rearrange("p b d -> p (b d)").rearrange("p (k t) -> p k t", k=K16)
        xn2T = buf_a[:, :].rearrange("p (k t) -> p k t", k=K16)
        xn = buf_b[:, :].rearrange("p (b d) -> p b d", b=NB)
        xn_k = buf_b[:, :].rearrange("p (b q k) -> p b k q", b=NB, k=K16)
        mixT = buf_b[:, :].rearrange("p (k t) -> p k t", k=K16)
        at = [0]

        def part(n):
            at[0] += n
            return buf_g[:, at[0] - n:at[0]]

        bias_sb = part(HEADS * T).rearrange("p (h n) -> p h n", h=HEADS)
        decay_sb = part(RHEADS * T)
        qT = part(512).rearrange("p (h t) -> p h t", h=2)
        kT = part(512).rearrange("p (h t) -> p h t", h=2)
        vv = part(512).rearrange("p (b n) -> p b n", b=2)
        pp = part(2 * TRI).rearrange("p (h n) -> p h n", h=2)
        ppT = part(2 * TRI).rearrange("p (h n) -> p h n", h=2)
        yy = part(512).rearrange("p (b n) -> p b n", b=2)
        sg = part(512).rearrange("p (b n) -> p b n", b=2)
        junk = part(512)
        ada_row = part(ROWS * CW).rearrange("p (m n) -> p m n", m=ROWS)
        assert at[0] <= K16 * SLOTS
        scoreT = pp[:, 0, :]
        xgT = buf_g[:, :].rearrange("p (k s) -> p k s", k=K16)
        is_item = buf_m[:, 1024:1024 + (OVER + 1) * E].rearrange("p (t e) -> p t e", e=E)
        item_tmp = buf_m[:, 1280:1280 + (OVER + 1) * E].rearrange("p (t e) -> p t e", e=E)
        onehot = buf_r[:, 0:1024].rearrange("p (b s) -> p b s", b=NB)
        diag = buf_r[:, 1024:2048].rearrange("p (b q n) -> p b q n", b=NB, q=4)
        iota_s = buf_m[:, 1024:1536]
        gate_f = buf_m[:, 0:1024]
        keys = buf_a[:, 0:1024].rearrange("p (q t) -> p q t", q=4)
        comb = buf_a[:, 1024:1280]
        comb2 = buf_a[:, 1280:1536]
        sil = buf_a[:, 1536:2048]
        gg = buf_a[:, 2048:2560]
        ggT = buf_a[:, 2560:2560 + K4 * CAP].rearrange("p (k s) -> p k s", k=K4)
        xe = buf_b[:, 0:K16 * CAP].rearrange("p (k s) -> p k s", k=K16)
        yg = buf_b[:, 1024:2048]
        answer = buf_g[:, 0:NB * D].rearrange("p (b d) -> p b d", b=NB)
        square = buf_g[:, NB * D:NB * D + 8 * 512].rearrange("p (j n) -> p j n", n=512)

        banks = [ctx.enter_context(nc.psum_tensor(f"bank{i}", [P, 512], F32)) for i in range(8)]
        ada_ps = banks[0:2]
        proj_ps = banks[2:4]
        turn_ps = banks[4:8]
        sc_ps, sc2_ps, tr_ps, pv_ps = banks[4:8]
        k_ps = [pv_ps, sc2_ps]
        out_ps = [banks[2:4], banks[0:2]]
        h_ps, gt_ps = banks[0], banks[1]
        y_ps = banks[2:4]
        add_ps = banks[4:8]

        small_in = sem("small_in")
        x_in = sem("x_in")
        const_in = sem("const_in")
        late_in = sem("late_in")
        arrived = [sem(f"arrived{i}") for i in range(RING)]
        chunk_used = sem("chunk_used")
        w_hi_ready = sem("w_hi_ready")
        w_lo_ready = sem("w_lo_ready")
        split_used = sem("split_used")
        h_hi_ready = sem("h_hi_ready")
        h_lo_ready = sem("h_lo_ready")
        mix_hi_ready = sem("mix_hi_ready")
        mix_lo_ready = sem("mix_lo_ready")
        consts_made = sem("consts_made")
        bias_step = sem("bias_step")
        c_ready = sem("c_ready")
        sq_done = sem("sq_done")
        ms_done = sem("ms_done")
        rt_done = sem("rt_done")
        rinv_done = sem("rinv_done")
        xn_ready = sem("xn_ready")
        turned = sem("turned")
        evac_dve = sem("evac_dve")
        evac_act = sem("evac_act")
        ada_copied = sem("ada_copied")
        row_stored = [sem(f"row_stored{m}") for m in range(ROWS)]
        cols_made = sem("cols_made")
        dve_step = sem("dve_step")
        mod_dve = sem("mod_dve")
        mod_act = sem("mod_act")
        col_ready = sem("col_ready")
        p0_out = sem("p0_out")
        p1_out = sem("p1_out")
        scored = sem("scored")
        logits = sem("logits")
        max_ready = sem("max_ready")
        exp_done = sem("exp_done")
        probs_ready = sem("probs_ready")
        probs_turned = sem("probs_turned")
        pT0_ready = sem("pT0_ready")
        pT1_ready = sem("pT1_ready")
        pv_done = sem("pv_done")
        mix_dve = sem("mix_dve")
        mix_act = sem("mix_act")
        decayed = sem("decayed")
        ret_pv = sem("ret_pv")
        ret_sq = sem("ret_sq")
        ret_ms = sem("ret_ms")
        ret_rt = sem("ret_rt")
        ret_step = sem("ret_step")
        ret_y = sem("ret_y")
        ret_turned = sem("ret_turned")
        ret_mix = sem("ret_mix")
        gate_rows = sem("gate_rows")
        gatef_rows = sem("gatef_rows")
        mod2_in = sem("mod2_in")
        gm_ps = sem("gm_ps")
        gm_ready = sem("gm_ready")
        x1_piece = sem("x1_piece")
        gf_ps = sem("gf_ps")
        gf_ready = sem("gf_ready")
        logits_ps = sem("logits_ps")
        route_exp_in = sem("route_exp_in")
        route_exp = sem("route_exp")
        picks = sem("picks")
        counts_ps = sem("counts_ps")
        counts_sb = sem("counts_sb")
        starts_ps = sem("starts_ps")
        onehot_ready = sem("onehot_ready")
        diag_ready = sem("diag_ready")
        keys_ps = sem("keys_ps")
        keys_ready = sem("keys_ready")
        iota_ready = sem("iota_ready")
        gathered = sem("gathered")
        starts_ready = sem("starts_ready")
        tables_ready = sem("tables_ready")
        final_w_in = sem("final_w_in")
        xe_ready = sem("xe_ready")
        sil_ready = sem("sil_ready")
        g_ready = sem("g_ready")
        gT_ps = sem("gT_ps")
        gT_ready = sem("gT_ready")
        yg_ready = sem("yg_ready")
        comb_step = sem("comb_step")
        comb_ready = sem("comb_ready")
        add_done = sem("add_done")
        added = sem("added")
        out_dve = sem("out_dve")
        out_act = sem("out_act")
        weighted = sem("weighted")
        inverse_ready = sem("inverse_ready")
        stored = sem("stored")

        ada_v = w_ada[0].rearrange("(p k) n -> p k n", k=K16)
        win_v = w_in[0].rearrange("(p k) n -> p k n", k=K16)
        wout_v = w_out[0].rearrange("(k p) n -> p k n", p=P)
        w13_v = [w[0].rearrange("e (p k) n -> p e k n", k=K16) for w in (w1, w3)]
        w2_v = w2[0].rearrange("e (p k) n -> p e k n", k=K4)

        def slot_cols(n):
            return ring[:, n % RING, :].rearrange("p (k n) -> p k n", k=K16)

        def slot_512(n):
            return ring[:, n % RING, :].rearrange("p (k n) -> p k n", n=512)

        def slot_w2(n):
            return ring[:, n % RING, :].rearrange("p (k n) -> p k n", n=D)

        def quarter(n, qr):
            return ring[:, n % RING, qr * QUARTER:(qr + 1) * QUARTER]

        def wait(eng, s, value):
            if isinstance(value, int) and value <= 0:
                return
            eng.wait_ge(s, value)

        def await_chunk(eng, n, turns=0):
            eng.wait_ge(arrived[n % RING], (turns + n // RING + 1) * 16)

        block = ctx.enter_context(nc.Block())

        @block.sync
        def _(sp):
            def load(n, turns, dst, src):
                wait(sp, chunk_used, turns * RING + (n - RING + 1))
                sp.dma_start(dst, src).then_inc(arrived[n % RING], 16)

            def ada(n, turns, a):
                load(n, turns, slot_cols(n), ada_v[:, :, bass.ds(a * CW, CW)])

            def win(n, turns, col):
                load(n, turns, slot_cols(n), win_v[:, :, bass.ds(col, CW)])

            def expert(n0, turns, e):
                for hf in range(2):
                    for m in range(2):
                        n = n0 + 2 * hf + m
                        load(n, turns, slot_512(n), w13_v[m][:, e, 8 * hf:8 * hf + 8, :].rearrange("p o k n -> p (o k) n"))
                for hf in range(2):
                    n = n0 + 4 + hf
                    load(n, turns, slot_w2(n), w2_v[:, e, 2 * hf:2 * hf + 2, :].rearrange("p o k n -> p (o k) n"))

            sp.dma_start(c_col[:], c.rearrange("o (p k) -> p (o k)", k=K16)).then_inc(small_in, 16)
            sp.dma_start(x_a, x.rearrange("o (b p) d -> p (o b) d", p=P)).then_inc(x_in, 16)
            for n in range(RING):
                ada(n, 0, n)
            sp.dma_start(b_col[:], b_ada.rearrange("o (s p k) -> p (o s) k", k=K16, p=P)).then_inc(const_in, 16)
            sp.dma_start(mix_w[:], norm_mix_w.rearrange("o (p k) -> p (o k)", k=K16)).then_inc(const_in, 16)
            for n in range(RING, N_A):
                ada(n, 0, n)
            with sp.Fori(0, PAIRS) as i:
                for m in range(3):
                    win(B1_0 + 2 * m, i, 1024 * m + i * CW)
                    ada(B1_0 + 2 * m + 1, i, 2 * SECT + m + i * 3)
            sp.dma_start(ffn_w[:], norm_ffn_w.rearrange("o (p k) -> p (o k)", k=K16)).then_inc(late_in, 16)
            with nc.allow_non_contiguous_dma(reason="1024 weights, once"):
                sp.dma_start(ret_w[:], ret_norm_w.rearrange("o (k p) -> p (o k)", p=P)).then_inc(late_in, 16)
                sp.dma_start(w_route[:, :, 0:4], w_group.rearrange("o (p k) g -> p (o k) g", k=K16)).then_inc(late_in, 16)
                for g in range(GROUPS):
                    sp.dma_start(w_route[:, :, 4 + EPG * g:4 + EPG * (g + 1)],
                                 w_router[0, g].rearrange("(p k) e -> p k e", k=K16)).then_inc(late_in, 16)
            sp.dma_start(b_route[:, 0:4], b_group[0].partition_broadcast(P)).then_inc(late_in, 16)
            sp.dma_start(b_route[:, 4:4 + E], b_router.rearrange("o g e -> (o g e)").partition_broadcast(P)).then_inc(late_in, 16)
            sp.dma_start(decay_sb, decay).then_inc(late_in, 16)
            with sp.Fori(0, RHEADS // 2) as i:
                for r in range(2):
                    n = B2_0 + 9 * r
                    for m in range(4):
                        win(n + 2 * m, i * 3, 3072 + 1024 * m + r * CW + i * (2 * CW))
                        ada(n + 2 * m + 1, i * 3, 2 * SECT + 3 * PAIRS + 5 * r + m + i * 10)
                    ada(n + 8, i * 3, 2 * SECT + 3 * PAIRS + 5 * r + 4 + i * 10)
            for cc in range(4):
                for hf in range(2):
                    n = C_0 + 2 * cc + hf
                    load(n, 0, slot_512(n), wout_v[:, 8 * hf:8 * hf + 8, cc * 512:(cc + 1) * 512])
                if cc == 1:
                    sp.wait_ge(split_used, W_C)
                    sp.dma_start(xs[:], x.rearrange("o (b p) d -> p (o b) d", p=P)).then_inc(x_in, 16)
            with sp.Fori(0, E - 1) as e:
                expert(D_0, e, bass.ds(e, 1))
            sp.wait_ge(tables_ready, 1)
            items = sp.value_load(n_over[0:1, 0:1], min_val=0, max_val=OVER)
            with sp.Fori(0, OVER) as t:
                with sp.If(t < items):
                    e = sp.value_load(item_e[0:1, bass.ds(t, 1)], min_val=0, max_val=E - 1)
                    expert(D_0, t + (E - 1), bass.ds(e, 1))
                sp.end_ifs()
            expert(D_0, items + (E - 1), slice(E - 1, E))
            for h in range(4):
                b, q = h // 2, h % 2
                sp.wait_ge((out_dve, out_act)[q], b + 1)
                sp.dma_start(out[0, b * P:(b + 1) * P, q * 1024:(q + 1) * 1024],
                             answer[:, b, q * 1024:(q + 1) * 1024]).then_inc(stored, 16)
            sp.wait_ge(stored, 64)

        @block.gpsimd
        def _(pool):
            nc.gpsimd.memset(c_pad[:], 0.0).then_inc(consts_made, 1)
            nc.gpsimd.memset(ones[:], 1.0).then_inc(consts_made, 1)
            pool.wait_ge(consts_made, 2)
            nc.gpsimd.affine_select(out=ident[:], in_=ones[:], compare_op=ALU.is_equal, fill=0.0, base=0,
                                    pattern=[[-1, P]], channel_multiplier=1).then_inc(consts_made, 1)
            nc.gpsimd.affine_select(out=before[:], in_=ones[:], compare_op=ALU.is_gt, fill=0.0, base=0,
                                    pattern=[[1, P]], channel_multiplier=-1).then_inc(consts_made, 1)
            nc.gpsimd.iota(rev8[:], pattern=[[-1, 8]], base=8, channel_multiplier=0,
                           allow_small_or_imprecise_dtypes=True).then_inc(consts_made, 1)
            nc.gpsimd.iota(e256[:, 0, :], pattern=[[256, E]], base=0, channel_multiplier=0,
                           allow_small_or_imprecise_dtypes=True).then_inc(consts_made, 1)
            nc.gpsimd.iota(key_tab[:, 0:E], pattern=[[256, E]], base=0, channel_multiplier=0,
                           allow_small_or_imprecise_dtypes=True).then_inc(consts_made, 1)
            for hf in range(2):
                pool.wait_ge(consts_made, 7 + hf)
                nc.gpsimd.iota(lane[CAP * hf:CAP * (hf + 1), :], pattern=[[0, 1]], base=0, channel_multiplier=1,
                               allow_small_or_imprecise_dtypes=True).then_inc(consts_made, 1)
            pool.wait_ge(consts_made, 9)
            for m in range(ROWS):
                nc.gpsimd.memset(ada_row[:, m, :], 0.0).then_inc(row_stored[m], 16)
            for j, base in enumerate((0, -P)):
                nc.gpsimd.iota(junk[:, j * P:(j + 1) * P], pattern=[[1, P]], base=base, channel_multiplier=-1,
                               allow_small_or_imprecise_dtypes=True).then_inc(bias_step, 1)
            pool.wait_ge(bias_step, 2)
            tile = junk[:, 0:P]
            nc.gpsimd.affine_select(out=tile, in_=tile, compare_op=ALU.is_ge, fill=-1e34, base=0,
                                    pattern=[[-1, P]], channel_multiplier=1).then_inc(bias_step, 1)
            pool.wait_ge(bias_step, 3)
            for h in range(HEADS):
                nc.gpsimd.tensor_scalar(bias_sb[:, h, :], junk[:, 0:T], 2.0 ** (-8.0 * (h + 1) / HEADS), None,
                                        ALU.mult).then_inc(bias_step, 1)
            nc.gpsimd.iota(over_cap[:], pattern=[[CAP, OVER + 1]], base=CAP, channel_multiplier=0,
                           allow_small_or_imprecise_dtypes=True).then_inc(bias_step, 1)
            nc.gpsimd.iota(over_t[:], pattern=[[1, OVER + 1]], base=0, channel_multiplier=0,
                           allow_small_or_imprecise_dtypes=True).then_inc(bias_step, 1)
            pool.wait_ge(x1_piece, 4 * NB)
            nc.gpsimd.iota(iota_s, pattern=[[1, 512]], base=0, channel_multiplier=0,
                           allow_small_or_imprecise_dtypes=True).then_inc(iota_ready, 1)
            pool.wait_ge(sq_done, NB + 4 * NB)
            nc.gpsimd.memset(xgT[:, :, 2 * T:SLOTS], 0.0).then_inc(iota_ready, 1)

        @block.tensor
        def _(pe):
            mm = nc.tensor.matmul

            def turn_group(g):
                bank = turn_ps[g % 4]
                for j in range(4):
                    last = nc.tensor.transpose(bank[:, j * P:(j + 1) * P], xn_k[:, j % 2, 2 * g + j // 2, :],
                                               ident[:])
                last.then_inc(turned, 1)

            def ada(n, turns, par, copied):
                await_chunk(pe, n, turns)
                wait(pe, ada_copied, copied)
                w = slot_cols(n)
                for k in range(K16):
                    g = 32 * (k % 4)
                    last = mm(ada_ps[par][g:g + 32, 0:CW], c_pad[:, k, :], w[:, k, :],
                              start=k < 4, stop=k >= K16 - 4)
                last.then_inc(chunk_used, 1)

            def products(x, plan):
                for qr in range(4):
                    pe.wait_ge(w_lo_ready, x + (qr + 1))
                    for j, ((out_, stationary, moving), start, stop) in enumerate(plan(qr)):
                        last = mm(out_, stationary, moving, start=start, stop=stop)
                        if qr == 3 and j == 0:
                            last.then_inc(chunk_used, 1)
                    last.then_inc(split_used, 1)

            W, H = (w_hi, w_lo), (h_hi, h_lo)
            PARTS = ((0, 0), (0, 1), (1, 0))

            def proj_T(x, pair):
                def plan(qr):
                    for h in range(2):
                        for k in range(4):
                            for pw, ph in PARTS:
                                col = k * CW + h * P
                                yield ((pair[h][:, 0:T], W[pw][:, qr % 2, col:col + P],
                                        H[ph][:, 4 * qr + k, :]),
                                       (qr, k, pw, ph) == (0, 0, 0, 0), (qr, k, pw) == (3, 3, 1))
                products(x, plan)

            def proj(x, pair):
                def plan(qr):
                    for b in range(NB):
                        for k in range(4):
                            for pw, ph in PARTS:
                                yield ((pair[b][:, 0:CW], H[ph][:, 4 * qr + k, b * P:(b + 1) * P],
                                        W[pw][:, qr % 2, k * CW:(k + 1) * CW]),
                                       (qr, k, pw, ph) == (0, 0, 0, 0), (qr, k, pw) == (3, 3, 1))
                products(x, plan)

            def mix_out(x, hf, pair):
                mix = (mix_hi, mix_lo)

                def plan(qr):
                    for k in range(2):
                        for b in range(NB):
                            for pw, ph in PARTS:
                                yield ((pair[b][:, :], mix[ph][:, 8 * hf + 2 * qr + k, b * P:(b + 1) * P],
                                        W[pw][:, qr % 2, k * 512:(k + 1) * 512]),
                                       (hf, qr, k, pw, ph) == (0, 0, 0, 0, 0), (hf, qr, k, pw) == (1, 3, 1, 1))
                products(x, plan)

            pe.wait_ge(consts_made, 4)
            pe.wait_ge(xn_ready, 1)
            for g in range(8):
                if g >= 4:
                    pe.wait_ge(evac_dve if g % 2 == 0 else evac_act, (g - 4) // 2 + 1)
                turn_group(g)
            pe.wait_ge(c_ready, 1)
            for n in range(N_A):
                ada(n, 0, n % 2, n - 1)
            pe.wait_ge(ada_copied, N_A)
            pe.wait_ge(evac_dve, 4)
            pe.wait_ge(evac_act, 4)
            for s, rows in enumerate((buf_m, buf_r)):
                rows_k = rows[:, :].rearrange("p (q k) -> p k q", k=K16)
                for k in range(K16):
                    last = mm(sc_ps[:, s * K16 + k:s * K16 + k + 1], rows_k[:, k, :], ones[:, 0:1],
                              start=True, stop=True)
            last.then_inc(cols_made, 1)
            pe.wait_ge(h_lo_ready, 1)

            with pe.Fori(0, PAIRS) as i:
                a0 = 2 * SECT
                proj_T(i * 12, proj_ps)
                ada(B1_0 + 1, i, 0, i * 3 + a0)
                proj_T(i * 12 + 4, k_ps)
                ada(B1_0 + 3, i, 1, i * 3 + a0)
                pe.wait_ge(p0_out, i * 4 + 2)
                pe.wait_ge(p1_out, i * 2 + 2)
                for h, bank in enumerate((sc_ps, sc2_ps)):
                    mm(bank[:, 0:P], qT[:, h, 0:P], kT[:, h, 0:P], start=True, stop=True)
                    mm(bank[:, P:TRI], qT[:, h, P:T], kT[:, h, :], start=True, stop=True).then_inc(scored, 1)
                proj(i * 12 + 8, proj_ps)
                pe.wait_ge(probs_ready, i + 1)
                for h, bank in enumerate((tr_ps, sc2_ps)):
                    for j in range(3):
                        last = nc.tensor.transpose(bank[:, j * P:(j + 1) * P], pp[:, h, j * P:(j + 1) * P], ident[:])
                    last.then_inc(probs_turned, 1)
                ada(B1_0 + 5, i, 0, i * 3 + a0 + 1)
                pe.wait_ge(p0_out, i * 4 + 4)
                for h, bank in enumerate((pv_ps, tr_ps)):
                    pe.wait_ge((pT0_ready, pT1_ready)[h], i + 1)
                    v = vv[:, :, h * DH:(h + 1) * DH]
                    mm(bank[:, 0:P], v[:, 0, :], ppT[:, h, 0:P], start=True, stop=True)
                    mm(bank[:, P:T], v[:, 0, :], ppT[:, h, P:T], start=True, stop=False)
                    mm(bank[:, P:T], v[:, 1, :], ppT[:, h, T:TRI], start=False, stop=True).then_inc(pv_done, 1)
                pe.wait_ge(mix_dve, i + 1)
                pe.wait_ge(mix_act, i + 1)

            with pe.Fori(0, RHEADS // 2) as i:
                for r in range(2):
                    n, t3, head = B2_0 + 9 * r, i * 3, i * 2 + r
                    a0 = 2 * SECT + 3 * PAIRS + 5 * r
                    w0 = W_B2 + 16 * r
                    proj_T(i * 32 + w0, proj_ps)
                    ada(n + 1, t3, 0, i * 10 + a0)
                    proj_T(i * 32 + (w0 + 4), k_ps)
                    ada(n + 3, t3, 1, i * 10 + a0)
                    pe.wait_ge(p0_out, head * 4 + (4 * PAIRS + 2))
                    pe.wait_ge(p1_out, head * 4 + (2 * PAIRS + 2))
                    for j in range(2):
                        mm(sc_ps[:, 0:T], kT[:, j, 0:P], qT[:, j, :], start=j == 0, stop=j == 1)
                    for j in range(2):
                        last = mm(sc_ps[:, T:TRI], kT[:, j, P:T], qT[:, j, P:T], start=j == 0, stop=j == 1)
                    last.then_inc(scored, 1)
                    proj(i * 32 + (w0 + 8), proj_ps)
                    ada(n + 5, t3, 0, i * 10 + (a0 + 1))
                    pe.wait_ge(decayed, head + 1)
                    pe.wait_ge(p0_out, head * 4 + (4 * PAIRS + 4))
                    mm(pv_ps[:, 0:T], scoreT[:, 0:P], vv[:, 0, :], start=True, stop=True)
                    mm(pv_ps[:, T:512], scoreT[:, P:T], vv[:, 0, :], start=True, stop=False)
                    mm(pv_ps[:, T:512], scoreT[:, T:TRI], vv[:, 1, :], start=False, stop=True).then_inc(ret_pv, 1)
                    proj(i * 32 + (w0 + 12), proj_ps)
                    ada(n + 7, t3, 1, i * 10 + (a0 + 2))
                    ada(n + 8, t3, 0, i * 10 + (a0 + 3))
                    pe.wait_ge(ret_y, head + 1)
                    for j in range(4):
                        last = nc.tensor.transpose(tr_ps[:, j * P:(j + 1) * P], yy[:, j % 2, (j // 2) * P:(j // 2 + 1) * P],
                                                   ident[:])
                    last.then_inc(ret_turned, 1)

            pe.wait_ge(mix_lo_ready, 1)
            for cc in range(4):
                wait(pe, x1_piece, NB * (cc - 1))
                for hf in range(2):
                    if (cc, hf) == (0, 1):
                        pe.wait_ge(mix_lo_ready, 2)
                    mix_out(W_C + 8 * cc + 4 * hf, hf, out_ps[cc % 2])
                if cc == 0:
                    pe.wait_ge(ada_copied, 6 * SECT)
                    pe.wait_ge(ret_mix, RHEADS)
                    pe.wait_ge(gate_rows, 32)
                    for q in range(4):
                        mm(turn_ps[q][:, :], ones[0:5, :], buf_r[0:5, q * 512:(q + 1) * 512],
                           start=True, stop=True).then_inc(gm_ps, 1)

            pe.wait_ge(xn_ready, 2)
            pe.wait_ge(gm_ready, 4)
            for g in range(8):
                wait(pe, evac_dve if g % 2 == 0 else evac_act, 4 + (g - 4) // 2 + 1 if g >= 4 else 0)
                turn_group(g)
            pe.wait_ge(gatef_rows, 32)
            for q in range(2):
                for half in range(2):
                    last = mm(ada_ps[q][CAP * half:CAP * (half + 1), :], ones[0:5, 0:CAP],
                              buf_r[0:5, half * 1024 + q * 512:half * 1024 + (q + 1) * 512], start=True, stop=True)
                last.then_inc(gf_ps, 1)
            pe.wait_ge(evac_dve, 8)
            pe.wait_ge(evac_act, 8)
            pe.wait_ge(late_in, LATE * 16)
            for b in range(NB):
                for k in range(K16):
                    last = mm(proj_ps[0][:, b * 36:(b + 1) * 36], xn2T[:, k, b * P:(b + 1) * P], w_route[:, k, :],
                              start=k == 0, stop=k == K16 - 1)
            last.then_inc(logits_ps, 1)
            pe.wait_ge(picks, 1)
            pe.wait_ge(gf_ready, 2)
            cps = proj_ps[1]
            mm(cps[:, 0:E], ones[:], both[:, 0, :], start=True, stop=False)
            mm(cps[:, 0:E], ones[:], both[:, 1, :], start=False, stop=True)
            mm(cps[:, E:2 * E], before[:], both[:, 0, :], start=True, stop=True)
            mm(cps[:, 2 * E:3 * E], ones[:], both[:, 0, :], start=True, stop=False)
            mm(cps[:, 2 * E:3 * E], before[:], both[:, 1, :], start=False, stop=True)
            mm(ada_ps[0][0:E, 0:1], both[:, 0, :], ones[:, 0:1], start=True, stop=False)
            mm(ada_ps[0][0:E, 0:1], both[:, 1, :], ones[:, 0:1], start=False, stop=True).then_inc(counts_ps, 1)
            pe.wait_ge(counts_sb, 1)
            mm(ada_ps[1][:, 0:E], cnt_rep[:, 0, :], before[0:E, 0:E], start=True, stop=True)
            mm(ada_ps[1][:, E:2 * E], cnt_rep[:, 1, :], before[0:E, 0:E], start=True, stop=True).then_inc(starts_ps, 1)
            pe.wait_ge(onehot_ready, 1)
            for k in range(K16):
                if k >= 4:
                    wait(pe, evac_dve if k % 2 == 0 else evac_act, 8 + (k - 4) // 2 + 1)
                for b in range(NB):
                    last = mm(turn_ps[k % 4][:, :], xn_k[:, b, k, :], onehot[:, b, :], start=b == 0, stop=b == 1)
                last.then_inc(gathered, 1)
            pe.wait_ge(diag_ready, 1)
            for b in range(NB):
                last = mm(proj_ps[b][:, :], ones[:], diag[:, b], start=True, stop=True)
            last.then_inc(keys_ps, 1)

            def hidden(n):
                pe.wait_ge(xe_ready, n + 1)
                for hf in range(2):
                    for m in range(2):
                        await_chunk(pe, D_0 + 2 * hf + m, n)
                    w = [slot_512(D_0 + 2 * hf + m) for m in range(2)]
                    for k in range(8):
                        for m in range(2):
                            last = mm(h_ps[CAP * m:CAP * (m + 1), :], xe[:, 8 * hf + k, :], w[m][:, k, :],
                                      start=hf == 0 and k == 0, stop=hf == 1 and k == 7)
                            if k == 7:
                                last.then_inc(chunk_used, 1)

            def turn_hidden(n):
                pe.wait_ge(g_ready, n + 1)
                g_k = gg[0:CAP, :].rearrange("p (q k) -> p k q", k=K4)
                for k in range(K4):
                    last = mm(gt_ps[:, k * CAP:(k + 1) * CAP], g_k[:, k, :], ident[0:CAP, 0:CAP],
                              start=True, stop=True)
                last.then_inc(gT_ps, 1)

            def outputs(n, yg_free):
                pe.wait_ge(gT_ready, n + 1)
                wait(pe, yg_ready, yg_free)
                for hf in range(2):
                    await_chunk(pe, D_0 + 4 + hf, n)
                    w = slot_w2(D_0 + 4 + hf)
                    for k in range(2):
                        for q in range(2):
                            for half in range(2):
                                col = half * 1024 + q * 512
                                last = mm(y_ps[q][CAP * half:CAP * (half + 1), :], ggT[:, 2 * hf + k, :],
                                          w[:, k, col:col + 512], start=hf == 0 and k == 0, stop=hf == 1 and k == 1)
                    last.then_inc(chunk_used, 1)

            def add_up(n):
                pe.wait_ge(comb_ready, n + 1)
                for j in range(4):
                    b, q = j // 2, j % 2
                    if j >= 2:
                        pe.wait_ge(added, n * 4 + (j - 1))
                    for half in range(2):
                        rows = slice(CAP * half, CAP * (half + 1))
                        last = mm(add_ps[2 * (j % 2) + half][:, :], comb[rows, b * P:(b + 1) * P],
                                  yg[rows, q * 512:(q + 1) * 512], start=True, stop=True)
                    last.then_inc(add_done, 1)

            pe.wait_ge(keys_ready, 1)
            pe.wait_ge(evac_dve, 16)
            pe.wait_ge(evac_act, 16)
            def item(n):
                hidden(n)
                add_up(n - 1)
                turn_hidden(n)
                outputs(n, n)

            hidden(0)
            turn_hidden(0)
            outputs(0, 0)
            with pe.Fori(1, E - 1) as n:
                item(n)
            pe.wait_ge(tables_ready, 1)
            items = pe.value_load(n_over[0:1, 0:1], min_val=0, max_val=OVER)
            with pe.Fori(0, OVER) as t:
                with pe.If(t < items):
                    item(t + (E - 1))
                pe.end_ifs()
            item(items + (E - 1))
            add_up(items + (E - 1))

        @block.scalar
        def _(act):
            act.wait_ge(small_in, 16)
            act.wait_ge(consts_made, 1)
            nc.scalar.activation(c_pad[:, :, 0], c_col[:], ACT.Silu).then_inc(c_ready, 1)
            act.wait_ge(x_in, 16)
            for b in range(NB):
                nc.scalar.activation(xn[:, b, :], x_a[:, b, :], ACT.Square,
                                     accum_out=sumsq[:, b, 0:1]).then_inc(sq_done, 1)
            act.wait_ge(ms_done, 1)
            nc.scalar.activation(rt[:], ms[:], ACT.Sqrt).then_inc(rt_done, 1)
            for g in range(1, 8, 2):
                act.wait_ge(turned, g + 1)
                nc.scalar.copy(xnT[:, 2 * g:2 * g + 2, :].rearrange("p k t -> p (k t)"),
                               turn_ps[g % 4][:, :]).then_inc(evac_act, 1)
            for n in range(N_A):
                act.wait_ge(chunk_used, n + 1)
                rows = buf_m if n < SECT else buf_r
                nc.scalar.copy(rows[:, (n % SECT) * CW:(n % SECT + 1) * CW],
                               ada_ps[n % 2][:, 0:CW]).then_inc(ada_copied, 1)
            act.wait_ge(col_ready, 1)
            for k in range(1, K16, 2):
                last = nc.scalar.activation(xnT[:, k, :], xnT[:, k, :], ACT.Identity, bias=shift[:, k:k + 1],
                                            scale=scale[:, k:k + 1])
            last.then_inc(mod_act, 1)

            def split_hi(n, turns, qr, x):
                if qr == 0:
                    await_chunk(act, n, turns)
                wait(act, split_used, x + (qr - 1))
                nc.scalar.copy(w_hi[:, qr % 2, :], quarter(n, qr)).then_inc(w_hi_ready, 1)

            act.wait_ge(xn_ready, 1)
            for k, mod in ((1, mod_act), (0, mod_dve)):
                act.wait_ge(mod, 1)
                nc.scalar.copy(h_hi[:, k:K16:2, :], xnT[:, k:K16:2, :]).then_inc(h_hi_ready, 1)
            for qr in range(2):
                split_hi(B1_0, 0, qr, 0)

            def ada_row_out(used, m, par, stored_before, copied, a):
                act.wait_ge(chunk_used, used)
                act.wait_ge(row_stored[m], stored_before)
                nc.scalar.copy(ada_row[:, m, :], ada_ps[par][:, 0:CW]).then_inc(ada_copied, 1)
                act.wait_ge(ada_copied, copied)
                act.dma_start(rows_dram[:, bass.ds(a * CW, CW)], ada_row[0:P:32, m, :]).then_inc(row_stored[m], 16)

            def attention_rows(i, m, par):
                ada_row_out(i * 6 + (B1_0 + 2 * m + 2), m, par, i * 16 + 16, i * 3 + (2 * SECT + m + 1),
                            i * 3 + (2 * SECT + m))

            with act.Fori(0, PAIRS) as i:
                def hi(m, qr):
                    split_hi(B1_0 + 2 * m, i, qr, i * 12 + 4 * m)

                hi(0, 2), hi(0, 3), hi(1, 0), hi(1, 1)
                attention_rows(i, 0, 0)
                hi(1, 2), hi(1, 3), hi(2, 0)
                act.wait_ge(split_used, i * 12 + 8)
                for j in range(2):
                    nc.scalar.copy(kT[:, j, :], k_ps[j][:, 0:T]).then_inc(p1_out, 1)
                hi(2, 1)
                attention_rows(i, 1, 1)
                hi(2, 2)
                act.wait_ge(max_ready, i + 1)
                for h in range(2):
                    for b, (lo, hi_) in enumerate(((0, P), (P, TRI))):
                        nc.scalar.activation(pp[:, h, lo:hi_], pp[:, h, lo:hi_], ACT.Exp, bias=smax[:, b, h:h + 1],
                                             accum_out=ssum[:, b, h:h + 1]).then_inc(exp_done, 1)
                hi(2, 3)
                hi(3, 0)
                hi(3, 1)
                act.wait_ge(probs_turned, i * 2 + 2)
                nc.scalar.copy(ppT[:, 1, :], sc2_ps[:, 0:TRI]).then_inc(pT1_ready, 1)
                attention_rows(i, 2, 0)
                act.wait_ge(pv_done, i * 2 + 2)
                nc.scalar.copy(mixT[:, bass.ds(i * 2 + 1, 1), :], tr_ps[:, 0:T].rearrange("p (o t) -> p o t", o=1)
                               ).then_inc(mix_act, 1)

            def mix_split_hi(half):
                nc.scalar.copy(mix_hi[:, 8 * half:8 * half + 8, :], mixT[:, 8 * half:8 * half + 8, :]
                               ).then_inc(mix_hi_ready, 1)

            act.wait_ge(mix_dve, PAIRS)
            act.wait_ge(mix_act, PAIRS)
            mix_split_hi(0)

            def retention_rows(i, r, m, par):
                a = 2 * SECT + 3 * PAIRS + 5 * r + m
                before_ = 1 + r + (PAIRS if m < 3 else 0)
                ada_row_out(i * 18 + (B2_0 + 9 * r + (2 * m + 2 if m < 4 else 9)), m, par, i * 32 + 16 * before_,
                            i * 10 + (a + 1), i * 10 + a)

            with act.Fori(0, RHEADS // 2) as i:
                for r in range(2):
                    head = i * 2 + r

                    def hi(m, qr):
                        n = B2_0 + 9 * r + (2 * m if m < 4 else 9)
                        split_hi(n, i * 3, qr, i * 32 + (W_B2 + 16 * r + 4 * m))

                    hi(0, 2), hi(0, 3), hi(1, 0), hi(1, 1)
                    retention_rows(i, r, 0, 0)
                    hi(1, 2), hi(1, 3), hi(2, 0)
                    act.wait_ge(split_used, i * 32 + (W_B2 + 16 * r + 8))
                    for j in range(2):
                        nc.scalar.copy(kT[:, j, :], k_ps[j][:, 0:T]).then_inc(p1_out, 1)
                    hi(2, 1)
                    retention_rows(i, r, 1, 1)
                    hi(2, 2), hi(2, 3), hi(3, 0), hi(3, 1)
                    retention_rows(i, r, 2, 0)
                    act.wait_ge(ret_pv, head + 1)
                    for b in range(NB):
                        nc.scalar.activation(junk[:, b * DR:(b + 1) * DR], pv_ps[:, b * DR:(b + 1) * DR], ACT.Square,
                                             accum_out=sumsq[:, b, 0:1]).then_inc(ret_sq, 1)
                    hi(3, 2)
                    act.wait_ge(ret_ms, head + 1)
                    nc.scalar.activation(rt[:], ms[:], ACT.Sqrt).then_inc(ret_rt, 1)
                    hi(3, 3), hi(4, 0)
                    act.wait_ge(split_used, i * 32 + (W_B2 + 16 * r + 16))
                    for j in range(2):
                        nc.scalar.activation(sg[:, j, :], proj_ps[j][:, 0:CW], ACT.Silu).then_inc(p1_out, 1)
                    hi(4, 1)
                    retention_rows(i, r, 3, 1)
                    retention_rows(i, r, 4, 0)

            act.wait_ge(ret_mix, RHEADS)
            mix_split_hi(1)

            def w_out_hi(u):
                for qr in range(2, 6):
                    if u + qr // 4 < N_C:
                        split_hi(C_0 + u + qr // 4, 0, qr % 4, W_C + 4 * (u + qr // 4))

            w_out_hi(0)
            for m in range(ROWS):
                act.wait_ge(row_stored[m], 16 * (1 + RHEADS + (PAIRS if m < 3 else 0)))
            act.dma_start(buf_r[0:4, :], rows_dram[:, 2 * D:3 * D]).then_inc(gate_rows, 16)
            act.dma_start(buf_r[4:5, :], b_ada[:, 2 * D:3 * D]).then_inc(gate_rows, 16)
            for s in range(2):
                act.dma_start(mod_raw[:, :, s, :], rows_dram[:, (3 + s) * D:(4 + s) * D].rearrange(
                    "r (p k) -> p r k", k=K16)).then_inc(mod2_in, 16)
            w_out_hi(1)
            for q in range(4):
                act.wait_ge(gm_ps, q + 1)
                nc.scalar.copy(buf_m[:, q * 512:(q + 1) * 512], turn_ps[q][:, :]).then_inc(gm_ready, 1)
            act.dma_start(buf_r[0:4, :], rows_dram[:, 5 * D:6 * D]).then_inc(gatef_rows, 16)
            act.dma_start(buf_r[4:5, :], b_ada[:, 5 * D:6 * D]).then_inc(gatef_rows, 16)
            for cc in range(4):
                if cc < 3:
                    w_out_hi(2 * cc + 2)
                for b in range(NB):
                    act.wait_ge(x1_piece, NB * cc + b + 1)
                    act.wait_ge(sq_done, NB + NB * cc + b)
                    nc.scalar.activation(junk, xs[:, b, cc * 512:(cc + 1) * 512], ACT.Square,
                                         accum_out=sumsq[:, b, cc:cc + 1]).then_inc(sq_done, 1)
                if cc < 3:
                    w_out_hi(2 * cc + 3)
            act.wait_ge(ms_done, 2)
            nc.scalar.activation(rt[:], ms[:], ACT.Sqrt).then_inc(rt_done, 1)
            act.wait_ge(col_ready, 2)
            for g in range(1, 8, 2):
                act.wait_ge(turned, 8 + g + 1)
                for j in range(2):
                    k = 2 * g + j
                    last = nc.scalar.activation(xn2T[:, k, :], turn_ps[g % 4][:, j * T:(j + 1) * T], ACT.Identity,
                                                bias=shift[:, k:k + 1], scale=scale[:, k:k + 1])
                last.then_inc(evac_act, 1)
            for q in range(2):
                act.wait_ge(gf_ps, q + 1)
                nc.scalar.copy(gate_f[:, q * 512:(q + 1) * 512], ada_ps[q][:, :]).then_inc(gf_ready, 1)
            for j in range(2):
                act.wait_ge(route_exp_in, j + 1)
                nc.scalar.activation(exp_out[j], exp_in[j], ACT.Exp).then_inc(route_exp, 1)
            act.wait_ge(iota_ready, 2)
            for k in range(1, K16, 2):
                act.wait_ge(gathered, k + 1)
                nc.scalar.activation(xgT[:, k, 0:2 * T], turn_ps[k % 4][:, :], ACT.Identity, bias=shift[:, k:k + 1],
                                     scale=scale[:, k:k + 1]).then_inc(evac_act, 1)
            act.wait_ge(keys_ps, 1)
            act.dma_start(buf_r[:], norm_final_w.partition_broadcast(P)).then_inc(final_w_in, 16)

            def expert_act(n):
                act.wait_ge(chunk_used, n * 6 + (D_0 + 4))
                nc.scalar.activation(sil[0:CAP, :], h_ps[0:CAP, :], ACT.Silu).then_inc(sil_ready, 1)
                act.wait_ge(gT_ps, n + 1)
                nc.scalar.copy(ggT.rearrange("p k s -> p (k s)"), gt_ps[:, 0:K4 * CAP]).then_inc(gT_ready, 1)

            with act.Fori(0, E - 1) as n:
                expert_act(n)
            act.wait_ge(tables_ready, 1)
            items = act.value_load(n_over[0:1, 0:1], min_val=0, max_val=OVER)
            with act.Fori(0, OVER) as t:
                with act.If(t < items):
                    expert_act(t + (E - 1))
                act.end_ifs()
            expert_act(items + (E - 1))
            for j in range(4):
                act.wait_ge(added, items * 4 + (4 * (E - 1) + j + 1))
                b, q = j // 2, j % 2
                for half in range(2):
                    col = half * 1024 + q * 512
                    nc.scalar.activation(square[:, 2 * j + half, :], xs[:, b, col:col + 512], ACT.Square,
                                         accum_out=sumsq[:, b, 2 * q + half:2 * q + half + 1]).then_inc(sq_done, 1)
            act.wait_ge(ms_done, 3)
            nc.scalar.activation(rt[:], ms[:], ACT.Sqrt).then_inc(rt_done, 1)
            act.wait_ge(inverse_ready, 1)
            for b in range(NB):
                piece = answer[:, b, 1024:2048]
                nc.scalar.activation(piece, piece, ACT.Copy, scale=rinv[:, b:b + 1]).then_inc(out_act, 1)

        @block.vector
        def _(dve):
            v = nc.vector
            steps = [0]

            def step(ins):
                steps[0] += 1
                ins.then_inc(dve_step, 1)
                dve.wait_ge(dve_step, steps[0])

            def inverse_rms(nth, parts, ready=None):
                if parts > 1:
                    step(v.tensor_reduce(ms[:], sumsq[:, :, 0:parts], AX, ALU.add))
                    src = ms[:]
                else:
                    src = sumsq[:, :, 0]
                v.tensor_scalar(ms[:], src, 1.0 / D, EPS, ALU.mult, ALU.add).then_inc(ms_done, 1)
                dve.wait_ge(rt_done, nth)
                last = v.reciprocal(rinv[:], rt[:])
                if ready is None:
                    step(last)
                else:
                    last.then_inc(ready, 1)
                    dve.wait_ge(ready, 1)

            dve.wait_ge(sq_done, NB)
            inverse_rms(1, 1)
            for b in range(NB):
                last = v.tensor_scalar(xn[:, b, :], x_a[:, b, :], rinv[:, b:b + 1], None, ALU.mult)
            last.then_inc(xn_ready, 1)
            for g in range(0, 8, 2):
                dve.wait_ge(turned, g + 1)
                v.tensor_copy(xnT[:, 2 * g:2 * g + 2, :].rearrange("p k t -> p (k t)"),
                              turn_ps[g % 4][:, :]).then_inc(evac_dve, 1)
            dve.wait_ge(const_in, 2 * 16)
            dve.wait_ge(cols_made, 1)
            v.tensor_tensor(shift[:], sc_ps[:, 0:K16], b_col[:, 0, :], ALU.add)
            step(v.tensor_tensor(scale[:], sc_ps[:, K16:2 * K16], b_col[:, 1, :], ALU.add))
            v.scalar_tensor_tensor(out=scale[:], in0=scale[:], scalar=1.0, in1=mix_w[:], op0=ALU.add,
                                   op1=ALU.mult).then_inc(col_ready, 1)
            dve.wait_ge(col_ready, 1)
            dve.wait_ge(evac_dve, 4)
            for k in range(0, K16, 2):
                last = v.tensor_scalar(xnT[:, k, :], xnT[:, k, :], scale[:, k:k + 1], shift[:, k:k + 1],
                                       ALU.mult, ALU.add)
            last.then_inc(mod_dve, 1)

            def split_lo(n, qr, x):
                dve.wait_ge(w_hi_ready, x + (qr + 1))
                v.tensor_tensor(w_lo[:, qr % 2, :], quarter(n, qr), w_hi[:, qr % 2, :],
                                ALU.subtract).then_inc(w_lo_ready, 1)

            for j, k in enumerate((1, 0)):
                dve.wait_ge(h_hi_ready, j + 1)
                if k == 0:
                    dve.wait_ge(mod_dve, 1)
                last = v.tensor_tensor(h_lo[:, k:K16:2, :], xnT[:, k:K16:2, :], h_hi[:, k:K16:2, :], ALU.subtract)
            last.then_inc(h_lo_ready, 1)
            for qr in range(2):
                split_lo(B1_0, qr, 0)

            dve.wait_ge(bias_step, 3 + HEADS + 2)
            with dve.Fori(0, PAIRS) as i:
                def lo(m, qr):
                    split_lo(B1_0 + 2 * m, qr, i * 12 + 4 * m)

                lo(0, 2), lo(0, 3), lo(1, 0)
                dve.wait_ge(split_used, i * 12 + 4)
                for j in range(2):
                    v.tensor_copy(qT[:, j, :], proj_ps[j][:, 0:T]).then_inc(p0_out, 1)
                lo(1, 1), lo(1, 2), lo(1, 3), lo(2, 0), lo(2, 1)
                for h, bank in enumerate((sc_ps, sc2_ps)):
                    dve.wait_ge(scored, i * 2 + (h + 1))
                    bias = bias_sb[:, bass.ds(i * 2 + h, 1), :].rearrange("p o n -> p (o n)")
                    for at_, n in ((0, T), (T, P)):
                        v.scalar_tensor_tensor(out=pp[:, h, at_:at_ + n], in0=bank[:, at_:at_ + n], scalar=DH ** -0.5,
                                               in1=bias[:, 0:n], op0=ALU.mult, op1=ALU.add).then_inc(logits, 1)
                dve.wait_ge(logits, i * 6 + 4)
                v.tensor_reduce(smax[:, 0, :], pp[:, :, 0:P], AX, ALU.max).then_inc(logits, 1)
                v.tensor_reduce(smax[:, 1, :], pp[:, :, P:TRI], AX, ALU.max).then_inc(logits, 1)
                dve.wait_ge(logits, i * 6 + 6)
                v.tensor_scalar(smax[:], smax[:], -1.0, None, ALU.mult).then_inc(max_ready, 1)
                lo(2, 2)
                dve.wait_ge(exp_done, i * 4 + 4)
                v.reciprocal(sinv[:], ssum[:]).then_inc(ret_step, 1)
                dve.wait_ge(ret_step, i + 1)
                for h in range(2):
                    for b, (lo_, hi_) in enumerate(((0, P), (P, TRI))):
                        last = v.tensor_scalar(pp[:, h, lo_:hi_], pp[:, h, lo_:hi_], sinv[:, b, h:h + 1], None, ALU.mult)
                last.then_inc(probs_ready, 1)
                lo(2, 3), lo(3, 0)
                dve.wait_ge(split_used, i * 12 + 12)
                for j in range(2):
                    v.tensor_copy(vv[:, j, :], proj_ps[j][:, 0:CW]).then_inc(p0_out, 1)
                lo(3, 1)
                dve.wait_ge(probs_turned, i * 2 + 1)
                v.tensor_copy(ppT[:, 0, :], tr_ps[:, 0:TRI]).then_inc(pT0_ready, 1)
                dve.wait_ge(pv_done, i * 2 + 1)
                v.tensor_copy(mixT[:, bass.ds(i * 2, 1), :], pv_ps[:, 0:T].rearrange("p (o t) -> p o t", o=1)
                              ).then_inc(mix_dve, 1)

            def mix_split_lo(half):
                rows = slice(8 * half, 8 * half + 8)
                dve.wait_ge(mix_hi_ready, half + 1)
                v.tensor_tensor(mix_lo[:, rows, :], mixT[:, rows, :], mix_hi[:, rows, :],
                                ALU.subtract).then_inc(mix_lo_ready, 1)

            mix_split_lo(0)

            dve.wait_ge(late_in, LATE * 16)
            with dve.Fori(0, RHEADS // 2) as i:
                for r in range(2):
                    head = i * 2 + r

                    def lo(m, qr):
                        n = B2_0 + 9 * r + (2 * m if m < 4 else 9)
                        split_lo(n, qr, i * 32 + (W_B2 + 16 * r + 4 * m))

                    lo(0, 2), lo(0, 3), lo(1, 0)
                    dve.wait_ge(split_used, i * 32 + (W_B2 + 16 * r + 4))
                    for j in range(2):
                        v.tensor_copy(qT[:, j, :], proj_ps[j][:, 0:T]).then_inc(p0_out, 1)
                    lo(1, 1), lo(1, 2), lo(1, 3), lo(2, 0), lo(2, 1)
                    dve.wait_ge(scored, head + (2 * PAIRS + 1))
                    for at_, n in ((0, T), (T, P)):
                        last = v.tensor_tensor(scoreT[:, at_:at_ + n], sc_ps[:, at_:at_ + n],
                                               decay_sb[:, bass.ds(head * T, n)], ALU.mult)
                    last.then_inc(decayed, 1)
                    lo(2, 2), lo(2, 3), lo(3, 0)
                    dve.wait_ge(split_used, i * 32 + (W_B2 + 16 * r + 12))
                    for j in range(2):
                        v.tensor_copy(vv[:, j, :], proj_ps[j][:, 0:CW]).then_inc(p0_out, 1)
                    lo(3, 1)
                    dve.wait_ge(ret_sq, head * 2 + 2)
                    v.tensor_scalar(ms[:], sumsq[:, :, 0], 1.0 / DR, EPS, ALU.mult, ALU.add).then_inc(ret_ms, 1)
                    lo(3, 2)
                    dve.wait_ge(ret_rt, head + 1)
                    v.reciprocal(rinv[:], rt[:]).then_inc(ret_step, 1)
                    dve.wait_ge(ret_step, head * 3 + (PAIRS + 1))
                    for b in range(NB):
                        v.tensor_scalar(yy[:, b, :], pv_ps[:, b * DR:(b + 1) * DR], rinv[:, b:b + 1], None,
                                        ALU.mult).then_inc(ret_step, 1)
                    lo(3, 3), lo(4, 0)
                    dve.wait_ge(ret_step, head * 3 + (PAIRS + 3))
                    dve.wait_ge(p1_out, head * 4 + (2 * PAIRS + 4))
                    v.tensor_tensor(yy, yy, sg, ALU.mult).then_inc(ret_y, 1)
                    lo(4, 1)
                    dve.wait_ge(ret_turned, head + 1)
                    for j in range(2):
                        last = v.tensor_scalar(mixT[:, bass.ds(head * 2 + (HEADS + j), 1), :],
                                               tr_ps[:, j * T:(j + 1) * T].rearrange("p (o t) -> p o t", o=1),
                                               ret_w[:, bass.ds(head * 2 + j, 1)], None, ALU.mult)
                    last.then_inc(ret_mix, 1)

            mix_split_lo(1)

            tmp = yy.rearrange("p b n -> p (b n)")
            tmps = [tmp, sg.rearrange("p b n -> p (b n)")]

            def w_out_lo(u):
                for qr in range(2, 6):
                    if u + qr // 4 < N_C:
                        split_lo(C_0 + u + qr // 4, qr % 4, W_C + 4 * (u + qr // 4))

            w_out_lo(0)
            w_out_lo(1)
            dve.wait_ge(x_in, 32)
            for cc in range(4):
                dve.wait_ge(split_used, W_C + 8 * (cc + 1))
                dve.wait_ge(gm_ready, cc + 1)
                for b in range(NB):
                    step(v.tensor_tensor(tmps[b], out_ps[cc % 2][b][:, :], buf_m[:, cc * 512:(cc + 1) * 512], ALU.mult))
                    piece = xs[:, b, cc * 512:(cc + 1) * 512]
                    v.tensor_tensor(piece, piece, tmps[b], ALU.add).then_inc(x1_piece, 1)
                if cc < 3:
                    w_out_lo(2 * cc + 2)
                    w_out_lo(2 * cc + 3)
            dve.wait_ge(mod2_in, 32)
            step(v.tensor_reduce(sums2[:], mod_raw[:].rearrange("p r s k -> p (s k) r"), AX, ALU.add))
            v.tensor_tensor(shift[:], sums2[:, 0:K16], b_col[:, 3, :], ALU.add)
            step(v.tensor_tensor(scale[:], sums2[:, K16:2 * K16], b_col[:, 4, :], ALU.add))
            v.scalar_tensor_tensor(out=scale[:], in0=scale[:], scalar=1.0, in1=ffn_w[:], op0=ALU.add,
                                   op1=ALU.mult).then_inc(col_ready, 1)
            dve.wait_ge(col_ready, 2)
            dve.wait_ge(sq_done, NB + 4 * NB)
            inverse_rms(2, 4)
            for b in range(NB):
                last = v.tensor_scalar(xn[:, b, :], xs[:, b, :], rinv[:, b:b + 1], None, ALU.mult)
            last.then_inc(xn_ready, 1)
            for g in range(0, 8, 2):
                dve.wait_ge(turned, 8 + g + 1)
                for j in range(2):
                    k = 2 * g + j
                    last = v.tensor_scalar(xn2T[:, k, :], turn_ps[g % 4][:, j * T:(j + 1) * T], scale[:, k:k + 1],
                                           shift[:, k:k + 1], ALU.mult, ALU.add)
                last.then_inc(evac_dve, 1)

            def wide(a, n):
                return a.rearrange("p (b o) -> p b o", o=1).to_broadcast([P, NB, n])

            def const(a, n):
                return a.rearrange("p (o n) -> p o n", o=1).to_broadcast([P, NB, n])

            def pick(values, rev, best, eq, top, onehot_):
                n = values.shape[2]
                step(v.tensor_reduce(best, values, AX, ALU.max))
                step(v.tensor_tensor(eq, values, wide(best, n), ALU.is_equal))
                step(v.tensor_tensor(eq, eq, const(rev, n), ALU.mult))
                step(v.tensor_reduce(top, eq, AX, ALU.max))
                step(v.tensor_tensor(onehot_, const(rev, n), wide(top, n), ALU.is_equal))

            dve.wait_ge(logits_ps, 1)
            dve.wait_ge(consts_made, 9)
            step(v.tensor_tensor(lg, proj_ps[0][:, 0:72].rearrange("p (b n) -> p b n", b=NB),
                                 const(b_route[:], 36), ALU.add))
            pick(lg[:, :, 0:4], rev8[:, 4:8], gmax, eq4, top1, og)
            v.tensor_tensor(exp_in[0].rearrange("p (b n) -> p b n", b=NB), lg[:, :, 0:4], wide(gmax, 4),
                            ALU.subtract).then_inc(route_exp_in, 1)
            lgr = lg[:, :, 4:36].rearrange("p b (g e) -> p b g e", g=GROUPS)
            for b in range(NB):
                last = v.tensor_tensor(lsel[:, b], lgr[:, b], og[:, b].rearrange("p (g o) -> p g o", o=1).to_broadcast(
                    [P, GROUPS, EPG]), ALU.mult)
            step(last)
            step(v.tensor_reduce(el, lsel.rearrange("p b g e -> p b e g"), AX, ALU.add))
            pick(el, rev8[:], m1, eq8, top1, o1)
            step(v.scalar_tensor_tensor(out=el, in0=o1, scalar=-1e30, in1=el, op0=ALU.mult, op1=ALU.add))
            pick(el, rev8[:], m2, eq8, top1, o2)
            v.tensor_tensor(exp_in[1], m2, m1, ALU.subtract).then_inc(route_exp_in, 1)
            dve.wait_ge(route_exp, 1)
            step(v.tensor_reduce(gsum, exp_out[0].rearrange("p (b n) -> p b n", b=NB), AX, ALU.add))
            for q, o in enumerate((o1, o2)):
                for b in range(NB):
                    last = v.tensor_tensor(chosen[:, q, b].rearrange("p (g e) -> p g e", g=GROUPS),
                                           og[:, b].rearrange("p (g o) -> p g o", o=1).to_broadcast([P, GROUPS, EPG]),
                                           o[:, b].rearrange("p (o e) -> p o e", o=1).to_broadcast([P, GROUPS, EPG]),
                                           ALU.mult)
            step(last)
            v.tensor_tensor(both, chosen[:, 0], chosen[:, 1], ALU.add).then_inc(picks, 1)
            dve.wait_ge(route_exp, 2)
            step(v.tensor_scalar(w_tok[:, 1, :], exp_out[1], 1.0, None, ALU.add))
            step(v.tensor_tensor(w_tok[:, 1, :], w_tok[:, 1, :], gsum, ALU.mult))
            step(v.reciprocal(w_tok[:, 0, :], w_tok[:, 1, :]))
            step(v.tensor_tensor(w_tok[:, 1, :], w_tok[:, 0, :], exp_out[1], ALU.mult))
            dve.wait_ge(counts_ps, 1)
            v.tensor_copy(cnt, proj_ps[1][:, 0:3 * E])
            step(v.tensor_copy(cnt_col[:, 0:1], ada_ps[0][0:E, 0:1]))
            step(v.tensor_scalar(cnt_col[:, 1:2], cnt_col[:, 0:1], float(CAP), None, ALU.is_gt))
            for j in range(2, 4):
                step(v.scalar_tensor_tensor(out=cnt_col[:, 1:2], in0=cnt_col[:, 0:1], scalar=float(CAP * j),
                                            in1=cnt_col[:, 1:2], op0=ALU.is_gt, op1=ALU.add))
            v.tensor_copy(cnt_rep, cnt_col.rearrange("p (q o) -> p q o", o=1).to_broadcast([E, 2, P])).then_inc(counts_sb, 1)
            dve.wait_ge(starts_ps, 1)
            step(v.tensor_copy(first, ada_ps[1][:, 0:2 * E]))
            ranks = cnt[:, E:3 * E].rearrange("p (b e) -> p b e", b=NB)
            v.tensor_tensor(where[:, 0], ranks, const(first[:, 0:E], E), ALU.add)
            step(v.tensor_tensor(where[:, 1], ranks, e256[:].to_broadcast([P, NB, E]), ALU.add))
            for s in range(2):
                for q in range(2):
                    step(v.tensor_tensor(wtmp, chosen[:, q], where[:, s], ALU.mult))
                    step(v.tensor_reduce(slot_key[:, s, q, :], wtmp, AX, ALU.add))
            dve.wait_ge(iota_ready, 1)
            dve.wait_ge(gf_ps, 2)
            for b in range(NB):
                step(v.tensor_scalar(onehot[:, b, :], iota_s, slot_key[:, 0, 0, b:b + 1], None, ALU.is_equal))
                last = v.scalar_tensor_tensor(out=onehot[:, b, :], in0=iota_s, scalar=slot_key[:, 0, 1, b:b + 1],
                                              in1=onehot[:, b, :], op0=ALU.is_equal, op1=ALU.add)
            last.then_inc(onehot_ready, 1)
            for b in range(NB):
                for q in range(4):
                    s = slot_key[:, 1, q, b:b + 1] if q < 2 else w_tok[:, q - 2, b:b + 1]
                    last = v.tensor_scalar(diag[:, b, q, :], ident[:], s, None, ALU.mult)
            last.then_inc(diag_ready, 1)
            dve.wait_ge(iota_ready, 2)
            for k in range(0, K16, 2):
                dve.wait_ge(gathered, k + 1)
                v.tensor_scalar(xgT[:, k, 0:2 * T], turn_ps[k % 4][:, :], scale[:, k:k + 1], shift[:, k:k + 1],
                                ALU.mult, ALU.add).then_inc(evac_dve, 1)
            v.tensor_copy(start_tab[:, 0:E], first[0:1, 0:E]).then_inc(starts_ready, 1)
            dve.wait_ge(keys_ps, 1)
            for b in range(NB):
                last = v.tensor_copy(keys[:, :, b * P:(b + 1) * P],
                                     proj_ps[b][:, :].rearrange("p (q n) -> p q n", q=4))
            last.then_inc(keys_ready, 1)

            def tables():
                over, upto, less = tab[:, 0:E], tab[:, E:2 * E], first[:, E:2 * E]
                step(v.tensor_scalar(over, cnt[:, 0:E], float(CAP), None, ALU.is_gt))
                for j in range(2, 4):
                    step(v.scalar_tensor_tensor(out=over, in0=cnt[:, 0:E], scalar=float(CAP * j), in1=over,
                                                op0=ALU.is_gt, op1=ALU.add))
                step(v.tensor_tensor(upto, over, less, ALU.add))
                step(v.tensor_copy(n_over[:], upto[0:1, E - 1:E]))

                def by_expert(a):
                    return a.rearrange("p (o e) -> p o e", o=1).to_broadcast([P, OVER + 1, E])

                def by_item(a):
                    return a.rearrange("p (t o) -> p t o", o=1).to_broadcast([P, OVER + 1, E])

                step(v.tensor_tensor(is_item, by_expert(less), by_item(over_t[:]), ALU.is_le))
                step(v.tensor_tensor(item_tmp, by_expert(upto), by_item(over_t[:]), ALU.is_gt))
                step(v.tensor_tensor(is_item, is_item, item_tmp, ALU.mult))
                step(v.tensor_reduce(item_is, is_item, AX, ALU.add))
                for src, dst, last_one in ((first[:, 0:E], item_slot, first[:, E - 1:E]),
                                           (e256[:, 0, :], item_key, e256[:, 0, E - 1:E])):
                    step(v.scalar_tensor_tensor(out=over, in0=less, scalar=-float(CAP), in1=src, op0=ALU.mult,
                                                op1=ALU.add))
                    step(v.tensor_tensor(item_tmp, is_item, by_expert(over), ALU.mult))
                    step(v.tensor_reduce(dst, item_tmp, AX, ALU.add))
                    step(v.tensor_scalar(item_pad, over_cap[:], last_one, None, ALU.subtract))
                    step(v.tensor_tensor(item_pad, item_pad, item_is, ALU.mult))
                    step(v.tensor_tensor(dst, dst, item_pad, ALU.add))
                    step(v.tensor_scalar(dst, dst, last_one, None, ALU.add))
                step(v.tensor_copy(start_tab[:, E - 1:E + OVER], item_slot[0:1, :]))
                step(v.tensor_copy(key_tab[:, E - 1:E + OVER], item_key))
                step(v.tensor_tensor(item_tmp, is_item, by_expert(e256[:, 0, :]), ALU.mult))
                step(v.tensor_reduce(item_pad, item_tmp, AX, ALU.add))
                v.tensor_scalar(item_e[:, 0:OVER + 1], item_pad[0:1, :], 1.0 / 256, None,
                                ALU.mult).then_inc(tables_ready, 1)

            def fetch(n):
                dve.wait_ge(chunk_used, n * 6 + (D_0 - 2))
                s = dve.value_load(start_tab[0:1, bass.ds(n, 1)], min_val=0, max_val=2 * T)
                v.tensor_copy(xe, xgT[:, :, bass.ds(s, CAP)]).then_inc(xe_ready, 1)

            def gate_answers(n):
                dve.wait_ge(chunk_used, n * 6 + (D_0 + 6))
                for q in range(2):
                    last = v.tensor_tensor(yg[:, q * 512:(q + 1) * 512], y_ps[q][:, :], gate_f[:, q * 512:(q + 1) * 512],
                                           ALU.mult)
                last.then_inc(yg_ready, 1)

            def weights_of(n):
                v.tensor_tensor(key_col[:], lane[:], key_tab[:, bass.ds(n, 1)], ALU.add).then_inc(comb_step, 1)
                dve.wait_ge(comb_step, n * 3 + 1)
                v.scalar_tensor_tensor(out=comb, in0=keys[:, 0, :], scalar=key_col[:, 0:1], in1=keys[:, 2, :],
                                       op0=ALU.is_equal, op1=ALU.mult).then_inc(comb_step, 1)
                v.scalar_tensor_tensor(out=comb2, in0=keys[:, 1, :], scalar=key_col[:, 0:1], in1=keys[:, 3, :],
                                       op0=ALU.is_equal, op1=ALU.mult).then_inc(comb_step, 1)
                dve.wait_ge(comb_step, n * 3 + 3)
                dve.wait_ge(yg_ready, n + 1)
                v.tensor_tensor(comb, comb, comb2, ALU.add).then_inc(comb_ready, 1)

            def gated(n):
                dve.wait_ge(sil_ready, n + 1)
                v.tensor_tensor(gg[0:CAP, :], sil[0:CAP, :], h_ps[CAP:2 * CAP, :], ALU.mult).then_inc(g_ready, 1)

            def add_pair(n, j):
                b, q = j // 2, j % 2
                dve.wait_ge(add_done, n * 4 + (j + 1))
                for half in range(2):
                    col = half * 1024 + q * 512
                    piece = xs[:, b, col:col + 512]
                    last = v.tensor_tensor(piece, piece, add_ps[2 * (j % 2) + half][:, :], ALU.add)
                last.then_inc(added, 1)

            def add_answers(n):
                for j in range(4):
                    add_pair(n, j)

            dve.wait_ge(starts_ready, 1)
            dve.wait_ge(evac_act, 16)
            dve.wait_ge(evac_dve, 16)
            dve.wait_ge(keys_ready, 1)
            fetch(0)
            tables()

            def item(n):
                fetch(n)
                gate_answers(n - 1)
                weights_of(n - 1)
                gated(n)
                add_answers(n - 1)

            gated(0)
            with dve.Fori(1, E - 1) as n:
                item(n)
            dve.wait_ge(tables_ready, 1)
            items = dve.value_load(n_over[0:1, 0:1], min_val=0, max_val=OVER)
            with dve.Fori(0, OVER) as t:
                with dve.If(t < items):
                    item(t + (E - 1))
                dve.end_ifs()
            item(items + (E - 1))
            gate_answers(items + (E - 1))
            weights_of(items + (E - 1))

            def weigh(b):
                return v.tensor_tensor(answer[:, b, :], xs[:, b, :], buf_r[:], ALU.mult)

            dve.wait_ge(final_w_in, 16)
            for j in range(4):
                add_pair(items + (E - 1), j)
                if j == 1:
                    dve.wait_ge(added, items * 4 + (4 * (E - 1) + 2))
                    weigh(0)
            dve.wait_ge(added, items * 4 + 4 * E)
            weigh(1).then_inc(weighted, 1)
            dve.wait_ge(weighted, 1)
            dve.wait_ge(sq_done, NB + 4 * NB + 8)
            inverse_rms(3, 4, inverse_ready)
            for b in range(NB):
                piece = answer[:, b, 0:1024]
                v.tensor_scalar(piece, piece, rinv[:, b:b + 1], None, ALU.mult).then_inc(out_dve, 1)


def decays():
    import numpy as np

    t = np.arange(P, dtype=np.float32)
    far = t[:, None] - t[None, :]
    causal = far >= 0
    decay = np.zeros((P, RHEADS, 2 * P), np.float32)
    for h in range(RHEADS):
        gamma = 1.0 - 2.0 ** (-5.0 - h)
        own = np.where(causal, gamma ** np.maximum(far, 0), 0.0).T
        decay[:, h] = np.concatenate([own, gamma ** (far + P).T], 1) * DR ** -0.5
    return decay.astype(np.float32).reshape(P, -1)


_INS = ["x", "c", "w_ada", "b_ada", "norm_mix_w", "w_in", "ret_norm_w", "w_out", "norm_ffn_w", "w_group",
        "b_group", "w_router", "b_router", "w1", "w3", "w2", "norm_final_w"]


def kernel(**inputs):
    import numpy as np
    import concourse.bacc as bacc
    from concourse.bass_utils import run_bass_kernel_spmd as run

    nc = bacc.Bacc("TRN2", target_bir_lowering=False, num_devices=1)
    arrays = {f"in_{n}": np.ascontiguousarray(inputs[n]) for n in _INS}
    arrays["decay"] = decays()
    args = [nc.dram_tensor(n, a.shape, mybir.dt.from_np(a.dtype), kind="ExternalInput").ap() for n, a in arrays.items()]
    rows_dram = nc.dram_tensor("ada_rows", [4, 6 * D], F32, kind="Internal").ap()
    out = nc.dram_tensor("out", [1, T, D], F32, kind="ExternalOutput").ap()
    build(nc, *args, rows_dram, out)
    return run(nc, [arrays], core_ids=[0]).results[0]["out"]
```

```python
from contextlib import ExitStack

import concourse.bass as bass
from concourse import mybir

F32 = mybir.dt.float32
F32R = mybir.dt.float32r
I32 = mybir.dt.int32
ALU = mybir.AluOpType
ACT = mybir.ActivationFunctionType
AX = mybir.AxisListType.X

P = 128
D = 2048
T = 256
NB = T // P
K16 = D // P
HEADS, DH = 8, 128
PAIRS = HEADS // 2
RHEADS, DR = 4, 256
CW = 256
SECT = D // CW
E, DE = 32, 512
GROUPS, EPG = 4, 8
K4 = DE // P
CAP = 64
OVER = (2 * T - 1) // CAP
SLOTS = 2 * T + CAP
RING = 6
LATE = 10
CH = 4096
EPS = 1e-6
ROUTE = 900
QUARTER = CH // 4
TRI = 384
N_A, N_B1, N_B2, N_C = 2 * SECT, 6 * PAIRS, 9 * RHEADS, 8
B1_0, B2_0 = N_A, N_A + N_B1
C_0 = B2_0 + N_B2
W_B2 = 4 * 3 * PAIRS
W_C = W_B2 + 4 * 4 * RHEADS
ROWS = 5
D_0 = C_0 + N_C


def build(nc, x, c, w_ada, b_ada, norm_mix_w, w_in, ret_norm_w, w_out, norm_ffn_w, w_group, b_group,
          w_router, b_router, w1, w3, w2, norm_final_w, decay, rows_dram, out):
    ctx = ExitStack()
    with ctx:
        def sb(name, shape, dt=F32):
            return ctx.enter_context(nc.sbuf_tensor(name, shape, dt))

        def sem(name):
            return ctx.enter_context(nc.semaphore(name))

        def place(name, shape):
            tile_ = sb(name, shape)
            return tile_, nc.sbuf_base - 4 * shape[1] * (shape + [1])[2]

        def in_place_of(name, shape, offset):
            return nc.alloc_sbuf_tensor_at(name, shape, F32R, offset=offset)

        ring = sb("ring", [P, RING, CH])
        buf_a, at_a = place("buf_a", [P, CH])
        xs, at_x = place("xs", [P, NB, D])
        buf_b, at_b = place("buf_b", [P, CH])
        buf_g, at_g = place("buf_g", [P, K16 * SLOTS])
        buf_mr, at_mr = place("buf_mr", [P, 2 * D])
        buf_m = buf_mr[:, 0:D]
        buf_r = buf_mr[:, D:2 * D]
        w_hi = in_place_of("w_hi", [P, 2, QUARTER], at_a)
        w_lo = in_place_of("w_lo", [P, 2, QUARTER], at_a + 4 * 2 * QUARTER)
        h_hi = in_place_of("h_hi", [P, K16, T], at_mr)
        h_lo = in_place_of("h_lo", [P, K16, T], at_x)
        mix_hi = in_place_of("mix_hi", [P, K16, T], at_g)
        mix_lo = in_place_of("mix_lo", [P, K16, T], at_b)
        x1n_hi = in_place_of("x1n_hi", [P, NB, D], at_a)
        x1n_lo = in_place_of("x1n_lo", [P, NB, D], at_b)
        onehot = in_place_of("onehot", [P, NB, 2 * T], at_mr + 4 * D)
        c_route = sb("c_route", [P, K16 * (32 + 4 + E)])
        c_pad = c_route[:, 0:K16 * 32].rearrange("p (k m) -> p k m", k=K16)
        w_route = c_route[:, K16 * 32:K16 * (32 + 4 + E)].rearrange("p (k n) -> p k n", k=K16)
        ident = sb("ident", [P, P])
        ones = sb("ones", [P, P])
        before = sb("before", [P, P])
        b_route = sb("b_route", [P, 4 + E])
        c_col = sb("c_col", [P, K16])
        b_col = sb("b_col", [P, 6, K16])
        mix_w = sb("mix_w", [P, K16])
        ffn_w = sb("ffn_w", [P, K16])
        ret_w = sb("ret_w", [P, 8])
        mod_raw = sb("mod_raw", [P, 4, 2, K16])
        shift = sb("shift", [P, K16])
        scale = sb("scale", [P, K16])
        sumsq = sb("sumsq", [P, NB, 4])
        ms = sb("ms", [P, NB])
        rt = sb("rt", [P, NB])
        rinv = sb("rinv", [P, NB])
        smax = sb("smax", [P, 2, 2])
        ssum = sb("ssum", [P, 2, 2])
        sinv = sb("sinv", [P, 2, 2])
        rev8 = sb("rev8", [P, 8])
        e256 = sb("e256", [P, 1, E])
        lane = sb("lane", [P, 1])
        key_tab = sb("key_tab", [P, E + OVER + 1])
        start_tab = sb("start_tab", [1, E + OVER + 1], I32)
        item_e = sb("item_e", [1, OVER + 1], I32)
        n_over = sb("n_over", [1, 1], I32)
        key_col = sb("key_col", [P, 1])
        over_cap = sb("over_cap", [P, OVER + 1])
        over_t = sb("over_t", [P, OVER + 1])
        sums2 = sb("sums2", [P, 2 * K16])
        route = sb("route", [P, ROUTE])

        used = [0]

        def small(n, rows=P):
            used[0] += n
            assert used[0] <= ROUTE
            return route[0:rows, used[0] - n:used[0]]

        lg = small(NB * 36).rearrange("p (b n) -> p b n", b=NB)
        gmax, top1, m1, m2, gsum = (small(NB) for _ in range(5))
        eq4 = small(NB * 4).rearrange("p (b n) -> p b n", b=NB)
        og = small(NB * 4).rearrange("p (b n) -> p b n", b=NB)
        exp_in = [small(NB * 4), small(NB)]
        exp_out = [small(NB * 4), small(NB)]
        lsel = small(NB * E).rearrange("p (b g e) -> p b g e", b=NB, g=GROUPS)
        el, eq8, o1, o2 = (small(NB * EPG).rearrange("p (b e) -> p b e", b=NB) for _ in range(4))
        chosen = small(2 * NB * E).rearrange("p (q b e) -> p q b e", q=2, b=NB)
        both = small(NB * E).rearrange("p (b e) -> p b e", b=NB)
        w_tok = small(2 * NB).rearrange("p (q b) -> p q b", q=2)
        cnt = small(3 * E)
        cnt_col = small(2, E)
        cnt_rep = buf_m[0:E, 1536:1792].rearrange("p (q m) -> p q m", q=2)
        first = small(2 * E)
        where = small(2 * NB * E).rearrange("p (s b e) -> p s b e", s=2, b=NB)
        wtmp = small(NB * E).rearrange("p (b e) -> p b e", b=NB)
        slot_key = small(2 * 2 * NB).rearrange("p (s q b) -> p s q b", s=2, q=2)
        tab = small(2 * E)
        item_is, item_slot, item_key, item_pad = (small(OVER + 1) for _ in range(4))

        x_a = buf_a[:, :].rearrange("p (b d) -> p b d", b=NB)
        xnT = xs[:, :, :].rearrange("p b d -> p (b d)").rearrange("p (k t) -> p k t", k=K16)
        xn2T = buf_a[:, :].rearrange("p (k t) -> p k t", k=K16)
        xn = buf_b[:, :].rearrange("p (b d) -> p b d", b=NB)
        xn_k = buf_b[:, :].rearrange("p (b q k) -> p b k q", b=NB, k=K16)
        mixT = buf_b[:, :].rearrange("p (k t) -> p k t", k=K16)
        at = [0]

        def part(n):
            at[0] += n
            return buf_g[:, at[0] - n:at[0]]

        bias_sb = part(HEADS * T).rearrange("p (h n) -> p h n", h=HEADS)
        decay_sb = part(RHEADS * T)
        qT = part(512).rearrange("p (h t) -> p h t", h=2)
        kT = part(512).rearrange("p (h t) -> p h t", h=2)
        vv = part(512).rearrange("p (b n) -> p b n", b=2)
        pp = part(2 * TRI).rearrange("p (h n) -> p h n", h=2)
        ppT = part(2 * TRI).rearrange("p (h n) -> p h n", h=2)
        yy = part(512).rearrange("p (b n) -> p b n", b=2)
        sg = part(512).rearrange("p (b n) -> p b n", b=2)
        junk = part(512)
        ada_row = part(ROWS * CW).rearrange("p (m n) -> p m n", m=ROWS)
        assert at[0] <= K16 * SLOTS
        scoreT = pp[:, 0, :]
        xgT = buf_g[:, :].rearrange("p (k s) -> p k s", k=K16)
        is_item = buf_m[:, 1024:1024 + (OVER + 1) * E].rearrange("p (t e) -> p t e", e=E)
        item_tmp = buf_m[:, 1280:1280 + (OVER + 1) * E].rearrange("p (t e) -> p t e", e=E)
        diag = buf_r[:, 1024:2048].rearrange("p (b q n) -> p b q n", b=NB, q=4)
        iota_s = buf_m[:, 1024:1536]
        gate_f = buf_m[:, 0:1024]
        keys = buf_a[:, 0:1024].rearrange("p (q t) -> p q t", q=4)
        comb = buf_a[:, 1024:1280]
        comb2 = buf_a[:, 1280:1536]
        sil = buf_a[:, 1536:2048]
        gg = buf_a[:, 2048:2560]
        ggT = buf_a[:, 2560:2560 + K4 * CAP].rearrange("p (k s) -> p k s", k=K4)
        xe = c_route[:, 0:K16 * CAP].rearrange("p (k s) -> p k s", k=K16)
        yg = buf_b[:, 1024:2048]
        answer = buf_g[:, 0:NB * D].rearrange("p (b d) -> p b d", b=NB)
        square = buf_g[:, NB * D:NB * D + 8 * 512].rearrange("p (j n) -> p j n", n=512)

        banks = [ctx.enter_context(nc.psum_tensor(f"bank{i}", [P, 512], F32)) for i in range(8)]
        ada_ps = banks[0:2]
        proj_ps = banks[2:4]
        turn_ps = banks[4:8]
        sc_ps, sc2_ps, tr_ps, pv_ps = banks[4:8]
        k_ps = [pv_ps, sc2_ps]
        out_ps = [banks[2:4], banks[0:2]]
        h_ps, gt_ps = banks[0], banks[1]
        y_ps = banks[2:4]
        add_ps = banks[4:8]
        last_add_ps = banks[4:8] + banks[0:4]

        small_in = sem("small_in")
        x_in = sem("x_in")
        const_in = sem("const_in")
        late_in = sem("late_in")
        arrived = [sem(f"arrived{i}") for i in range(RING)]
        chunk_used = sem("chunk_used")
        w_hi_ready = sem("w_hi_ready")
        w_lo_ready = sem("w_lo_ready")
        split_used = sem("split_used")
        h_hi_ready = sem("h_hi_ready")
        h_lo_ready = sem("h_lo_ready")
        mix_hi_ready = sem("mix_hi_ready")
        mix_lo_ready = sem("mix_lo_ready")
        consts_made = sem("consts_made")
        bias_step = sem("bias_step")
        c_ready = sem("c_ready")
        sq_done = sem("sq_done")
        ms_done = sem("ms_done")
        rt_done = sem("rt_done")
        xn_ready = sem("xn_ready")
        turned = sem("turned")
        evac_dve = sem("evac_dve")
        evac_act = sem("evac_act")
        ada_copied = sem("ada_copied")
        row_stored = [sem(f"row_stored{m}") for m in range(ROWS)]
        cols_made = sem("cols_made")
        dve_step = sem("dve_step")
        mod_dve = sem("mod_dve")
        mod_act = sem("mod_act")
        col_ready = sem("col_ready")
        p0_out = sem("p0_out")
        p1_out = sem("p1_out")
        scored = sem("scored")
        logits = sem("logits")
        max_ready = sem("max_ready")
        exp_done = sem("exp_done")
        probs_ready = sem("probs_ready")
        probs_turned = sem("probs_turned")
        pT0_ready = sem("pT0_ready")
        pT1_ready = sem("pT1_ready")
        pv_done = sem("pv_done")
        mix_dve = sem("mix_dve")
        mix_act = sem("mix_act")
        decayed = sem("decayed")
        ret_pv = sem("ret_pv")
        ret_sq = sem("ret_sq")
        ret_ms = sem("ret_ms")
        ret_rt = sem("ret_rt")
        ret_step = sem("ret_step")
        ret_y = sem("ret_y")
        ret_turned = sem("ret_turned")
        ret_mix = sem("ret_mix")
        gate_rows = sem("gate_rows")
        gatef_rows = sem("gatef_rows")
        mod2_in = sem("mod2_in")
        gm_ps = sem("gm_ps")
        gm_ready = sem("gm_ready")
        x1_piece = sem("x1_piece")
        gf_ps = sem("gf_ps")
        gf_ready = sem("gf_ready")
        logits_ps = sem("logits_ps")
        route_exp_in = sem("route_exp_in")
        route_exp = sem("route_exp")
        x1n_hi_ready = sem("x1n_hi_ready")
        x1n_lo_ready = sem("x1n_lo_ready")
        picks = sem("picks")
        counts_ps = sem("counts_ps")
        counts_sb = sem("counts_sb")
        starts_ps = sem("starts_ps")
        onehot_ready = sem("onehot_ready")
        diag_ready = sem("diag_ready")
        keys_ps = sem("keys_ps")
        keys_ready = sem("keys_ready")
        iota_ready = sem("iota_ready")
        gathered = sem("gathered")
        starts_ready = sem("starts_ready")
        tables_ready = sem("tables_ready")
        final_w_in = sem("final_w_in")
        xe_ready = sem("xe_ready")
        xe_rest_ready = sem("xe_rest_ready")
        sil_ready = sem("sil_ready")
        g_ready = sem("g_ready")
        gT_ps = sem("gT_ps")
        gT_ready = sem("gT_ready")
        yg_ready = sem("yg_ready")
        comb_step = sem("comb_step")
        comb_ready = sem("comb_ready")
        add_done = sem("add_done")
        added = sem("added")
        out_ready = sem("out_ready")
        stored = sem("stored")

        ada_v = w_ada[0].rearrange("(p k) n -> p k n", k=K16)
        win_v = w_in[0].rearrange("(p k) n -> p k n", k=K16)
        wout_v = w_out[0].rearrange("(k p) n -> p k n", p=P)
        w13_v = [w[0].rearrange("e (p k) n -> p e k n", k=K16) for w in (w1, w3)]
        w2_v = w2[0].rearrange("e (p k) n -> p e k n", k=K4)

        def slot_cols(n):
            return ring[:, n % RING, :].rearrange("p (k n) -> p k n", k=K16)

        def slot_512(n):
            return ring[:, n % RING, :].rearrange("p (k n) -> p k n", n=512)

        def slot_w2(n):
            return ring[:, n % RING, :].rearrange("p (k n) -> p k n", n=D)

        def quarter(n, qr):
            return ring[:, n % RING, qr * QUARTER:(qr + 1) * QUARTER]

        def wait(eng, s, value):
            if isinstance(value, int) and value <= 0:
                return
            eng.wait_ge(s, value)

        def await_chunk(eng, n, turns=0):
            eng.wait_ge(arrived[n % RING], (turns + n // RING + 1) * 16)

        block = ctx.enter_context(nc.Block())

        @block.sync
        def _(sp):
            def load(n, turns, dst, src):
                wait(sp, chunk_used, turns * RING + (n - RING + 1))
                sp.dma_start(dst, src).then_inc(arrived[n % RING], 16)

            def ada(n, turns, a):
                load(n, turns, slot_cols(n), ada_v[:, :, bass.ds(a * CW, CW)])

            def win(n, turns, col):
                load(n, turns, slot_cols(n), win_v[:, :, bass.ds(col, CW)])

            def expert(n0, turns, e):
                for hf in range(2):
                    for m in range(2):
                        n = n0 + 2 * hf + m
                        load(n, turns, slot_512(n), w13_v[m][:, e, 8 * hf:8 * hf + 8, :].rearrange("p o k n -> p (o k) n"))
                for hf in range(2):
                    n = n0 + 4 + hf
                    load(n, turns, slot_w2(n), w2_v[:, e, 2 * hf:2 * hf + 2, :].rearrange("p o k n -> p (o k) n"))

            sp.dma_start(c_col[:], c.rearrange("o (p k) -> p (o k)", k=K16)).then_inc(small_in, 16)
            sp.dma_start(x_a, x.rearrange("o (b p) d -> p (o b) d", p=P)).then_inc(x_in, 16)
            for n in range(RING):
                ada(n, 0, n)
            sp.dma_start(b_col[:], b_ada.rearrange("o (s p k) -> p (o s) k", k=K16, p=P)).then_inc(const_in, 16)
            sp.dma_start(mix_w[:], norm_mix_w.rearrange("o (p k) -> p (o k)", k=K16)).then_inc(const_in, 16)
            for n in range(RING, N_A):
                ada(n, 0, n)
            with sp.Fori(0, PAIRS) as i:
                for m in range(3):
                    win(B1_0 + 2 * m, i, 1024 * m + i * CW)
                    ada(B1_0 + 2 * m + 1, i, 2 * SECT + m + i * 3)
            sp.dma_start(ffn_w[:], norm_ffn_w.rearrange("o (p k) -> p (o k)", k=K16)).then_inc(late_in, 16)
            with nc.allow_non_contiguous_dma(reason="1024 weights, once"):
                sp.dma_start(ret_w[:], ret_norm_w.rearrange("o (k p) -> p (o k)", p=P)).then_inc(late_in, 16)
                sp.dma_start(w_route[:, :, 0:4], w_group.rearrange("o (p k) g -> p (o k) g", k=K16)).then_inc(late_in, 16)
                for g in range(GROUPS):
                    sp.dma_start(w_route[:, :, 4 + EPG * g:4 + EPG * (g + 1)],
                                 w_router[0, g].rearrange("(p k) e -> p k e", k=K16)).then_inc(late_in, 16)
            sp.dma_start(b_route[:, 0:4], b_group[0].partition_broadcast(P)).then_inc(late_in, 16)
            sp.dma_start(b_route[:, 4:4 + E], b_router.rearrange("o g e -> (o g e)").partition_broadcast(P)).then_inc(late_in, 16)
            sp.dma_start(decay_sb, decay).then_inc(late_in, 16)
            with sp.Fori(0, RHEADS // 2) as i:
                for r in range(2):
                    n = B2_0 + 9 * r
                    for m in range(4):
                        win(n + 2 * m, i * 3, 3072 + 1024 * m + r * CW + i * (2 * CW))
                        ada(n + 2 * m + 1, i * 3, 2 * SECT + 3 * PAIRS + 5 * r + m + i * 10)
                    ada(n + 8, i * 3, 2 * SECT + 3 * PAIRS + 5 * r + 4 + i * 10)
            for cc in range(4):
                for hf in range(2):
                    n = C_0 + 2 * cc + hf
                    load(n, 0, slot_512(n), wout_v[:, 8 * hf:8 * hf + 8, cc * 512:(cc + 1) * 512])
                if cc == 1:
                    sp.wait_ge(split_used, W_C)
                    sp.dma_start(xs[:], x.rearrange("o (b p) d -> p (o b) d", p=P)).then_inc(x_in, 16)
            with sp.Fori(0, E - 1) as e:
                expert(D_0, e, bass.ds(e, 1))
            sp.wait_ge(tables_ready, 1)
            items = sp.value_load(n_over[0:1, 0:1], min_val=0, max_val=OVER)
            with sp.Fori(0, OVER) as t:
                with sp.If(t < items):
                    e = sp.value_load(item_e[0:1, bass.ds(t, 1)], min_val=0, max_val=E - 1)
                    expert(D_0, t + (E - 1), bass.ds(e, 1))
                sp.end_ifs()
            expert(D_0, items + (E - 1), slice(E - 1, E))
            for h in range(4):
                b, q = h // 2, h % 2
                sp.wait_ge(out_ready, h + 1)
                sp.dma_start(out[0, b * P:(b + 1) * P, q * 1024:(q + 1) * 1024],
                             answer[:, b, q * 1024:(q + 1) * 1024]).then_inc(stored, 16)
            sp.wait_ge(stored, 64)

        @block.gpsimd
        def _(pool):
            nc.gpsimd.memset(c_pad, 0.0).then_inc(consts_made, 1)
            nc.gpsimd.memset(ones[:], 1.0).then_inc(consts_made, 1)
            pool.wait_ge(consts_made, 2)
            nc.gpsimd.affine_select(out=ident[:], in_=ones[:], compare_op=ALU.is_equal, fill=0.0, base=0,
                                    pattern=[[-1, P]], channel_multiplier=1).then_inc(consts_made, 1)
            nc.gpsimd.affine_select(out=before[:], in_=ones[:], compare_op=ALU.is_gt, fill=0.0, base=0,
                                    pattern=[[1, P]], channel_multiplier=-1).then_inc(consts_made, 1)
            nc.gpsimd.iota(rev8[:], pattern=[[-1, 8]], base=8, channel_multiplier=0,
                           allow_small_or_imprecise_dtypes=True).then_inc(consts_made, 1)
            nc.gpsimd.iota(e256[:, 0, :], pattern=[[256, E]], base=0, channel_multiplier=0,
                           allow_small_or_imprecise_dtypes=True).then_inc(consts_made, 1)
            nc.gpsimd.iota(key_tab[:, 0:E], pattern=[[256, E]], base=0, channel_multiplier=0,
                           allow_small_or_imprecise_dtypes=True).then_inc(consts_made, 1)
            for hf in range(2):
                pool.wait_ge(consts_made, 7 + hf)
                nc.gpsimd.iota(lane[CAP * hf:CAP * (hf + 1), :], pattern=[[0, 1]], base=0, channel_multiplier=1,
                               allow_small_or_imprecise_dtypes=True).then_inc(consts_made, 1)
            pool.wait_ge(consts_made, 9)
            for m in range(ROWS):
                nc.gpsimd.memset(ada_row[:, m, :], 0.0).then_inc(row_stored[m], 16)
            for j, base in enumerate((0, -P)):
                nc.gpsimd.iota(junk[:, j * P:(j + 1) * P], pattern=[[1, P]], base=base, channel_multiplier=-1,
                               allow_small_or_imprecise_dtypes=True).then_inc(bias_step, 1)
            pool.wait_ge(bias_step, 2)
            tile = junk[:, 0:P]
            nc.gpsimd.affine_select(out=tile, in_=tile, compare_op=ALU.is_ge, fill=-1e34, base=0,
                                    pattern=[[-1, P]], channel_multiplier=1).then_inc(bias_step, 1)
            pool.wait_ge(bias_step, 3)
            for h in range(HEADS):
                nc.gpsimd.tensor_scalar(bias_sb[:, h, :], junk[:, 0:T], 2.0 ** (-8.0 * (h + 1) / HEADS), None,
                                        ALU.mult).then_inc(bias_step, 1)
            nc.gpsimd.iota(over_cap[:], pattern=[[CAP, OVER + 1]], base=CAP, channel_multiplier=0,
                           allow_small_or_imprecise_dtypes=True).then_inc(bias_step, 1)
            nc.gpsimd.iota(over_t[:], pattern=[[1, OVER + 1]], base=0, channel_multiplier=0,
                           allow_small_or_imprecise_dtypes=True).then_inc(bias_step, 1)
            pool.wait_ge(x1_piece, 4 * NB)
            nc.gpsimd.iota(iota_s, pattern=[[1, 512]], base=0, channel_multiplier=0,
                           allow_small_or_imprecise_dtypes=True).then_inc(iota_ready, 1)
            pool.wait_ge(sq_done, NB + 4 * NB)
            nc.gpsimd.memset(xgT[:, :, 2 * T:SLOTS], 0.0).then_inc(iota_ready, 1)
            for b in range(NB):
                pool.wait_ge(x1n_hi_ready, b + 1)
                nc.gpsimd.tensor_tensor(x1n_lo[:, b, :], xn[:, b, :], x1n_hi[:, b, :],
                                        ALU.subtract).then_inc(x1n_lo_ready, 1)

        @block.tensor
        def _(pe):
            mm = nc.tensor.matmul

            def keep_warm(n, bank=turn_ps[3]):
                for _ in range(n):
                    mm(bank[:, 0:P], ones[:], ident[:], start=True, stop=True)

            def turn_group(g):
                bank = turn_ps[g % 4]
                for j in range(4):
                    last = nc.tensor.transpose(bank[:, j * P:(j + 1) * P], xn_k[:, j % 2, 2 * g + j // 2, :],
                                               ident[:])
                last.then_inc(turned, 1)

            def ada(n, turns, par, copied, halves=(0, 1)):
                if halves[0] == 0:
                    await_chunk(pe, n, turns)
                    wait(pe, ada_copied, copied)
                w = slot_cols(n)
                for k in range(8 * halves[0], 8 * halves[-1] + 8):
                    g = 32 * (k % 4)
                    last = mm(ada_ps[par][g:g + 32, 0:CW], c_pad[:, k, :], w[:, k, :],
                              start=k < 4, stop=k >= K16 - 4)
                if halves[-1] == 1:
                    last.then_inc(chunk_used, 1)

            def products(x, plan, half_ready=None):
                for qr in range(4):
                    if half_ready is not None and qr == 2:
                        pe.wait_ge(half_ready, 2)
                    pe.wait_ge(w_lo_ready, x + (qr + 1))
                    for j, ((out_, stationary, moving), start, stop) in enumerate(plan(qr)):
                        last = mm(out_, stationary, moving, start=start, stop=stop)
                        if qr == 3 and j == 0:
                            last.then_inc(chunk_used, 1)
                    last.then_inc(split_used, 1)

            W, H = (w_hi, w_lo), (h_hi, h_lo)
            PARTS = ((0, 0), (0, 1), (1, 0))

            def proj_T(x, pair, half_ready=None):
                def plan(qr):
                    for h in range(2):
                        for k in range(4):
                            for pw, ph in PARTS:
                                col = k * CW + h * P
                                yield ((pair[h][:, 0:T], W[pw][:, qr % 2, col:col + P],
                                        H[ph][:, 4 * qr + k, :]),
                                       (qr, k, pw, ph) == (0, 0, 0, 0), (qr, k, pw) == (3, 3, 1))
                products(x, plan, half_ready)

            def proj(x, pair):
                def plan(qr):
                    for b in range(NB):
                        for k in range(4):
                            for pw, ph in PARTS:
                                yield ((pair[b][:, 0:CW], H[ph][:, 4 * qr + k, b * P:(b + 1) * P],
                                        W[pw][:, qr % 2, k * CW:(k + 1) * CW]),
                                       (qr, k, pw, ph) == (0, 0, 0, 0), (qr, k, pw) == (3, 3, 1))
                products(x, plan)

            def mix_out(x, hf, pair):
                mix = (mix_hi, mix_lo)

                def plan(qr):
                    for k in range(2):
                        for b in range(NB):
                            for pw, ph in PARTS:
                                yield ((pair[b][:, :], mix[ph][:, 8 * hf + 2 * qr + k, b * P:(b + 1) * P],
                                        W[pw][:, qr % 2, k * 512:(k + 1) * 512]),
                                       (hf, qr, k, pw, ph) == (0, 0, 0, 0, 0), (hf, qr, k, pw) == (1, 3, 1, 1))
                products(x, plan)

            pe.wait_ge(consts_made, 4)
            pe.wait_ge(xn_ready, 1)
            for g in range(8):
                if g >= 4:
                    pe.wait_ge(evac_dve if g % 2 == 0 else evac_act, (g - 4) // 2 + 1)
                turn_group(g)
            pe.wait_ge(c_ready, 1)
            pe.wait_ge(evac_dve, 4)
            pe.wait_ge(evac_act, 4)

            def to_columns(j):
                pe.wait_ge(ada_copied, 2 * j + 2)
                s, q = j // 4, 32 * (j % 4)
                rows_k = (buf_m, buf_r)[s].rearrange("p (q k) -> p k q", k=K16)
                for k in range(K16):
                    last = mm(sc_ps[q:q + 32, s * K16 + k:s * K16 + k + 1], rows_k[:, k, q:q + 32], ones[:, 0:1],
                              start=True, stop=True)
                return last

            for n in range(N_A):
                ada(n, 0, n % 2, n - 1)
                if n % 2 == 0 and n > 0:
                    to_columns(n // 2 - 1)
            to_columns(N_A // 2 - 1).then_inc(cols_made, 1)
            keep_warm(32)
            pe.wait_ge(h_lo_ready, 1)
            pe.wait_ge(h_lo_ready, 1)

            with pe.Fori(0, PAIRS) as i:
                a0 = 2 * SECT
                proj_T(i * 12, proj_ps, h_lo_ready)
                ada(B1_0 + 1, i, 0, i * 3 + a0)
                proj_T(i * 12 + 4, k_ps)
                ada(B1_0 + 3, i, 1, i * 3 + a0)
                pe.wait_ge(p0_out, i * 4 + 2)
                pe.wait_ge(p1_out, i * 2 + 2)
                for h, bank in enumerate((sc_ps, sc2_ps)):
                    mm(bank[:, 0:P], qT[:, h, 0:P], kT[:, h, 0:P], start=True, stop=True)
                    mm(bank[:, P:TRI], qT[:, h, P:T], kT[:, h, :], start=True, stop=True).then_inc(scored, 1)
                proj(i * 12 + 8, proj_ps)
                pe.wait_ge(probs_ready, i + 1)
                for h, bank in enumerate((tr_ps, sc2_ps)):
                    for j in range(3):
                        last = nc.tensor.transpose(bank[:, j * P:(j + 1) * P], pp[:, h, j * P:(j + 1) * P], ident[:])
                    last.then_inc(probs_turned, 1)
                ada(B1_0 + 5, i, 0, i * 3 + a0 + 1, (0,))
                pe.wait_ge(p0_out, i * 4 + 4)
                for h, bank in enumerate((pv_ps, tr_ps)):
                    pe.wait_ge((pT0_ready, pT1_ready)[h], i + 1)
                    v = vv[:, :, h * DH:(h + 1) * DH]
                    mm(bank[:, 0:P], v[:, 0, :], ppT[:, h, 0:P], start=True, stop=True)
                    mm(bank[:, P:T], v[:, 0, :], ppT[:, h, P:T], start=True, stop=False)
                    mm(bank[:, P:T], v[:, 1, :], ppT[:, h, T:TRI], start=False, stop=True).then_inc(pv_done, 1)
                ada(B1_0 + 5, i, 0, None, (1,))
                pe.wait_ge(mix_dve, i + 1)
                pe.wait_ge(mix_act, i + 1)

            with pe.Fori(0, RHEADS // 2) as i:
                for r in range(2):
                    n, t3, head = B2_0 + 9 * r, i * 3, i * 2 + r
                    a0 = 2 * SECT + 3 * PAIRS + 5 * r
                    w0 = W_B2 + 16 * r
                    proj_T(i * 32 + w0, proj_ps)
                    ada(n + 1, t3, 0, i * 10 + a0)
                    proj_T(i * 32 + (w0 + 4), k_ps)
                    ada(n + 3, t3, 1, i * 10 + a0)
                    pe.wait_ge(p0_out, head * 4 + (4 * PAIRS + 2))
                    pe.wait_ge(p1_out, head * 4 + (2 * PAIRS + 2))
                    for j in range(2):
                        mm(sc_ps[:, 0:T], kT[:, j, 0:P], qT[:, j, :], start=j == 0, stop=j == 1)
                    for j in range(2):
                        last = mm(sc_ps[:, T:TRI], kT[:, j, P:T], qT[:, j, P:T], start=j == 0, stop=j == 1)
                    last.then_inc(scored, 1)
                    proj(i * 32 + (w0 + 8), proj_ps)
                    ada(n + 5, t3, 0, i * 10 + (a0 + 1))
                    pe.wait_ge(decayed, head + 1)
                    pe.wait_ge(p0_out, head * 4 + (4 * PAIRS + 4))
                    mm(pv_ps[:, 0:T], scoreT[:, 0:P], vv[:, 0, :], start=True, stop=True)
                    mm(pv_ps[:, T:512], scoreT[:, P:T], vv[:, 0, :], start=True, stop=False)
                    mm(pv_ps[:, T:512], scoreT[:, T:TRI], vv[:, 1, :], start=False, stop=True).then_inc(ret_pv, 1)
                    proj(i * 32 + (w0 + 12), proj_ps)
                    ada(n + 7, t3, 1, i * 10 + (a0 + 2))
                    ada(n + 8, t3, 0, i * 10 + (a0 + 3))
                    pe.wait_ge(ret_y, head + 1)
                    for j in range(4):
                        last = nc.tensor.transpose(tr_ps[:, j * P:(j + 1) * P], yy[:, j % 2, (j // 2) * P:(j // 2 + 1) * P],
                                                   ident[:])
                    last.then_inc(ret_turned, 1)

            pe.wait_ge(mix_lo_ready, 1)
            for cc in range(4):
                wait(pe, x1_piece, NB * (cc - 1))
                if cc == 1:
                    pe.wait_ge(ada_copied, 6 * SECT)
                for hf in range(2):
                    if (cc, hf) == (0, 1):
                        pe.wait_ge(mix_lo_ready, 2)
                    mix_out(W_C + 8 * cc + 4 * hf, hf, out_ps[cc % 2])
                    if (cc, hf) == (1, 0):
                        pe.wait_ge(ret_mix, RHEADS)
                        pe.wait_ge(gate_rows, 32)
                        for q in range(4):
                            mm(turn_ps[q][:, :], ones[0:5, :], buf_r[0:5, q * 512:(q + 1) * 512],
                               start=True, stop=True).then_inc(gm_ps, 1)

            pe.wait_ge(gm_ready, 4)
            keep_warm(11)
            pe.wait_ge(gatef_rows, 32)
            pe.wait_ge(x1_piece, 4 * NB)
            for q in range(2):
                for half in range(2):
                    last = mm(ada_ps[q][CAP * half:CAP * (half + 1), :], ones[0:5, 0:CAP],
                              buf_r[0:5, half * 1024 + q * 512:half * 1024 + (q + 1) * 512], start=True, stop=True)
                last.then_inc(gf_ps, 1)

            def logits_of(g):
                pe.wait_ge(evac_dve if g % 2 == 0 else evac_act, 4 + g // 2 + 1)
                for k in (2 * g, 2 * g + 1):
                    for b in range(NB):
                        last = mm(proj_ps[b][:, 0:36], xn2T[:, k, b * P:(b + 1) * P], w_route[:, k, :],
                                  start=k == 0, stop=k == K16 - 1)
                return last

            keep_warm(5)
            pe.wait_ge(late_in, LATE * 16)
            pe.wait_ge(xn_ready, 2)
            for g in range(8):
                wait(pe, evac_dve if g % 2 == 0 else evac_act, 4 + (g - 4) // 2 + 1 if g >= 4 else 0)
                turn_group(g)
                if g >= 3:
                    logits_of(g - 3)
            logits_of(5)
            logits_of(6)
            logits_of(7).then_inc(logits_ps, 1)
            keep_warm(24)
            pe.wait_ge(picks, 1)
            pe.wait_ge(gf_ready, 2)
            cps = proj_ps[1]
            mm(cps[:, 0:E], ones[:], both[:, 0, :], start=True, stop=False)
            mm(cps[:, 0:E], ones[:], both[:, 1, :], start=False, stop=True)
            mm(cps[:, E:2 * E], before[:], both[:, 0, :], start=True, stop=True)
            mm(cps[:, 2 * E:3 * E], ones[:], both[:, 0, :], start=True, stop=False)
            mm(cps[:, 2 * E:3 * E], before[:], both[:, 1, :], start=False, stop=True)
            mm(ada_ps[0][0:E, 0:1], both[:, 0, :], ones[:, 0:1], start=True, stop=False)
            mm(ada_ps[0][0:E, 0:1], both[:, 1, :], ones[:, 0:1], start=False, stop=True).then_inc(counts_ps, 1)
            pe.wait_ge(counts_sb, 1)
            mm(ada_ps[1][:, 0:E], cnt_rep[:, 0, :], before[0:E, 0:E], start=True, stop=True)
            mm(ada_ps[1][:, E:2 * E], cnt_rep[:, 1, :], before[0:E, 0:E], start=True, stop=True).then_inc(starts_ps, 1)
            def hidden(n, halves=(0, 1)):
                if halves[0] == 0:
                    pe.wait_ge(xe_ready, n + 1)
                for hf in halves:
                    for m in range(2):
                        await_chunk(pe, D_0 + 2 * hf + m, n)
                    w = [slot_512(D_0 + 2 * hf + m) for m in range(2)]
                    for k in range(8):
                        for m in range(2):
                            last = mm(h_ps[CAP * m:CAP * (m + 1), :], xe[:, 8 * hf + k, :], w[m][:, k, :],
                                      start=hf == 0 and k == 0, stop=hf == 1 and k == 7)
                            if k == 7:
                                last.then_inc(chunk_used, 1)

            keep_warm(26)
            x1n_parts = [t[:, :, :].rearrange("p b (q k) -> p b k q", k=K16) for t in (x1n_hi, x1n_lo)]
            pe.wait_ge(x1n_lo_ready, 2)
            pe.wait_ge(onehot_ready, 1)
            for k in range(K16):
                if k >= 4:
                    wait(pe, evac_dve if k % 2 == 0 else evac_act, 8 + (k - 4) // 2 + 1)
                for b in range(NB):
                    for j, part_ in enumerate(x1n_parts):
                        last = mm(turn_ps[k % 4][:, :], part_[:, b, k, :], onehot[:, b, :], start=b + j == 0,
                                  stop=b + j == 2)
                last.then_inc(gathered, 1)
                if k == 9:
                    hidden(0, (0,))
            pe.wait_ge(xe_rest_ready, 1)
            hidden(0, (1,))
            pe.wait_ge(diag_ready, 1)
            for b in range(NB):
                last = mm(proj_ps[b][:, :], ones[:], diag[:, b], start=True, stop=True)
            last.then_inc(keys_ps, 1)

            def turn_hidden(n):
                pe.wait_ge(g_ready, n + 1)
                g_k = gg[0:CAP, :].rearrange("p (q k) -> p k q", k=K4)
                for k in range(K4):
                    last = mm(gt_ps[:, k * CAP:(k + 1) * CAP], g_k[:, k, :], ident[0:CAP, 0:CAP],
                              start=True, stop=True)
                last.then_inc(gT_ps, 1)

            def outputs(n):
                pe.wait_ge(gT_ready, n + 1)
                for hf in range(2):
                    await_chunk(pe, D_0 + 4 + hf, n)
                    w = slot_w2(D_0 + 4 + hf)
                    for k in range(2):
                        for q in range(2):
                            for half in range(2):
                                col = half * 1024 + q * 512
                                last = mm(y_ps[q][CAP * half:CAP * (half + 1), :], ggT[:, 2 * hf + k, :],
                                          w[:, k, col:col + 512], start=hf == 0 and k == 0, stop=hf == 1 and k == 1)
                    last.then_inc(chunk_used, 1)

            def add_up(n, last_item=False):
                pe.wait_ge(comb_ready, n + 1)
                pe.wait_ge(yg_ready, n + 1)
                for j in range(4):
                    b, q = j // 2, j % 2
                    if j >= 2 and not last_item:
                        pe.wait_ge(added, n * 4 + (j - 1))
                    for half in range(2):
                        rows = slice(CAP * half, CAP * (half + 1))
                        last = mm((last_add_ps[2 * j + half] if last_item else add_ps[2 * (j % 2) + half])[:, :],
                                  comb[rows, b * P:(b + 1) * P], yg[rows, q * 512:(q + 1) * 512],
                                  start=True, stop=True)
                    last.then_inc(add_done, 1)

            def item(n, warm=(0, 0, 0)):
                hidden(n, (0,))
                add_up(n - 1)
                hidden(n, (1,))
                keep_warm(warm[0], gt_ps)
                turn_hidden(n)
                pe.wait_ge(yg_ready, n)
                keep_warm(warm[1], y_ps[0])
                outputs(n)
                keep_warm(warm[2], h_ps)

            turn_hidden(0)
            pe.wait_ge(keys_ready, 1)
            outputs(0)
            with pe.Fori(1, E - 1) as n:
                item(n)
            pe.wait_ge(tables_ready, 1)
            items = pe.value_load(n_over[0:1, 0:1], min_val=0, max_val=OVER)
            with pe.Fori(0, OVER) as t:
                with pe.If(t < items):
                    item(t + (E - 1))
                pe.end_ifs()
            item(items + (E - 1), warm=(6, 2, 6))
            add_up(items + (E - 1), last_item=True)

        @block.scalar
        def _(act):
            act.wait_ge(small_in, 16)
            act.wait_ge(consts_made, 1)
            nc.scalar.activation(c_pad[:, :, 0], c_col[:], ACT.Silu).then_inc(c_ready, 1)
            act.wait_ge(x_in, 16)
            for b in range(NB):
                nc.scalar.activation(xn[:, b, :], x_a[:, b, :], ACT.Square,
                                     accum_out=sumsq[:, b, 0:1]).then_inc(sq_done, 1)
            act.wait_ge(ms_done, 1)
            nc.scalar.activation(rt[:], ms[:], ACT.Sqrt).then_inc(rt_done, 1)
            for g in range(1, 8, 2):
                act.wait_ge(turned, g + 1)
                nc.scalar.copy(xnT[:, 2 * g:2 * g + 2, :].rearrange("p k t -> p (k t)"),
                               turn_ps[g % 4][:, :]).then_inc(evac_act, 1)
            for n in range(N_A):
                act.wait_ge(chunk_used, n + 1)
                rows = buf_m if n < SECT else buf_r
                nc.scalar.copy(rows[:, (n % SECT) * CW:(n % SECT + 1) * CW],
                               ada_ps[n % 2][:, 0:CW]).then_inc(ada_copied, 1)
            def split_hi(n, turns, qr, x):
                if qr == 0:
                    await_chunk(act, n, turns)
                wait(act, split_used, x + (qr - 1))
                nc.scalar.copy(w_hi[:, qr % 2, :], quarter(n, qr)).then_inc(w_hi_ready, 1)

            act.wait_ge(xn_ready, 1)
            for half in range(2):
                split_hi(B1_0, 0, half, 0)
                act.wait_ge(col_ready, 1)
                for k in range(8 * half + 1, 8 * half + 8, 2):
                    last = nc.scalar.activation(xnT[:, k, :], xnT[:, k, :], ACT.Identity, bias=shift[:, k:k + 1],
                                                scale=scale[:, k:k + 1])
                last.then_inc(mod_act, 1)
                act.wait_ge(mod_act, half + 1)
                act.wait_ge(mod_dve, half + 1)
                nc.scalar.copy(h_hi[:, 8 * half:8 * half + 8, :], xnT[:, 8 * half:8 * half + 8, :]
                               ).then_inc(h_hi_ready, 1)

            def ada_row_out(used, m, par, stored_before, copied, a):
                act.wait_ge(chunk_used, used)
                act.wait_ge(row_stored[m], stored_before)
                nc.scalar.copy(ada_row[:, m, :], ada_ps[par][:, 0:CW]).then_inc(ada_copied, 1)
                act.wait_ge(ada_copied, copied)
                act.dma_start(rows_dram[:, bass.ds(a * CW, CW)], ada_row[0:P:32, m, :]).then_inc(row_stored[m], 16)

            def attention_rows(i, m, par):
                ada_row_out(i * 6 + (B1_0 + 2 * m + 2), m, par, i * 16 + 16, i * 3 + (2 * SECT + m + 1),
                            i * 3 + (2 * SECT + m))

            with act.Fori(0, PAIRS) as i:
                def hi(m, qr):
                    split_hi(B1_0 + 2 * m, i, qr, i * 12 + 4 * m)

                hi(0, 2), hi(0, 3), hi(1, 0), hi(1, 1)
                attention_rows(i, 0, 0)
                hi(1, 2), hi(1, 3), hi(2, 0)
                act.wait_ge(split_used, i * 12 + 8)
                for j in range(2):
                    nc.scalar.copy(kT[:, j, :], k_ps[j][:, 0:T]).then_inc(p1_out, 1)
                hi(2, 1)
                attention_rows(i, 1, 1)
                hi(2, 2)
                act.wait_ge(max_ready, i + 1)
                for h in range(2):
                    for b, (lo, hi_) in enumerate(((0, P), (P, TRI))):
                        nc.scalar.activation(pp[:, h, lo:hi_], pp[:, h, lo:hi_], ACT.Exp, bias=smax[:, b, h:h + 1],
                                             accum_out=ssum[:, b, h:h + 1]).then_inc(exp_done, 1)
                hi(2, 3)
                hi(3, 0)
                hi(3, 1)
                act.wait_ge(probs_turned, i * 2 + 2)
                nc.scalar.copy(ppT[:, 1, :], sc2_ps[:, 0:TRI]).then_inc(pT1_ready, 1)
                act.wait_ge(pv_done, i * 2 + 2)
                nc.scalar.copy(mixT[:, bass.ds(i * 2 + 1, 1), :], tr_ps[:, 0:T].rearrange("p (o t) -> p o t", o=1)
                               ).then_inc(mix_act, 1)
                attention_rows(i, 2, 0)

            def mix_split_hi(half):
                nc.scalar.copy(mix_hi[:, 8 * half:8 * half + 8, :], mixT[:, 8 * half:8 * half + 8, :]
                               ).then_inc(mix_hi_ready, 1)

            act.wait_ge(mix_dve, PAIRS)
            act.wait_ge(mix_act, PAIRS)
            mix_split_hi(0)

            def retention_rows(i, r, m, par):
                a = 2 * SECT + 3 * PAIRS + 5 * r + m
                before_ = 1 + r + (PAIRS if m < 3 else 0)
                ada_row_out(i * 18 + (B2_0 + 9 * r + (2 * m + 2 if m < 4 else 9)), m, par, i * 32 + 16 * before_,
                            i * 10 + (a + 1), i * 10 + a)

            with act.Fori(0, RHEADS // 2) as i:
                for r in range(2):
                    head = i * 2 + r

                    def hi(m, qr):
                        n = B2_0 + 9 * r + (2 * m if m < 4 else 9)
                        split_hi(n, i * 3, qr, i * 32 + (W_B2 + 16 * r + 4 * m))

                    hi(0, 2), hi(0, 3), hi(1, 0), hi(1, 1)
                    retention_rows(i, r, 0, 0)
                    hi(1, 2), hi(1, 3), hi(2, 0)
                    act.wait_ge(split_used, i * 32 + (W_B2 + 16 * r + 8))
                    for j in range(2):
                        nc.scalar.copy(kT[:, j, :], k_ps[j][:, 0:T]).then_inc(p1_out, 1)
                    hi(2, 1)
                    retention_rows(i, r, 1, 1)
                    hi(2, 2), hi(2, 3), hi(3, 0), hi(3, 1)
                    retention_rows(i, r, 2, 0)
                    act.wait_ge(ret_pv, head + 1)
                    for b in range(NB):
                        nc.scalar.activation(junk[:, b * DR:(b + 1) * DR], pv_ps[:, b * DR:(b + 1) * DR], ACT.Square,
                                             accum_out=sumsq[:, b, 0:1]).then_inc(ret_sq, 1)
                    hi(3, 2)
                    act.wait_ge(ret_ms, head + 1)
                    nc.scalar.activation(rt[:], ms[:], ACT.Sqrt).then_inc(ret_rt, 1)
                    hi(3, 3), hi(4, 0)
                    act.wait_ge(split_used, i * 32 + (W_B2 + 16 * r + 16))
                    for j in range(2):
                        nc.scalar.activation(sg[:, j, :], proj_ps[j][:, 0:CW], ACT.Silu).then_inc(p1_out, 1)
                    hi(4, 1)
                    retention_rows(i, r, 3, 1)
                    retention_rows(i, r, 4, 0)

            act.wait_ge(ret_mix, RHEADS)
            mix_split_hi(1)

            def w_out_hi(u, quarters=range(2, 6)):
                for qr in quarters:
                    if u + qr // 4 < N_C:
                        split_hi(C_0 + u + qr // 4, 0, qr % 4, W_C + 4 * (u + qr // 4))

            w_out_hi(0)
            w_out_hi(1, (2, 3))
            for m in range(ROWS):
                act.wait_ge(row_stored[m], 16 * (1 + RHEADS + (PAIRS if m < 3 else 0)))
            act.dma_start(buf_r[0:4, :], rows_dram[:, 2 * D:3 * D]).then_inc(gate_rows, 16)
            act.dma_start(buf_r[4:5, :], b_ada[:, 2 * D:3 * D]).then_inc(gate_rows, 16)
            for s in range(2):
                act.dma_start(mod_raw[:, :, s, :], rows_dram[:, (3 + s) * D:(4 + s) * D].rearrange(
                    "r (p k) -> p r k", k=K16)).then_inc(mod2_in, 16)
            w_out_hi(1, (4, 5))
            w_out_hi(2)
            for q in range(4):
                act.wait_ge(gm_ps, q + 1)
                nc.scalar.copy(buf_m[:, q * 512:(q + 1) * 512], turn_ps[q][:, :]).then_inc(gm_ready, 1)
            act.dma_start(buf_r[0:4, :], rows_dram[:, 5 * D:6 * D]).then_inc(gatef_rows, 16)
            act.dma_start(buf_r[4:5, :], b_ada[:, 5 * D:6 * D]).then_inc(gatef_rows, 16)
            for cc in range(4):
                if cc < 3:
                    w_out_hi(2 * cc + 3)
                for b in range(NB):
                    act.wait_ge(x1_piece, NB * cc + b + 1)
                    act.wait_ge(sq_done, NB + NB * cc + b)
                    nc.scalar.activation(junk, xs[:, b, cc * 512:(cc + 1) * 512], ACT.Square,
                                         accum_out=sumsq[:, b, cc:cc + 1]).then_inc(sq_done, 1)
                if cc < 2:
                    w_out_hi(2 * cc + 4)
            act.wait_ge(ms_done, 2)
            nc.scalar.activation(rt[:], ms[:], ACT.Sqrt).then_inc(rt_done, 1)
            for q in range(2):
                act.wait_ge(gf_ps, q + 1)
                nc.scalar.copy(gate_f[:, q * 512:(q + 1) * 512], ada_ps[q][:, :]).then_inc(gf_ready, 1)
            act.wait_ge(col_ready, 2)
            for g in range(1, 8, 2):
                act.wait_ge(turned, 8 + g + 1)
                for j in range(2):
                    k = 2 * g + j
                    last = nc.scalar.activation(xn2T[:, k, :], turn_ps[g % 4][:, j * T:(j + 1) * T], ACT.Identity,
                                                bias=shift[:, k:k + 1], scale=scale[:, k:k + 1])
                last.then_inc(evac_act, 1)
            act.wait_ge(logits_ps, 1)
            for b in range(NB):
                nc.scalar.copy(x1n_hi[:, b, :], xn[:, b, :]).then_inc(x1n_hi_ready, 1)
            for j in range(2):
                act.wait_ge(route_exp_in, j + 1)
                nc.scalar.activation(exp_out[j], exp_in[j], ACT.Exp).then_inc(route_exp, 1)
            act.wait_ge(iota_ready, 2)
            for k in range(1, K16, 2):
                act.wait_ge(gathered, k + 1)
                nc.scalar.activation(xgT[:, k, 0:2 * T], turn_ps[k % 4][:, :], ACT.Identity, bias=shift[:, k:k + 1],
                                     scale=scale[:, k:k + 1]).then_inc(evac_act, 1)
            act.wait_ge(keys_ps, 1)
            act.dma_start(buf_r[:], norm_final_w.partition_broadcast(P)).then_inc(final_w_in, 16)

            def expert_act(n):
                act.wait_ge(chunk_used, n * 6 + (D_0 + 4))
                nc.scalar.activation(sil[0:CAP, :], h_ps[0:CAP, :], ACT.Silu).then_inc(sil_ready, 1)
                act.wait_ge(gT_ps, n + 1)
                nc.scalar.copy(ggT.rearrange("p k s -> p (k s)"), gt_ps[:, 0:K4 * CAP]).then_inc(gT_ready, 1)

            with act.Fori(0, E - 1) as n:
                expert_act(n)
            act.wait_ge(tables_ready, 1)
            items = act.value_load(n_over[0:1, 0:1], min_val=0, max_val=OVER)
            with act.Fori(0, OVER) as t:
                with act.If(t < items):
                    expert_act(t + (E - 1))
                act.end_ifs()
            expert_act(items + (E - 1))
            for j in range(4):
                act.wait_ge(added, items * 4 + (4 * (E - 1) + j + 1))
                b, q = j // 2, j % 2
                for half in range(2):
                    col = half * 1024 + q * 512
                    nc.scalar.activation(square[:, 2 * j + half, :], xs[:, b, col:col + 512], ACT.Square,
                                         accum_out=sumsq[:, b, 2 * q + half:2 * q + half + 1]).then_inc(sq_done, 1)
                if q == 1:
                    act.wait_ge(ms_done, 3 + b)
                    nc.scalar.activation(rt[:, b:b + 1], ms[:, b:b + 1], ACT.Sqrt).then_inc(rt_done, 1)

        @block.vector
        def _(dve):
            v = nc.vector
            steps = [0]

            def step(ins):
                steps[0] += 1
                ins.then_inc(dve_step, 1)
                dve.wait_ge(dve_step, steps[0])

            def inverse_rms(nth, parts):
                if parts > 1:
                    step(v.tensor_reduce(ms[:], sumsq[:, :, 0:parts], AX, ALU.add))
                    src = ms[:]
                else:
                    src = sumsq[:, :, 0]
                v.tensor_scalar(ms[:], src, 1.0 / D, EPS, ALU.mult, ALU.add).then_inc(ms_done, 1)
                dve.wait_ge(rt_done, nth)
                step(v.reciprocal(rinv[:], rt[:]))

            dve.wait_ge(sq_done, NB)
            inverse_rms(1, 1)
            for b in range(NB):
                last = v.tensor_scalar(xn[:, b, :], x_a[:, b, :], rinv[:, b:b + 1], None, ALU.mult)
            last.then_inc(xn_ready, 1)
            for g in range(0, 8, 2):
                dve.wait_ge(turned, g + 1)
                v.tensor_copy(xnT[:, 2 * g:2 * g + 2, :].rearrange("p k t -> p (k t)"),
                              turn_ps[g % 4][:, :]).then_inc(evac_dve, 1)
            def split_lo(n, qr, x):
                dve.wait_ge(w_hi_ready, x + (qr + 1))
                v.tensor_tensor(w_lo[:, qr % 2, :], quarter(n, qr), w_hi[:, qr % 2, :],
                                ALU.subtract).then_inc(w_lo_ready, 1)

            dve.wait_ge(const_in, 2 * 16)
            dve.wait_ge(cols_made, 1)
            v.tensor_tensor(shift[:], sc_ps[:, 0:K16], b_col[:, 0, :], ALU.add)
            step(v.tensor_tensor(scale[:], sc_ps[:, K16:2 * K16], b_col[:, 1, :], ALU.add))
            v.scalar_tensor_tensor(out=scale[:], in0=scale[:], scalar=1.0, in1=mix_w[:], op0=ALU.add,
                                   op1=ALU.mult).then_inc(col_ready, 1)
            dve.wait_ge(col_ready, 1)
            dve.wait_ge(evac_dve, 4)
            for half in range(2):
                for k in range(8 * half, 8 * half + 8, 2):
                    last = v.tensor_scalar(xnT[:, k, :], xnT[:, k, :], scale[:, k:k + 1], shift[:, k:k + 1],
                                           ALU.mult, ALU.add)
                last.then_inc(mod_dve, 1)
            dve.wait_ge(mod_dve, 2)
            for half in range(2):
                split_lo(B1_0, half, 0)
                rows = slice(8 * half, 8 * half + 8)
                dve.wait_ge(h_hi_ready, half + 1)
                v.tensor_tensor(h_lo[:, rows, :], xnT[:, rows, :], h_hi[:, rows, :],
                                ALU.subtract).then_inc(h_lo_ready, 1)

            dve.wait_ge(bias_step, 3 + HEADS + 2)
            with dve.Fori(0, PAIRS) as i:
                def lo(m, qr):
                    split_lo(B1_0 + 2 * m, qr, i * 12 + 4 * m)

                lo(0, 2), lo(0, 3), lo(1, 0)
                dve.wait_ge(split_used, i * 12 + 4)
                for j in range(2):
                    v.tensor_copy(qT[:, j, :], proj_ps[j][:, 0:T]).then_inc(p0_out, 1)
                lo(1, 1), lo(1, 2), lo(1, 3), lo(2, 0), lo(2, 1)
                for h, bank in enumerate((sc_ps, sc2_ps)):
                    dve.wait_ge(scored, i * 2 + (h + 1))
                    bias = bias_sb[:, bass.ds(i * 2 + h, 1), :].rearrange("p o n -> p (o n)")
                    for at_, n in ((0, T), (T, P)):
                        v.scalar_tensor_tensor(out=pp[:, h, at_:at_ + n], in0=bank[:, at_:at_ + n], scalar=DH ** -0.5,
                                               in1=bias[:, 0:n], op0=ALU.mult, op1=ALU.add).then_inc(logits, 1)
                dve.wait_ge(logits, i * 6 + 4)
                v.tensor_reduce(smax[:, 0, :], pp[:, :, 0:P], AX, ALU.max).then_inc(logits, 1)
                v.tensor_reduce(smax[:, 1, :], pp[:, :, P:TRI], AX, ALU.max).then_inc(logits, 1)
                dve.wait_ge(logits, i * 6 + 6)
                v.tensor_scalar(smax[:], smax[:], -1.0, None, ALU.mult).then_inc(max_ready, 1)
                lo(2, 2)
                dve.wait_ge(exp_done, i * 4 + 4)
                v.reciprocal(sinv[:], ssum[:]).then_inc(ret_step, 1)
                dve.wait_ge(ret_step, i + 1)
                for h in range(2):
                    for b, (lo_, hi_) in enumerate(((0, P), (P, TRI))):
                        last = v.tensor_scalar(pp[:, h, lo_:hi_], pp[:, h, lo_:hi_], sinv[:, b, h:h + 1], None, ALU.mult)
                last.then_inc(probs_ready, 1)
                lo(2, 3), lo(3, 0)
                dve.wait_ge(split_used, i * 12 + 12)
                for j in range(2):
                    v.tensor_copy(vv[:, j, :], proj_ps[j][:, 0:CW]).then_inc(p0_out, 1)
                lo(3, 1)
                dve.wait_ge(probs_turned, i * 2 + 1)
                v.tensor_copy(ppT[:, 0, :], tr_ps[:, 0:TRI]).then_inc(pT0_ready, 1)
                dve.wait_ge(pv_done, i * 2 + 1)
                v.tensor_copy(mixT[:, bass.ds(i * 2, 1), :], pv_ps[:, 0:T].rearrange("p (o t) -> p o t", o=1)
                              ).then_inc(mix_dve, 1)

            def mix_split_lo(half):
                rows = slice(8 * half, 8 * half + 8)
                dve.wait_ge(mix_hi_ready, half + 1)
                v.tensor_tensor(mix_lo[:, rows, :], mixT[:, rows, :], mix_hi[:, rows, :],
                                ALU.subtract).then_inc(mix_lo_ready, 1)

            mix_split_lo(0)

            dve.wait_ge(late_in, LATE * 16)
            with dve.Fori(0, RHEADS // 2) as i:
                for r in range(2):
                    head = i * 2 + r

                    def lo(m, qr):
                        n = B2_0 + 9 * r + (2 * m if m < 4 else 9)
                        split_lo(n, qr, i * 32 + (W_B2 + 16 * r + 4 * m))

                    lo(0, 2), lo(0, 3), lo(1, 0)
                    dve.wait_ge(split_used, i * 32 + (W_B2 + 16 * r + 4))
                    for j in range(2):
                        v.tensor_copy(qT[:, j, :], proj_ps[j][:, 0:T]).then_inc(p0_out, 1)
                    lo(1, 1), lo(1, 2), lo(1, 3), lo(2, 0), lo(2, 1)
                    dve.wait_ge(scored, head + (2 * PAIRS + 1))
                    for at_, n in ((0, T), (T, P)):
                        last = v.tensor_tensor(scoreT[:, at_:at_ + n], sc_ps[:, at_:at_ + n],
                                               decay_sb[:, bass.ds(head * T, n)], ALU.mult)
                    last.then_inc(decayed, 1)
                    lo(2, 2), lo(2, 3), lo(3, 0)
                    dve.wait_ge(split_used, i * 32 + (W_B2 + 16 * r + 12))
                    for j in range(2):
                        v.tensor_copy(vv[:, j, :], proj_ps[j][:, 0:CW]).then_inc(p0_out, 1)
                    lo(3, 1)
                    dve.wait_ge(ret_sq, head * 2 + 2)
                    v.tensor_scalar(ms[:], sumsq[:, :, 0], 1.0 / DR, EPS, ALU.mult, ALU.add).then_inc(ret_ms, 1)
                    lo(3, 2)
                    dve.wait_ge(ret_rt, head + 1)
                    v.reciprocal(rinv[:], rt[:]).then_inc(ret_step, 1)
                    dve.wait_ge(ret_step, head * 3 + (PAIRS + 1))
                    for b in range(NB):
                        v.tensor_scalar(yy[:, b, :], pv_ps[:, b * DR:(b + 1) * DR], rinv[:, b:b + 1], None,
                                        ALU.mult).then_inc(ret_step, 1)
                    lo(3, 3), lo(4, 0)
                    dve.wait_ge(ret_step, head * 3 + (PAIRS + 3))
                    dve.wait_ge(p1_out, head * 4 + (2 * PAIRS + 4))
                    v.tensor_tensor(yy, yy, sg, ALU.mult).then_inc(ret_y, 1)
                    lo(4, 1)
                    dve.wait_ge(ret_turned, head + 1)
                    for j in range(2):
                        last = v.tensor_scalar(mixT[:, bass.ds(head * 2 + (HEADS + j), 1), :],
                                               tr_ps[:, j * T:(j + 1) * T].rearrange("p (o t) -> p o t", o=1),
                                               ret_w[:, bass.ds(head * 2 + j, 1)], None, ALU.mult)
                    last.then_inc(ret_mix, 1)

            mix_split_lo(1)

            tmp = yy.rearrange("p b n -> p (b n)")
            tmps = [tmp, sg.rearrange("p b n -> p (b n)")]

            def w_out_lo(u):
                for qr in range(2, 6):
                    if u + qr // 4 < N_C:
                        split_lo(C_0 + u + qr // 4, qr % 4, W_C + 4 * (u + qr // 4))

            for u in range(3):
                w_out_lo(u)
            dve.wait_ge(x_in, 32)
            for cc in range(4):
                dve.wait_ge(split_used, W_C + 8 * (cc + 1))
                dve.wait_ge(gm_ready, cc + 1)
                for b in range(NB):
                    step(v.tensor_tensor(tmps[b], out_ps[cc % 2][b][:, :], buf_m[:, cc * 512:(cc + 1) * 512], ALU.mult))
                    piece = xs[:, b, cc * 512:(cc + 1) * 512]
                    v.tensor_tensor(piece, piece, tmps[b], ALU.add).then_inc(x1_piece, 1)
                for u in (2 * cc + 3, 2 * cc + 4):
                    if u < N_C:
                        w_out_lo(u)
            dve.wait_ge(mod2_in, 32)
            step(v.tensor_reduce(sums2[:], mod_raw[:].rearrange("p r s k -> p (s k) r"), AX, ALU.add))
            v.tensor_tensor(shift[:], sums2[:, 0:K16], b_col[:, 3, :], ALU.add)
            step(v.tensor_tensor(scale[:], sums2[:, K16:2 * K16], b_col[:, 4, :], ALU.add))
            v.scalar_tensor_tensor(out=scale[:], in0=scale[:], scalar=1.0, in1=ffn_w[:], op0=ALU.add,
                                   op1=ALU.mult).then_inc(col_ready, 1)
            dve.wait_ge(col_ready, 2)
            dve.wait_ge(sq_done, NB + 4 * NB)
            inverse_rms(2, 4)
            for b in range(NB):
                last = v.tensor_scalar(xn[:, b, :], xs[:, b, :], rinv[:, b:b + 1], None, ALU.mult)
            last.then_inc(xn_ready, 1)
            for g in range(0, 8, 2):
                dve.wait_ge(turned, 8 + g + 1)
                for j in range(2):
                    k = 2 * g + j
                    last = v.tensor_scalar(xn2T[:, k, :], turn_ps[g % 4][:, j * T:(j + 1) * T], scale[:, k:k + 1],
                                           shift[:, k:k + 1], ALU.mult, ALU.add)
                last.then_inc(evac_dve, 1)

            def wide(a, n):
                return a.rearrange("p (b o) -> p b o", o=1).to_broadcast([P, NB, n])

            def const(a, n):
                return a.rearrange("p (o n) -> p o n", o=1).to_broadcast([P, NB, n])

            def pick(values, rev, best, eq, top, onehot_):
                n = values.shape[2]
                step(v.tensor_reduce(best, values, AX, ALU.max))
                step(v.tensor_tensor(eq, values, wide(best, n), ALU.is_equal))
                step(v.tensor_tensor(eq, eq, const(rev, n), ALU.mult))
                step(v.tensor_reduce(top, eq, AX, ALU.max))
                step(v.tensor_tensor(onehot_, const(rev, n), wide(top, n), ALU.is_equal))

            dve.wait_ge(logits_ps, 1)
            dve.wait_ge(consts_made, 9)
            for b in range(NB):
                last = v.tensor_tensor(lg[:, b, :], proj_ps[b][:, 0:36], b_route[:], ALU.add)
            step(last)
            pick(lg[:, :, 0:4], rev8[:, 4:8], gmax, eq4, top1, og)
            v.tensor_tensor(exp_in[0].rearrange("p (b n) -> p b n", b=NB), lg[:, :, 0:4], wide(gmax, 4),
                            ALU.subtract).then_inc(route_exp_in, 1)
            lgr = lg[:, :, 4:36].rearrange("p b (g e) -> p b g e", g=GROUPS)
            for b in range(NB):
                last = v.tensor_tensor(lsel[:, b], lgr[:, b], og[:, b].rearrange("p (g o) -> p g o", o=1).to_broadcast(
                    [P, GROUPS, EPG]), ALU.mult)
            step(last)
            step(v.tensor_reduce(el, lsel.rearrange("p b g e -> p b e g"), AX, ALU.add))
            pick(el, rev8[:], m1, eq8, top1, o1)
            step(v.scalar_tensor_tensor(out=el, in0=o1, scalar=-1e30, in1=el, op0=ALU.mult, op1=ALU.add))
            pick(el, rev8[:], m2, eq8, top1, o2)
            v.tensor_tensor(exp_in[1], m2, m1, ALU.subtract).then_inc(route_exp_in, 1)
            dve.wait_ge(route_exp, 1)
            step(v.tensor_reduce(gsum, exp_out[0].rearrange("p (b n) -> p b n", b=NB), AX, ALU.add))
            for q, o in enumerate((o1, o2)):
                for b in range(NB):
                    last = v.tensor_tensor(chosen[:, q, b].rearrange("p (g e) -> p g e", g=GROUPS),
                                           og[:, b].rearrange("p (g o) -> p g o", o=1).to_broadcast([P, GROUPS, EPG]),
                                           o[:, b].rearrange("p (o e) -> p o e", o=1).to_broadcast([P, GROUPS, EPG]),
                                           ALU.mult)
            step(last)
            v.tensor_tensor(both, chosen[:, 0], chosen[:, 1], ALU.add).then_inc(picks, 1)
            dve.wait_ge(route_exp, 2)
            step(v.tensor_scalar(w_tok[:, 1, :], exp_out[1], 1.0, None, ALU.add))
            step(v.tensor_tensor(w_tok[:, 1, :], w_tok[:, 1, :], gsum, ALU.mult))
            step(v.reciprocal(w_tok[:, 0, :], w_tok[:, 1, :]))
            step(v.tensor_tensor(w_tok[:, 1, :], w_tok[:, 0, :], exp_out[1], ALU.mult))
            dve.wait_ge(counts_ps, 1)
            v.tensor_copy(cnt, proj_ps[1][:, 0:3 * E])
            step(v.tensor_copy(cnt_col[:, 0:1], ada_ps[0][0:E, 0:1]))
            step(v.tensor_scalar(cnt_col[:, 1:2], cnt_col[:, 0:1], float(CAP), None, ALU.is_gt))
            for j in range(2, 4):
                step(v.scalar_tensor_tensor(out=cnt_col[:, 1:2], in0=cnt_col[:, 0:1], scalar=float(CAP * j),
                                            in1=cnt_col[:, 1:2], op0=ALU.is_gt, op1=ALU.add))
            v.tensor_copy(cnt_rep, cnt_col.rearrange("p (q o) -> p q o", o=1).to_broadcast([E, 2, P])).then_inc(counts_sb, 1)
            dve.wait_ge(starts_ps, 1)
            step(v.tensor_copy(first, ada_ps[1][:, 0:2 * E]))
            ranks = cnt[:, E:3 * E].rearrange("p (b e) -> p b e", b=NB)
            v.tensor_tensor(where[:, 0], ranks, const(first[:, 0:E], E), ALU.add)
            step(v.tensor_tensor(where[:, 1], ranks, e256[:].to_broadcast([P, NB, E]), ALU.add))
            for s in range(2):
                for q in range(2):
                    step(v.tensor_tensor(wtmp, chosen[:, q], where[:, s], ALU.mult))
                    step(v.tensor_reduce(slot_key[:, s, q, :], wtmp, AX, ALU.add))
            dve.wait_ge(iota_ready, 1)
            dve.wait_ge(gf_ps, 2)
            for b in range(NB):
                step(v.tensor_scalar(onehot[:, b, :], iota_s, slot_key[:, 0, 0, b:b + 1], None, ALU.is_equal))
                last = v.scalar_tensor_tensor(out=onehot[:, b, :], in0=iota_s, scalar=slot_key[:, 0, 1, b:b + 1],
                                              in1=onehot[:, b, :], op0=ALU.is_equal, op1=ALU.add)
            last.then_inc(onehot_ready, 1)
            for b in range(NB):
                for q in range(4):
                    s = slot_key[:, 1, q, b:b + 1] if q < 2 else w_tok[:, q - 2, b:b + 1]
                    last = v.tensor_scalar(diag[:, b, q, :], ident[:], s, None, ALU.mult)
            last.then_inc(diag_ready, 1)
            v.tensor_copy(start_tab[:, 0:E], first[0:1, 0:E]).then_inc(starts_ready, 1)
            dve.wait_ge(iota_ready, 2)
            for k in range(0, K16, 2):
                dve.wait_ge(gathered, k + 1)
                v.tensor_scalar(xgT[:, k, 0:2 * T], turn_ps[k % 4][:, :], scale[:, k:k + 1], shift[:, k:k + 1],
                                ALU.mult, ALU.add).then_inc(evac_dve, 1)
                if k % 8 == 6:
                    rows = slice(k - 6, k + 2)
                    dve.wait_ge(evac_act, 8 + (k + 2) // 2)
                    dve.wait_ge(evac_dve, 8 + (k + 2) // 2)
                    v.tensor_copy(xe[:, rows, :], xgT[:, rows, 0:CAP]).then_inc((xe_ready, xe_rest_ready)[k // 8], 1)
            def keys_out():
                dve.wait_ge(keys_ps, 1)
                for b in range(NB):
                    last = v.tensor_copy(keys[:, :, b * P:(b + 1) * P],
                                         proj_ps[b][:, :].rearrange("p (q n) -> p q n", q=4))
                last.then_inc(keys_ready, 1)

            def tables():
                over, upto, less = tab[:, 0:E], tab[:, E:2 * E], first[:, E:2 * E]
                step(v.tensor_scalar(over, cnt[:, 0:E], float(CAP), None, ALU.is_gt))
                for j in range(2, 4):
                    step(v.scalar_tensor_tensor(out=over, in0=cnt[:, 0:E], scalar=float(CAP * j), in1=over,
                                                op0=ALU.is_gt, op1=ALU.add))
                step(v.tensor_tensor(upto, over, less, ALU.add))
                step(v.tensor_copy(n_over[:], upto[0:1, E - 1:E]))

                def by_expert(a):
                    return a.rearrange("p (o e) -> p o e", o=1).to_broadcast([P, OVER + 1, E])

                def by_item(a):
                    return a.rearrange("p (t o) -> p t o", o=1).to_broadcast([P, OVER + 1, E])

                step(v.tensor_tensor(is_item, by_expert(less), by_item(over_t[:]), ALU.is_le))
                step(v.tensor_tensor(item_tmp, by_expert(upto), by_item(over_t[:]), ALU.is_gt))
                step(v.tensor_tensor(is_item, is_item, item_tmp, ALU.mult))
                step(v.tensor_reduce(item_is, is_item, AX, ALU.add))
                for src, dst, last_one in ((first[:, 0:E], item_slot, first[:, E - 1:E]),
                                           (e256[:, 0, :], item_key, e256[:, 0, E - 1:E])):
                    step(v.scalar_tensor_tensor(out=over, in0=less, scalar=-float(CAP), in1=src, op0=ALU.mult,
                                                op1=ALU.add))
                    step(v.tensor_tensor(item_tmp, is_item, by_expert(over), ALU.mult))
                    step(v.tensor_reduce(dst, item_tmp, AX, ALU.add))
                    step(v.tensor_scalar(item_pad, over_cap[:], last_one, None, ALU.subtract))
                    step(v.tensor_tensor(item_pad, item_pad, item_is, ALU.mult))
                    step(v.tensor_tensor(dst, dst, item_pad, ALU.add))
                    step(v.tensor_scalar(dst, dst, last_one, None, ALU.add))
                step(v.tensor_copy(start_tab[:, E - 1:E + OVER], item_slot[0:1, :]))
                step(v.tensor_copy(key_tab[:, E - 1:E + OVER], item_key))
                step(v.tensor_tensor(item_tmp, is_item, by_expert(e256[:, 0, :]), ALU.mult))
                step(v.tensor_reduce(item_pad, item_tmp, AX, ALU.add))
                v.tensor_scalar(item_e[:, 0:OVER + 1], item_pad[0:1, :], 1.0 / 256, None,
                                ALU.mult).then_inc(tables_ready, 1)

            def fetch(n):
                dve.wait_ge(chunk_used, n * 6 + (D_0 - 2))
                s = dve.value_load(start_tab[0:1, bass.ds(n, 1)], min_val=0, max_val=2 * T)
                v.tensor_copy(xe, xgT[:, :, bass.ds(s, CAP)]).then_inc(xe_ready, 1)

            def gate_answers(n):
                dve.wait_ge(chunk_used, n * 6 + (D_0 + 6))
                for q in range(2):
                    last = v.tensor_tensor(yg[:, q * 512:(q + 1) * 512], y_ps[q][:, :], gate_f[:, q * 512:(q + 1) * 512],
                                           ALU.mult)
                last.then_inc(yg_ready, 1)

            def weights_of(n):
                v.tensor_tensor(key_col[:], lane[:], key_tab[:, bass.ds(n, 1)], ALU.add).then_inc(comb_step, 1)
                dve.wait_ge(comb_step, n * 3 + 1)
                v.scalar_tensor_tensor(out=comb, in0=keys[:, 0, :], scalar=key_col[:, 0:1], in1=keys[:, 2, :],
                                       op0=ALU.is_equal, op1=ALU.mult).then_inc(comb_step, 1)
                v.scalar_tensor_tensor(out=comb2, in0=keys[:, 1, :], scalar=key_col[:, 0:1], in1=keys[:, 3, :],
                                       op0=ALU.is_equal, op1=ALU.mult).then_inc(comb_step, 1)
                dve.wait_ge(comb_step, n * 3 + 3)
                v.tensor_tensor(comb, comb, comb2, ALU.add).then_inc(comb_ready, 1)

            def gated(n):
                dve.wait_ge(sil_ready, n + 1)
                v.tensor_tensor(gg[0:CAP, :], sil[0:CAP, :], h_ps[CAP:2 * CAP, :], ALU.mult).then_inc(g_ready, 1)

            def add_pair(n, j, ps=add_ps):
                b, q = j // 2, j % 2
                dve.wait_ge(add_done, n * 4 + (j + 1))
                for half in range(2):
                    col = half * 1024 + q * 512
                    piece = xs[:, b, col:col + 512]
                    last = v.tensor_tensor(piece, piece, ps[(2 * j + half) % len(ps)][:, :], ALU.add)
                last.then_inc(added, 1)

            def add_answers(n):
                for j in range(4):
                    add_pair(n, j)

            dve.wait_ge(starts_ready, 1)
            dve.wait_ge(evac_act, 16)
            dve.wait_ge(evac_dve, 16)
            gated(0)
            keys_out()
            dve.wait_ge(keys_ready, 1)
            weights_of(0)
            tables()

            def item(n):
                fetch(n)
                gate_answers(n - 1)
                add_answers(n - 1)
                gated(n)
                weights_of(n)

            with dve.Fori(1, E - 1) as n:
                item(n)
            dve.wait_ge(tables_ready, 1)
            items = dve.value_load(n_over[0:1, 0:1], min_val=0, max_val=OVER)
            with dve.Fori(0, OVER) as t:
                with dve.If(t < items):
                    item(t + (E - 1))
                dve.end_ifs()
            item(items + (E - 1))
            gate_answers(items + (E - 1))

            def final_norm(b):
                dve.wait_ge(sq_done, NB + 4 * NB + 4 * (b + 1))
                step(v.tensor_reduce(ms[:, b:b + 1], sumsq[:, b, 0:4], AX, ALU.add))
                v.tensor_scalar(ms[:, b:b + 1], ms[:, b:b + 1], 1.0 / D, EPS, ALU.mult, ALU.add).then_inc(ms_done, 1)
                if b == 0:
                    add_pair(items + (E - 1), 3, last_add_ps)
                dve.wait_ge(rt_done, 3 + b)
                step(v.reciprocal(rinv[:, b:b + 1], rt[:, b:b + 1]))
                for q in range(2):
                    cols = slice(q * 1024, (q + 1) * 1024)
                    v.scalar_tensor_tensor(out=answer[:, b, cols], in0=xs[:, b, cols], scalar=rinv[:, b:b + 1],
                                           in1=buf_r[:, cols], op0=ALU.mult, op1=ALU.mult).then_inc(out_ready, 1)

            for j in range(3):
                add_pair(items + (E - 1), j, last_add_ps)
            dve.wait_ge(final_w_in, 16)
            dve.wait_ge(added, items * 4 + (4 * (E - 1) + 2))
            final_norm(0)
            dve.wait_ge(added, items * 4 + 4 * E)
            final_norm(1)


def decays():
    import numpy as np

    t = np.arange(P, dtype=np.float32)
    far = t[:, None] - t[None, :]
    causal = far >= 0
    decay = np.zeros((P, RHEADS, 2 * P), np.float32)
    for h in range(RHEADS):
        gamma = 1.0 - 2.0 ** (-5.0 - h)
        own = np.where(causal, gamma ** np.maximum(far, 0), 0.0).T
        decay[:, h] = np.concatenate([own, gamma ** (far + P).T], 1) * DR ** -0.5
    return decay.astype(np.float32).reshape(P, -1)


_INS = ["x", "c", "w_ada", "b_ada", "norm_mix_w", "w_in", "ret_norm_w", "w_out", "norm_ffn_w", "w_group",
        "b_group", "w_router", "b_router", "w1", "w3", "w2", "norm_final_w"]


def kernel(**inputs):
    import numpy as np
    import concourse.bacc as bacc
    from concourse.bass_utils import run_bass_kernel_spmd as run

    nc = bacc.Bacc("TRN2", target_bir_lowering=False, num_devices=1)
    arrays = {f"in_{n}": np.ascontiguousarray(inputs[n]) for n in _INS}
    arrays["decay"] = decays()
    args = [nc.dram_tensor(n, a.shape, mybir.dt.from_np(a.dtype), kind="ExternalInput").ap() for n, a in arrays.items()]
    rows_dram = nc.dram_tensor("ada_rows", [4, 6 * D], F32, kind="Internal").ap()
    out = nc.dram_tensor("out", [1, T, D], F32, kind="ExternalOutput").ap()
    build(nc, *args, rows_dram, out)
    return run(nc, [arrays], core_ids=[0]).results[0]["out"]
```
